# Optimizing a Trainium2 kernel written in Bass

```python
import math
import jax, jax.numpy as jnp
from jax import lax
import numpy as np

D_MODEL = 2048
BATCH = 1
SEQ = 256
DEPTH = 1

GRID_W = 64
CTX_LEN = 256
GLA_HEADS = 8
GLA_DK = 64
GLA_DV = 128
GLA_RANK = 16
GLA_TAU = 16.0
GLA_CHUNK = 64
DIFF_HEADS = 8
DIFF_DQK = 64
DIFF_DV = 128
D_FF = 5632
CONV_W = 3
Q_BLOCK = 128
ROPE_THETA = 10000.0
EPS = 1e-6

GLA_QK = GLA_HEADS * GLA_DK
GLA_V = GLA_HEADS * GLA_DV
DIFF_QK = DIFF_HEADS * 2 * DIFF_DQK
DIFF_V = DIFF_HEADS * DIFF_DV
IN_SIZES = [GLA_QK, GLA_QK, GLA_V, GLA_V, GLA_RANK, GLA_RANK, DIFF_QK, DIFF_QK, DIFF_V]
D_IN = sum(IN_SIZES)
IN_OFFSETS = [int(v) for v in np.cumsum(IN_SIZES)[:-1]]


def rms_norm(x, w):
    xf = x.astype(jnp.float32)
    y = xf * lax.rsqrt(jnp.mean(xf * xf, axis=-1, keepdims=True) + EPS)
    return (y * w.astype(jnp.float32)).astype(x.dtype)

def modulate(h, shift, scale):
    return h * (1.0 + scale) + shift

def to_heads(t, n, d):
    B, T, _ = t.shape
    return t.reshape(B, T, n, d).transpose(0, 2, 1, 3)

def from_heads(t):
    B, n, T, d = t.shape
    return t.transpose(0, 2, 1, 3).reshape(B, T, n * d)

def rope_axis(x, ang):
    half = x.shape[-1] // 2
    x1, x2 = x[..., :half], x[..., half:]
    cos = jnp.cos(ang).astype(x.dtype)
    sin = jnp.sin(ang).astype(x.dtype)
    return jnp.concatenate([x1 * cos - x2 * sin, x2 * cos + x1 * sin], axis=-1)

def rope_2d(x, ang_row, ang_col):
    r = x.shape[-1] // 2
    return jnp.concatenate([rope_axis(x[..., :r], ang_row), rope_axis(x[..., r:], ang_col)], axis=-1)

def gla_scan(q, k, v, log_a, s0):
    B, H, T, dk = q.shape
    dv = v.shape[-1]
    n = T // GLA_CHUNK

    def chunks(t):
        return jnp.moveaxis(t.astype(jnp.float32).reshape(B, H, n, GLA_CHUNK, t.shape[-1]), 2, 0)

    lower = jnp.tril(jnp.ones((GLA_CHUNK, GLA_CHUNK), dtype=bool))[:, :, None]

    def step(state, inp):
        qc, kc, vc, ac = inp
        b = jnp.cumsum(ac, axis=2)
        o_inter = jnp.einsum('bhid,bhde->bhie', qc * jnp.exp(b), state)
        rel = b[:, :, :, None, :] - b[:, :, None, :, :]
        decay = jnp.exp(jnp.where(lower, rel, -jnp.inf))
        scores = jnp.einsum('bhid,bhjd,bhijd->bhij', qc, kc, decay)
        o_intra = jnp.einsum('bhij,bhje->bhie', scores, vc)
        b_last = b[:, :, -1:, :]
        state = jnp.exp(b_last[:, :, 0, :])[..., None] * state + jnp.einsum(
            'bhjd,bhje->bhde', kc * jnp.exp(b_last - b), vc)
        return state, o_inter + o_intra

    s_final, o = lax.scan(step, s0.astype(jnp.float32), (chunks(q), chunks(k), chunks(v), chunks(log_a)))
    o = jnp.moveaxis(o, 0, 2).reshape(B, H, T, dv)
    return o.astype(v.dtype), s_final

def diff_softmax(q, k, v, lam):
    s = jnp.einsum('bhmqd,bhmkd->bhmqk', q, k).astype(jnp.float32) * (DIFF_DQK ** -0.5)
    p = jax.nn.softmax(s, axis=-1)
    a = p[:, :, 0] - lam * p[:, :, 1]
    return jnp.einsum('bhqk,bhkd->bhqd', a.astype(v.dtype), v)

def conv_ffn(h, w_up, conv_w, conv_b, w_down):
    u = h @ w_up
    T = u.shape[1]
    pad = CONV_W // 2
    up = jnp.pad(u, ((0, 0), (pad, pad), (0, 0)))
    u = sum(up[:, j:j + T] * conv_w[j] for j in range(CONV_W)) + conv_b
    gate, val = jnp.split(u, 2, axis=-1)
    return (jax.nn.silu(gate) * val) @ w_down

def hybrid_layer(x, ctx, c, c_ctx, w_ada, b_ada, norm1_w, w_in, w_a_up_f, b_a_f, w_a_up_b, b_a_b,
                 gla_onorm_w, diff_qnorm_w, diff_knorm_w, lambda_q1, lambda_k1, lambda_q2, lambda_k2,
                 diff_onorm_w, w_proj_gla, w_proj_diff, w_gate, b_gate, w_out, norm2_w, w_up, conv_w,
                 conv_b, w_down, ang_row, ang_col, lam_init, update_ctx):
    B, S, _ = x.shape
    sh1, sc1, g1, sh2, sc2, g2 = [m[:, None, :] for m in
                                  jnp.split(jax.nn.silu(c) @ w_ada + b_ada, 6, axis=-1)]
    sh1c, sc1c, g1c, sh2c, sc2c, g2c = jnp.split(jax.nn.silu(c_ctx) @ w_ada + b_ada, 6, axis=-1)

    h_l = modulate(rms_norm(x, norm1_w), sh1, sc1)
    h_c = modulate(rms_norm(ctx, norm1_w), sh1c, sc1c)
    gq_l, gk_l, gv_l, gr_l, gaf_l, gab_l, dq_l, dk_l, dv_l = jnp.split(h_l @ w_in, IN_OFFSETS, axis=-1)
    gq_c, gk_c, gv_c, gr_c, gaf_c, gab_c, dq_c, dk_c, dv_c = jnp.split(h_c @ w_in, IN_OFFSETS, axis=-1)

    def gla_heads(gq, gk, gv, gaf, gab):
        q = to_heads(gq, GLA_HEADS, GLA_DK) * (GLA_DK ** -0.5)
        k = to_heads(gk, GLA_HEADS, GLA_DK)
        v = to_heads(gv, GLA_HEADS, GLA_DV)
        la_f = to_heads(jax.nn.log_sigmoid((gaf @ w_a_up_f + b_a_f).astype(jnp.float32)) / GLA_TAU,
                        GLA_HEADS, GLA_DK)
        la_b = to_heads(jax.nn.log_sigmoid((gab @ w_a_up_b + b_a_b).astype(jnp.float32)) / GLA_TAU,
                        GLA_HEADS, GLA_DK)
        return q, k, v, la_f, la_b

    aq_l, ak_l, av_l, alf_l, alb_l = gla_heads(gq_l, gk_l, gv_l, gaf_l, gab_l)
    aq_c, ak_c, av_c, alf_c, alb_c = gla_heads(gq_c, gk_c, gv_c, gaf_c, gab_c)
    zeros = jnp.zeros((B, GLA_HEADS, GLA_DK, GLA_DV), jnp.float32)

    def flip(t):
        return jnp.flip(t, axis=2)

    o_cf, s_cf = gla_scan(aq_c, ak_c, av_c, alf_c, zeros)
    o_lf, _ = gla_scan(aq_l, ak_l, av_l, alf_l, s_cf)
    o_cb, s_cb = gla_scan(flip(aq_c), flip(ak_c), flip(av_c), flip(alb_c), zeros)
    o_lb, _ = gla_scan(flip(aq_l), flip(ak_l), flip(av_l), flip(alb_l), s_cb)

    def gla_out(o, r):
        return from_heads(rms_norm(o, gla_onorm_w)) * jax.nn.silu(r)

    def diff_qk(t, w):
        Bt, T, _ = t.shape
        t = t.reshape(Bt, T, DIFF_HEADS, 2, DIFF_DQK).transpose(0, 2, 3, 1, 4)
        return rms_norm(t, w)

    q_l = rope_2d(diff_qk(dq_l, diff_qnorm_w), ang_row, ang_col)
    k_l = rope_2d(diff_qk(dk_l, diff_knorm_w), ang_row, ang_col)
    k_c = diff_qk(dk_c, diff_knorm_w)
    v_l = to_heads(dv_l, DIFF_HEADS, DIFF_DV)
    v_c = to_heads(dv_c, DIFF_HEADS, DIFF_DV)
    lam = (jnp.exp(jnp.sum(lambda_q1.astype(jnp.float32) * lambda_k1.astype(jnp.float32)))
           - jnp.exp(jnp.sum(lambda_q2.astype(jnp.float32) * lambda_k2.astype(jnp.float32))) + lam_init)

    k_all = jnp.concatenate([k_c, k_l], axis=3)
    v_all = jnp.concatenate([v_c, v_l], axis=2)
    nb = S // Q_BLOCK
    q_blocks = jnp.moveaxis(q_l.reshape(B, DIFF_HEADS, 2, nb, Q_BLOCK, DIFF_DQK), 3, 0)
    o_diff = lax.map(lambda qb: diff_softmax(qb, k_all, v_all, lam), q_blocks)
    o_diff = jnp.moveaxis(o_diff, 0, 2).reshape(B, DIFF_HEADS, S, DIFF_DV)

    def diff_out(o):
        return from_heads(rms_norm(o, diff_onorm_w) * (1.0 - lam_init))

    def merge(h, ya, yb):
        g_a, g_b = jnp.split(jax.nn.sigmoid(h @ w_gate + b_gate), 2, axis=-1)
        return (g_a * (ya @ w_proj_gla) + g_b * (yb @ w_proj_diff)) @ w_out

    mix_l = merge(h_l, gla_out(o_lf + flip(o_lb), gr_l), diff_out(o_diff))
    x_new = x + g1 * mix_l
    h2_l = modulate(rms_norm(x_new, norm2_w), sh2, sc2)
    x_new = x_new + g2 * conv_ffn(h2_l, w_up, conv_w, conv_b, w_down)

    if update_ctx:
        q_c = diff_qk(dq_c, diff_qnorm_w)
        o_diff_c = diff_softmax(q_c, k_c, v_c, lam)
        mix_c = merge(h_c, gla_out(o_cf + flip(o_cb), gr_c), diff_out(o_diff_c))
        ctx = ctx + g1c * mix_c
        h2_c = modulate(rms_norm(ctx, norm2_w), sh2c, sc2c)
        ctx = ctx + g2c * conv_ffn(h2_c, w_up, conv_w, conv_b, w_down)
    return x_new, ctx

def first_inputs(seed: int = 0) -> dict:
    key = jax.random.key(seed)
    ks = jax.random.split(key, 32)
    f32 = jnp.float32
    D = D_MODEL

    def nrm(k, shape, scale):
        return jax.random.normal(k, shape, f32) * scale

    def gain(k, shape):
        return 1.0 + 0.02 * jax.random.normal(k, shape, f32)

    return {
        "x": nrm(ks[0], (BATCH, SEQ, D), 1.0),
        "c": nrm(ks[1], (BATCH, D), 1.0),
        "ctx": nrm(ks[2], (BATCH, CTX_LEN, D), 1.0),
        "c_ctx": nrm(ks[3], (D,), 1.0),
        "w_ada": nrm(ks[4], (DEPTH, D, 6 * D), D ** -0.5),
        "b_ada": nrm(ks[5], (DEPTH, 6 * D), 0.01),
        "norm1_w": gain(ks[6], (DEPTH, D)),
        "w_in": nrm(ks[7], (DEPTH, D, D_IN), D ** -0.5),
        "w_a_up_f": nrm(ks[8], (DEPTH, GLA_RANK, GLA_QK), GLA_RANK ** -0.5),
        "b_a_f": 1.0 + nrm(ks[9], (DEPTH, GLA_QK), 0.1),
        "w_a_up_b": nrm(ks[10], (DEPTH, GLA_RANK, GLA_QK), GLA_RANK ** -0.5),
        "b_a_b": 1.0 + nrm(ks[11], (DEPTH, GLA_QK), 0.1),
        "gla_onorm_w": gain(ks[12], (DEPTH, GLA_DV)),
        "diff_qnorm_w": gain(ks[13], (DEPTH, DIFF_DQK)),
        "diff_knorm_w": gain(ks[14], (DEPTH, DIFF_DQK)),
        "lambda_q1": nrm(ks[15], (DEPTH, DIFF_DQK), 0.1),
        "lambda_k1": nrm(ks[16], (DEPTH, DIFF_DQK), 0.1),
        "lambda_q2": nrm(ks[17], (DEPTH, DIFF_DQK), 0.1),
        "lambda_k2": nrm(ks[18], (DEPTH, DIFF_DQK), 0.1),
        "diff_onorm_w": gain(ks[19], (DEPTH, DIFF_DV)),
        "w_proj_gla": nrm(ks[20], (DEPTH, GLA_V, D), GLA_V ** -0.5),
        "w_proj_diff": nrm(ks[21], (DEPTH, DIFF_V, D), DIFF_V ** -0.5),
        "w_gate": nrm(ks[22], (DEPTH, D, 2 * D), D ** -0.5),
        "b_gate": nrm(ks[23], (DEPTH, 2 * D), 0.01),
        "w_out": nrm(ks[24], (DEPTH, D, D), D ** -0.5),
        "norm2_w": gain(ks[25], (DEPTH, D)),
        "w_up": nrm(ks[26], (DEPTH, D, 2 * D_FF), D ** -0.5),
        "conv_w": nrm(ks[27], (DEPTH, CONV_W, 2 * D_FF), CONV_W ** -0.5),
        "conv_b": nrm(ks[28], (DEPTH, 2 * D_FF), 0.01),
        "w_down": nrm(ks[29], (DEPTH, D_FF, D), D_FF ** -0.5),
    }

def first_block(x, c, ctx, c_ctx, w_ada, b_ada, norm1_w, w_in, w_a_up_f, b_a_f, w_a_up_b, b_a_b,
              gla_onorm_w, diff_qnorm_w, diff_knorm_w, lambda_q1, lambda_k1, lambda_q2, lambda_k2,
              diff_onorm_w, w_proj_gla, w_proj_diff, w_gate, b_gate, w_out, norm2_w, w_up, conv_w,
              conv_b, w_down):
    S = x.shape[1]
    ROWS = S // GRID_W
    pos_row = jnp.repeat(jnp.arange(ROWS), GRID_W).astype(jnp.float32)
    pos_col = jnp.tile(jnp.arange(GRID_W), ROWS).astype(jnp.float32)
    n_freq = DIFF_DQK // 4
    inv_freq = ROPE_THETA ** (-jnp.arange(n_freq, dtype=jnp.float32) / n_freq)
    ang_row = pos_row[:, None] * inv_freq
    ang_col = pos_col[:, None] * inv_freq
    for i in range(DEPTH):
        lam_init = 0.8 - 0.6 * math.exp(-0.3 * i)
        x, ctx = hybrid_layer(
            x, ctx, c, c_ctx, w_ada[i], b_ada[i], norm1_w[i], w_in[i], w_a_up_f[i], b_a_f[i],
            w_a_up_b[i], b_a_b[i], gla_onorm_w[i], diff_qnorm_w[i], diff_knorm_w[i], lambda_q1[i],
            lambda_k1[i], lambda_q2[i], lambda_k2[i], diff_onorm_w[i], w_proj_gla[i], w_proj_diff[i],
            w_gate[i], b_gate[i], w_out[i], norm2_w[i], w_up[i], conv_w[i], conv_b[i], w_down[i],
            ang_row, ang_col, lam_init, i < DEPTH - 1)
    return x


MEM_LEN = 256
NEG_BIG = 1e9

MLA_HEADS = 8
MLA_NOPE = 128
MLA_ROPE = 64
MLA_V = 128
MLA_Q_RANK = 512
MLA_KV_RANK = 512

NSA_HEADS = 4
NSA_DK = 192
NSA_DV = 128
CMP_LEN = 32
CMP_STRIDE = 16
SLC_LEN = 64
SLC_TOPN = 16
WIN = 512

MEM_HEADS = 4
MEM_DH = 128

MLA_WIDTH = MLA_HEADS * MLA_V
NSA_WIDTH = NSA_HEADS * NSA_DV
MEM_WIDTH = MEM_HEADS * MEM_DH
MIX_WIDTH = MLA_WIDTH + NSA_WIDTH + MEM_WIDTH

IN_SPLITS = (
    MLA_Q_RANK, MLA_KV_RANK, MLA_ROPE, MLA_WIDTH,
    NSA_HEADS * NSA_DK, NSA_DK, NSA_DV, NSA_DK, NSA_DV,
    NSA_DK, NSA_DV, 3 * NSA_HEADS, NSA_WIDTH,
    MEM_WIDTH, MEM_WIDTH,
)
D_IN_2 = sum(IN_SPLITS)


def rmsnorm(x, g):
    xf = x.astype(jnp.float32)
    y = xf * lax.rsqrt(jnp.mean(xf * xf, axis=-1, keepdims=True) + EPS)
    return (y * g.astype(jnp.float32)).astype(x.dtype)

def masked_softmax(s, mask):
    s = jnp.where(mask, s.astype(jnp.float32), -1e30)
    m = jnp.max(s, axis=-1, keepdims=True)
    p = jnp.exp(s - m) * mask
    return p / (jnp.sum(p, axis=-1, keepdims=True) + 1e-20)

def alibi_slopes(n):
    return 2.0 ** (-8.0 * jnp.arange(1, n + 1, dtype=jnp.float32) / n)

def apply_rope(x, cos, sin):
    x1, x2 = jnp.split(x.astype(jnp.float32), 2, axis=-1)
    return jnp.concatenate([x1 * cos - x2 * sin, x1 * sin + x2 * cos], axis=-1).astype(x.dtype)

def to_blocks(a):
    b, s = a.shape[:2]
    return jnp.moveaxis(a.reshape(b, s // Q_BLOCK, Q_BLOCK, *a.shape[2:]), 1, 0)

def from_blocks(a):
    a = jnp.moveaxis(a, 0, 1)
    return a.reshape(a.shape[0], -1, *a.shape[3:])

def mla_mixer(c_q, c_kv, k_rope, cos, sin, q_norm_g, w_uq, kv_norm_g, w_ukv):
    b, s, _ = c_q.shape
    q = (rmsnorm(c_q, q_norm_g) @ w_uq).reshape(b, s, MLA_HEADS, MLA_NOPE + MLA_ROPE)
    q = jnp.concatenate([q[..., :MLA_NOPE],
                         apply_rope(q[..., MLA_NOPE:], cos[:, None], sin[:, None])], axis=-1)
    kv = (rmsnorm(c_kv, kv_norm_g) @ w_ukv).reshape(b, s, MLA_HEADS, MLA_NOPE + MLA_V)
    k_pe = apply_rope(k_rope, cos, sin)
    k = jnp.concatenate([kv[..., :MLA_NOPE],
                         jnp.broadcast_to(k_pe[:, :, None], (b, s, MLA_HEADS, MLA_ROPE))], axis=-1)
    v = kv[..., MLA_NOPE:]
    scale = (MLA_NOPE + MLA_ROPE) ** -0.5
    kpos = jnp.arange(s)

    def block(args):
        qb, i = args
        qpos = i * Q_BLOCK + jnp.arange(Q_BLOCK)
        sc = jnp.einsum('bqhd,bkhd->bhqk', qb, k, preferred_element_type=jnp.float32) * scale
        p = masked_softmax(sc, kpos[None, :] <= qpos[:, None])
        return jnp.einsum('bhqk,bkhd->bqhd', p.astype(v.dtype), v)

    o = lax.map(block, (to_blocks(q), jnp.arange(s // Q_BLOCK)))
    return from_blocks(o).reshape(b, s, MLA_WIDTH)

def compress(a, pe, w1, w2):
    b, s, d = a.shape
    ch = a.reshape(b, s // CMP_STRIDE, CMP_STRIDE, d)
    blocks = jnp.concatenate([ch[:, :-1], ch[:, 1:]], axis=2) + pe
    return jax.nn.silu(blocks.reshape(b, -1, CMP_LEN * d) @ w1) @ w2

def nsa_mixer(q, k_c, v_c, k_s, v_s, k_w, v_w, gate_logits,
              cmp_pe_k, cmp_pe_v, cmp_w1k, cmp_w2k, cmp_w1v, cmp_w2v):
    b, s, _ = q.shape
    q = q.reshape(b, s, NSA_HEADS, NSA_DK)
    gates = jax.nn.sigmoid(gate_logits.astype(jnp.float32)).reshape(b, s, NSA_HEADS, 3)
    scale = NSA_DK ** -0.5
    slopes = alibi_slopes(NSA_HEADS)[None, :, None, None]

    k_cmp = compress(k_c, cmp_pe_k, cmp_w1k, cmp_w2k)
    v_cmp = compress(v_c, cmp_pe_v, cmp_w1v, cmp_w2v)
    n_c = k_cmp.shape[1]
    c_start = jnp.arange(n_c) * CMP_STRIDE
    cmp_end = c_start + CMP_LEN - 1
    cmp_pos = c_start.astype(jnp.float32) + (CMP_LEN - 1) / 2.0

    n_s = s // SLC_LEN
    top_n = min(SLC_TOPN, n_s)
    k_blk = k_s.reshape(b, n_s, SLC_LEN, NSA_DK)
    v_blk = v_s.reshape(b, n_s, SLC_LEN, NSA_DV)
    s_start = jnp.arange(n_s) * SLC_LEN
    overlap = ((c_start[:, None] < s_start[None, :] + SLC_LEN) &
               (c_start[:, None] + CMP_LEN > s_start[None, :])).astype(jnp.float32)
    j = jnp.arange(n_s)

    k_wp = jnp.pad(k_w, ((0, 0), (WIN, 0), (0, 0)))
    v_wp = jnp.pad(v_w, ((0, 0), (WIN, 0), (0, 0)))

    def block(args):
        qb, gb, i = args
        t = i * Q_BLOCK + jnp.arange(Q_BLOCK)
        tf = t.astype(jnp.float32)

        sc = jnp.einsum('bqhd,bnd->bhqn', qb, k_cmp, preferred_element_type=jnp.float32) * scale
        sc = sc - slopes * (tf[:, None] - cmp_pos[None, :])
        p_cmp = masked_softmax(sc, cmp_end[None, :] <= t[:, None])
        o_cmp = jnp.einsum('bhqn,bnd->bqhd', p_cmp.astype(v_cmp.dtype), v_cmp)

        imp = jnp.einsum('bhqn,nm->bqm', p_cmp, overlap)
        cur = t // SLC_LEN
        forced = (j[None, :] == 0) | (j[None, :] == cur[:, None]) | (j[None, :] == cur[:, None] - 1)
        imp = jnp.where(forced, NEG_BIG, imp)
        imp = jnp.where(j[None, :] > cur[:, None], -NEG_BIG, imp)
        _, idx = lax.top_k(imp, top_n)
        ks = jax.vmap(lambda kb, ix: kb[ix])(k_blk, idx)
        vs = jax.vmap(lambda vb, ix: vb[ix])(v_blk, idx).reshape(b, Q_BLOCK, top_n * SLC_LEN, NSA_DV)
        spos = (idx[..., None] * SLC_LEN + jnp.arange(SLC_LEN)).reshape(b, Q_BLOCK, top_n * SLC_LEN)
        ss = jnp.einsum('bqhd,bqnld->bhqnl', qb, ks, preferred_element_type=jnp.float32)
        ss = ss.reshape(b, NSA_HEADS, Q_BLOCK, top_n * SLC_LEN) * scale
        ss = ss - slopes * (tf[None, None, :, None] - spos[:, None].astype(jnp.float32))
        p_s = masked_softmax(ss, (spos <= t[None, :, None])[:, None])
        o_slc = jnp.einsum('bhqk,bqkd->bqhd', p_s.astype(vs.dtype), vs)

        kw = lax.dynamic_slice_in_dim(k_wp, i * Q_BLOCK, WIN + Q_BLOCK, axis=1)
        vw = lax.dynamic_slice_in_dim(v_wp, i * Q_BLOCK, WIN + Q_BLOCK, axis=1)
        wpos = i * Q_BLOCK - WIN + jnp.arange(WIN + Q_BLOCK)
        rel = t[:, None] - wpos[None, :]
        sw = jnp.einsum('bqhd,bkd->bhqk', qb, kw, preferred_element_type=jnp.float32) * scale
        sw = sw - slopes * rel.astype(jnp.float32)
        p_w = masked_softmax(sw, (rel >= 0) & (rel < WIN) & (wpos[None, :] >= 0))
        o_win = jnp.einsum('bhqk,bkd->bqhd', p_w.astype(vw.dtype), vw)

        o = gb[..., 0:1] * o_cmp + gb[..., 1:2] * o_slc + gb[..., 2:3] * o_win
        return o.astype(qb.dtype)

    o = lax.map(block, (to_blocks(q), to_blocks(gates), jnp.arange(s // Q_BLOCK)))
    return from_blocks(o).reshape(b, s, NSA_WIDTH)

def memory_mixer(q, mem, mem_norm_g, w_mem_kv):
    b, s, _ = q.shape
    q = q.reshape(b, s, MEM_HEADS, MEM_DH)
    kv = (rmsnorm(mem, mem_norm_g) @ w_mem_kv).reshape(b, mem.shape[1], 2, MEM_HEADS, MEM_DH)
    k, v = kv[:, :, 0], kv[:, :, 1]
    sc = jnp.einsum('bshd,bmhd->bhsm', q, k, preferred_element_type=jnp.float32) * MEM_DH ** -0.5
    p = jax.nn.softmax(sc, axis=-1)
    return jnp.einsum('bhsm,bmhd->bshd', p.astype(v.dtype), v).reshape(b, s, MEM_WIDTH)

def hybrid_layer_2(x, mem, cos, sin, norm_g, w_in, q_norm_g, w_uq, kv_norm_g, w_ukv,
                 cmp_pe_k, cmp_pe_v, cmp_w1k, cmp_w2k, cmp_w1v, cmp_w2v,
                 mem_norm_g, w_mem_kv, w_out):
    h = rmsnorm(x, norm_g) @ w_in
    offsets = np.cumsum(IN_SPLITS)[:-1].tolist()
    (c_q, c_kv, k_rope, z_mla, q_nsa, k_c, v_c, k_s, v_s, k_w, v_w, g_nsa, z_nsa,
     q_mem, z_mem) = jnp.split(h, offsets, axis=-1)
    o_mla = mla_mixer(c_q, c_kv, k_rope, cos, sin, q_norm_g, w_uq, kv_norm_g, w_ukv) * jax.nn.silu(z_mla)
    o_nsa = nsa_mixer(q_nsa, k_c, v_c, k_s, v_s, k_w, v_w, g_nsa,
                      cmp_pe_k, cmp_pe_v, cmp_w1k, cmp_w2k, cmp_w1v, cmp_w2v) * jax.nn.silu(z_nsa)
    o_mem = memory_mixer(q_mem, mem, mem_norm_g, w_mem_kv) * jax.nn.silu(z_mem)
    o = jnp.concatenate([o_mla, o_nsa, o_mem], axis=-1) @ w_out
    return x + o.astype(x.dtype)

def second_inputs(seed: int = 0) -> dict:
    key = jax.random.key(seed)
    ks = jax.random.split(key, 20)

    def nrm(k, shape, scale):
        return jax.random.normal(k, shape, jnp.float32) * scale

    def gain(k, shape):
        return 1.0 + 0.01 * jax.random.normal(k, shape, jnp.float32)

    return {
        "x": nrm(ks[0], (BATCH, SEQ, D_MODEL), 1.0),
        "mem": nrm(ks[1], (BATCH, MEM_LEN, D_MODEL), 1.0),
        "norm_g": gain(ks[2], (DEPTH, D_MODEL)),
        "w_in": nrm(ks[3], (DEPTH, D_MODEL, D_IN_2), D_MODEL ** -0.5),
        "q_norm_g": gain(ks[4], (DEPTH, MLA_Q_RANK)),
        "w_uq": nrm(ks[5], (DEPTH, MLA_Q_RANK, MLA_HEADS * (MLA_NOPE + MLA_ROPE)), MLA_Q_RANK ** -0.5),
        "kv_norm_g": gain(ks[6], (DEPTH, MLA_KV_RANK)),
        "w_ukv": nrm(ks[7], (DEPTH, MLA_KV_RANK, MLA_HEADS * (MLA_NOPE + MLA_V)), MLA_KV_RANK ** -0.5),
        "cmp_pe_k": nrm(ks[8], (DEPTH, CMP_LEN, NSA_DK), 0.02),
        "cmp_pe_v": nrm(ks[9], (DEPTH, CMP_LEN, NSA_DV), 0.02),
        "cmp_w1k": nrm(ks[10], (DEPTH, CMP_LEN * NSA_DK, NSA_DK), (CMP_LEN * NSA_DK) ** -0.5),
        "cmp_w2k": nrm(ks[11], (DEPTH, NSA_DK, NSA_DK), NSA_DK ** -0.5),
        "cmp_w1v": nrm(ks[12], (DEPTH, CMP_LEN * NSA_DV, NSA_DV), (CMP_LEN * NSA_DV) ** -0.5),
        "cmp_w2v": nrm(ks[13], (DEPTH, NSA_DV, NSA_DV), NSA_DV ** -0.5),
        "mem_norm_g": gain(ks[14], (DEPTH, D_MODEL)),
        "w_mem_kv": nrm(ks[15], (DEPTH, D_MODEL, 2 * MEM_WIDTH), D_MODEL ** -0.5),
        "w_out": nrm(ks[16], (DEPTH, MIX_WIDTH, D_MODEL), MIX_WIDTH ** -0.5),
        "final_norm_g": gain(ks[17], (D_MODEL,)),
    }

def second_block(x, mem, norm_g, w_in, q_norm_g, w_uq, kv_norm_g, w_ukv,
              cmp_pe_k, cmp_pe_v, cmp_w1k, cmp_w2k, cmp_w1v, cmp_w2v,
              mem_norm_g, w_mem_kv, w_out, final_norm_g):
    s = x.shape[1]
    pos = jnp.arange(s, dtype=jnp.float32)
    inv_freq = ROPE_THETA ** (-jnp.arange(0, MLA_ROPE, 2, dtype=jnp.float32) / MLA_ROPE)
    ang = pos[:, None] * inv_freq[None, :]
    cos, sin = jnp.cos(ang), jnp.sin(ang)
    for l in range(DEPTH):
        x = hybrid_layer_2(x, mem, cos, sin, norm_g[l], w_in[l], q_norm_g[l], w_uq[l],
                         kv_norm_g[l], w_ukv[l], cmp_pe_k[l], cmp_pe_v[l], cmp_w1k[l],
                         cmp_w2k[l], cmp_w1v[l], cmp_w2v[l], mem_norm_g[l], w_mem_kv[l], w_out[l])
    return rmsnorm(x, final_norm_g)


def setup_inputs(seed=0):
    out = dict(first_inputs(seed))
    for name, value in second_inputs(seed + 1).items():
        if name != "x":
            out[name + "_2"] = value
    return out


def reference(
    x, c, ctx, c_ctx, w_ada, b_ada, norm1_w, w_in, w_a_up_f, b_a_f, w_a_up_b, b_a_b,
    gla_onorm_w, diff_qnorm_w, diff_knorm_w, lambda_q1, lambda_k1, lambda_q2, lambda_k2,
    diff_onorm_w, w_proj_gla, w_proj_diff, w_gate, b_gate, w_out, norm2_w, w_up, conv_w, conv_b,
    w_down, mem_2, norm_g_2, w_in_2, q_norm_g_2, w_uq_2, kv_norm_g_2, w_ukv_2, cmp_pe_k_2,
    cmp_pe_v_2, cmp_w1k_2, cmp_w2k_2, cmp_w1v_2, cmp_w2v_2, mem_norm_g_2, w_mem_kv_2, w_out_2,
    final_norm_g_2,
):
    x = first_block(
        x, c, ctx, c_ctx, w_ada, b_ada, norm1_w, w_in, w_a_up_f, b_a_f, w_a_up_b, b_a_b,
        gla_onorm_w, diff_qnorm_w, diff_knorm_w, lambda_q1, lambda_k1, lambda_q2, lambda_k2,
        diff_onorm_w, w_proj_gla, w_proj_diff, w_gate, b_gate, w_out, norm2_w, w_up, conv_w,
        conv_b, w_down,
    )
    return second_block(
        x, mem_2, norm_g_2, w_in_2, q_norm_g_2, w_uq_2, kv_norm_g_2, w_ukv_2, cmp_pe_k_2,
        cmp_pe_v_2, cmp_w1k_2, cmp_w2k_2, cmp_w1v_2, cmp_w2v_2, mem_norm_g_2, w_mem_kv_2,
        w_out_2, final_norm_g_2,
    )


_drawn_inputs = setup_inputs


def setup_inputs(seed=0):
    import zlib

    import numpy as np

    out = dict(_drawn_inputs(seed))
    spreads = {}
    factors = {'b_ada': 3.055,
     'norm1_w': 4.773,
     'b_a_f': 3.277,
     'b_a_b': 3.605,
     'gla_onorm_w': 8.0,
     'diff_qnorm_w': 8.0,
     'diff_knorm_w': 8.0,
     'lambda_q1': 6.512,
     'lambda_k1': 8.0,
     'lambda_q2': 6.924,
     'lambda_k2': 8.0,
     'diff_onorm_w': 8.0,
     'b_gate': 8.0,
     'norm2_w': 3.852,
     'conv_b': 8.0,
     'norm_g_2': 8.0,
     'q_norm_g_2': 8.0,
     'kv_norm_g_2': 8.0,
     'cmp_pe_k_2': 22.737,
     'cmp_pe_v_2': 64.0,
     'cmp_w1k_2': 5.479,
     'cmp_w2k_2': 5.324,
     'mem_norm_g_2': 8.0,
     'final_norm_g_2': 31.215}
    for name, (base, spread) in spreads.items():
        noise = np.random.default_rng([zlib.crc32(name.encode()), seed]).standard_normal(out[name].shape)
        drawn = base * np.exp(spread * noise) if base else spread * noise
        out[name] = __import__('jax').numpy.asarray(drawn.astype(out[name].dtype))
    for name, factor in factors.items():
        out[name] = (out[name] * factor).astype(out[name].dtype)
    return out
```

```python
import math
from contextlib import ExitStack

import numpy as np

import concourse.bass as bass
from concourse import mybir

F32 = mybir.dt.float32
ACT = mybir.ActivationFunctionType
ALU = mybir.AluOpType
AXX = mybir.AxisListType.X

P = 128
T = 256
D = 2048
KD = D // P
EPS = 1e-6
DFF = 5632
KF = DFF // P
GC = 16
NB = T // GC
TAU = 16.0
LAM_INIT = 0.8 - 0.6 * math.exp(0.0)
NSA_SCALE = 192 ** -0.5
MLA_SCALE = 192 ** -0.5
MEM_SCALE = 128 ** -0.5
NCMP = T // 16 - 1
MASKED = -1e30

VECTORS = [("b_ada", 96), ("norm1_w", 16), ("b_gate", 32), ("norm2_w", 16), ("conv_w", 264), ("conv_b", 88),
           ("norm_g_2", 16), ("q_norm_g_2", 4), ("kv_norm_g_2", 4), ("mem_norm_g_2", 16), ("final_norm_g_2", 16),
           ("b_a_f", 4), ("b_a_b", 4), ("gla_onorm_w", 1), ("diff_onorm_w", 1), ("c", 16), ("c_ctx", 16)]
HALF_ROWS = [("diff_qnorm_w", "diff_qnorm_w"), ("diff_knorm_w", "diff_knorm_w"),
             ("lambda_q1", "lambda_q2"), ("lambda_k1", "lambda_k2")]
VROW, _at = {}, 0
for _n, _c in VECTORS:
    VROW[_n] = _at
    _at += _c
for _a, _b in HALF_ROWS:
    VROW[_a] = _at
    _at += 1
NVEC = _at
NVEC_DMAS = sum((VROW[n] + c - 1) // P - VROW[n] // P + 1 for n, c in VECTORS) + 2 * len(HALF_ROWS)

CONSTS = [("ident", 128), ("ones", 128), ("blk64", 128), ("rot16", 128), ("rot32", 128), ("cos2d", T), ("sin2d", T),
          ("cmprel", 32), ("cmpmask", 32), ("mask_f", T), ("mask_b", T), ("headind", 2), ("rowsel", 2),
          ("cos1d", T), ("sin1d", T), ("rel", 2 * T)]
CCOL, _at = {}, 0
for _n, _c in CONSTS:
    CCOL[_n] = (_at, _c)
    _at += _c
NCONST = _at
NCONST1 = CCOL["cos1d"][0]


def shape_constants():
    c = np.zeros((P, NCONST), np.float32)

    def put(name, value):
        a, n = CCOL[name]
        c[:, a:a + n] = np.asarray(value, np.float32).reshape(P, n)

    p = np.arange(P)
    put("ident", np.eye(P))
    put("ones", np.ones((P, P)))
    put("blk64", (p[:, None] // 64 == p[None, :] // 64))

    def rotation(half):
        m = np.zeros((P, P), np.float32)
        for o in range(P):
            if (o // half) % 2 == 0:
                m[o + half, o] = -1.0
            else:
                m[o - half, o] = 1.0
        return m

    put("rot16", rotation(16))
    put("rot32", rotation(32))
    tok = np.arange(T)
    f16 = (np.float32(10000.0) ** (-(np.arange(16, dtype=np.float32)) / np.float32(16))).astype(np.float32)
    d = p % 64
    pos = np.where(d[:, None] < 32, (tok // 64)[None, :], (tok % 64)[None, :]).astype(np.float32)
    ang = pos * f16[d % 16][:, None]
    put("cos2d", np.cos(ang))
    put("sin2d", np.sin(ang))
    f32 = (np.float32(10000.0) ** (-(np.arange(0, 64, 2, dtype=np.float32)) / np.float32(64))).astype(np.float32)
    ang = tok.astype(np.float32)[None, :] * f32[d % 32][:, None]
    put("cos1d", np.cos(ang))
    put("sin1d", np.sin(ang))
    q = (np.arange(2)[None, :] * P + p[:, None]).astype(np.float32)
    rel = tok[None, None, :] - q[:, :, None]
    put("rel", np.where(rel <= 0, rel, MASKED))
    n = np.arange(16)
    end = n * 16 + 31
    ok = (end[None, None, :] <= q[:, :, None]) & (n < NCMP)[None, None, :]
    crel = (n * 16 + 15.5)[None, None, :] - q[:, :, None]
    put("cmprel", np.where(ok, crel, MASKED))
    put("cmpmask", ok)
    blk = p[:, None, None] // 16 == np.arange(8)[None, :, None]
    io = np.arange(16)[None, None, :]
    jo = p[:, None, None] % 16
    put("mask_f", np.tile((blk & (jo <= io)).reshape(P, 128), (1, 2)))
    put("mask_b", np.tile((blk & (jo >= io)).reshape(P, 128), (1, 2)))
    put("rowsel", p[:, None] % 32 == np.arange(2)[None, :])
    put("headind", p[:, None] // 64 == np.arange(2)[None, :])
    return c


SLOTS = 4
ADA_LATE = 16
SLOT_WORDS = 2048


def panel(w, col, width=512, rows=D, kt=4, step=0, kp=P):
    n = rows // kp
    return [(w, r * kp, min(kt, n - r), kp, col, width, step) for r in range(0, n, kt)]


def phases():
    out = []

    def phase(name, iters, jobs):
        out.append((name, iters, jobs))

    phase("ada_early", 4, [(panel("w_ada", 0, step=1024), (0,)), (panel("w_ada", 512, step=1024), (1,))])
    phase("gla_in", 1, [(panel("w_in", 512), (0, 1)), (panel("w_in", 1024), (0, 1)), (panel("w_in", 1536), (0, 1)),
                        (panel("w_in", 3072, 32, kt=16), (0, 1)), (panel("w_in", 0), (0,))])
    phase("dk_in", 1, [(panel("w_in", 4128), (0, 1)), (panel("w_in", 4640), (0, 1))])
    phase("dv_in", 1, [(panel("w_in", 5152), (0, 1)), (panel("w_in", 5664), (0, 1))])
    phase("dq_in", 1, [(panel("w_in", 3104), (0,)), (panel("w_in", 3616), (1,)),
                       (panel("w_in", 2048), (0,)), (panel("w_in", 2560), (1,))])
    phase("ada_late", 1, [(panel("w_ada", 4096 + 512 * n), (n % 2,)) for n in range(ADA_LATE)])
    phase("merge", 4, [(panel("w_gate", 0, step=512), (0,)), (panel("w_proj_gla", 0, rows=1024, step=512), (1,)),
                       (panel("w_gate", D, step=512), (0,)), (panel("w_proj_diff", 0, rows=1024, step=512), (1,))])
    phase("out", 2, [(panel("w_out", 0, step=1024), (0,)), (panel("w_out", 512, step=1024), (1,))])
    phase("up", KF // 4, [(panel("w_up", 0, step=512), (0,)), (panel("w_up", DFF, step=512), (1,))])
    phase("down", 2, [(panel("w_down", 0, rows=DFF, step=1024), (0,)), (panel("w_down", 512, rows=DFF, step=1024), (1,))])
    phase("mem", 1, [(panel("w_mem_kv_2", 0), (0,)), (panel("w_mem_kv_2", 512), (1,))])
    jobs = [(panel("w_in_2", c, w, kt=min(16, SLOT_WORDS // w)), (n % 2,)) for n, (_, c, w) in enumerate(IN2)]
    phase("in2", 1, jobs)
    phase("uq", 1, [(panel("w_uq_2", 384 * n, 384, rows=512), (n % 2,)) for n in range(4)])
    phase("ukv", 1, [(panel("w_ukv_2", 512 * n, 512, rows=512), (n % 2,)) for n in range(4)])
    phase("cmp", 1, [(panel("cmp_w1k_2", 0, 192, rows=6144, kt=8, kp=96), (0,)),
                     (panel("cmp_w1v_2", 0, 128, rows=4096, kt=16), (1,))])
    phase("out2", 2, [(panel("w_out_2", 0, step=1024), (0,)), (panel("w_out_2", 512, step=1024), (1,))])
    return out


IN2 = [("cq", 0, 512), ("ckv", 512, 512), ("krope", 1024, 64), ("z0", 1088, 512), ("z1", 1600, 512),
       ("qn0", 2112, 384), ("qn1", 2496, 384), ("kc", 2880, 192), ("vc", 3072, 128), ("ks", 3200, 192),
       ("vs", 3392, 128), ("kw", 3520, 192), ("vw", 3712, 128), ("gn", 3840, 12), ("z2", 3852, 512),
       ("qm", 4364, 512), ("z3", 4876, 512)]


class Stream:

    def __init__(self):
        self.phases = {n: (it, jobs) for n, it, jobs in phases()}
        self.info, last_use, g = {}, {}, 0
        landed = [0] * SLOTS
        uses = [0, 0]
        start = 0
        self.start = {}
        for name, (iters, jobs) in self.phases.items():
            n = sum(len(ch) for ch, _ in jobs)
            self.start[name] = start
            near = [None] * n
            for i in range(iters):
                for j in range(n):
                    s = (start + j) % SLOTS
                    far = g + i * n + j - last_use.get(s, -10 ** 6)
                    near[j] = far if near[j] is None else min(near[j], far)
                    last_use[s] = g + i * n + j
            near = [min(x, SLOTS) for x in near]
            per_slot = [sum((start + j) % SLOTS == s for j in range(n)) for s in range(SLOTS)]
            per_set = [sum(k in sets for _, sets in jobs) for k in (0, 1)]
            self.info[name] = (g, n, near, list(landed), per_slot, list(uses), per_set)
            start = (start + n) % SLOTS
            g += iters * n
            landed = [a + iters * b for a, b in zip(landed, per_slot)]
            uses = [a + iters * b for a, b in zip(uses, per_set)]

    def chunks(self, name):
        return [c for ch, _ in self.phases[name][1] for c in ch]

    def iters(self, name):
        return self.phases[name][0]

    def slot(self, name, j):
        return (self.start[name] + j) % SLOTS

    def slot_free(self, name, i, j):
        g, n, near, _, _, _, _ = self.info[name]
        return i * n + (g + j - near[j] + SLOTS + 1)

    def landed(self, name, i, j):
        _, _, _, landed, per_slot, _, _ = self.info[name]
        s = self.slot(name, j)
        return i * (16 * per_slot[s]) + 16 * (landed[s] + j // SLOTS + 1)

    def first(self, name, job):
        return sum(len(ch) for ch, _ in self.phases[name][1][:job])

    def done(self, name, i, job):
        g, n = self.info[name][:2]
        return i * n + (g + self.first(name, job + 1) + SLOTS)

    def set_uses(self, name, i, job, s):
        _, _, _, _, _, uses, per_set = self.info[name]
        before = sum(s in sets for _, sets in self.phases[name][1][:job])
        return i * per_set[s] + (uses[s] + before + 1)


def build(nc, dram, out_dram, x_spill):
    st = Stream()
    ctx = ExitStack()
    with ctx:
        def sb(name, shape):
            return ctx.enter_context(nc.sbuf_tensor(name, shape, F32))

        sems = {}

        def S(name):
            if name not in sems:
                sems[name] = ctx.enter_context(nc.semaphore(name))
            return sems[name]

        ring = sb("ring", [P, SLOTS, SLOT_WORDS])
        hL = sb("hL", [P, KD, T])
        hC = sb("hC", [P, KD, T])
        cst = sb("cst", [P, NCONST1])
        vec = sb("vec", [P, NVEC])
        ada = sb("ada", [P, 96, 2])
        csil = sb("csil", [P, KD, 32])
        ctmp = sb("ctmp", [P, 32])
        amod = sb("amod", [P, 3, KD])
        nbgate = sb("nbgate", [P, 32])
        rstd = sb("rstd", [P, 2, 512])
        small = sb("small", [P, 64])
        refs = sb("refs", [P, 2, 8, 17])
        shared = sb("shared", [P, 2, 512])
        wup = shared[0:32, :, :]
        big = sb("big", [P, 30240])
        psum = ctx.enter_context(nc.psum_tensor("psum", [P, 8 * 512], F32))

        def bank(b, a=0, n=512):
            return psum[:, b * 512 + a:b * 512 + a + n]

        def two_banks(n):
            return psum[:, 6 * 512:8 * 512].rearrange("p (a b) -> p a b", a=2)[:, :, 0:n]

        def set_of(s):
            return psum[:, s * 1024:s * 1024 + 1024]

        def C(name, parts=P):
            a, n = CCOL[name]
            if a >= NCONST1:
                return shared[0:parts, :, :].rearrange("p a b -> p (a b)")[:, a - NCONST1:a - NCONST1 + n]
            return cst[0:parts, a:a + n]

        def V(name, k=0, n=1):
            return vec[:, VROW[name] + k:VROW[name] + k + n]

        def cut(flat, *shape):
            if len(shape) == 2:
                return flat.rearrange("p (a b) -> p a b", a=shape[0])
            if len(shape) == 3:
                return flat.rearrange("p (a b c) -> p a b c", a=shape[0], b=shape[1])
            return flat

        def area(at, *shape):
            return cut(big[:, at:at + int(np.prod(shape))], *shape)

        def carea(at, *shape):
            return cut(hC[:, :, :].rearrange("p a b -> p (a b)")[:, at:at + int(np.prod(shape))], *shape)

        def larea(at, *shape):
            return cut(hL[:, :, :].rearrange("p a b -> p (a b)")[:, at:at + int(np.prod(shape))], *shape)

        vstage = area(0, 5, P)
        nat = area(1024, 4, D)
        xT0 = area(9216, KD, T)
        cT0 = area(13312, KD, T)
        rows_early = area(17408, 2, 512)
        gq = area(0, 4, T)
        gk = area(1024, 4, 2, T)
        gv = area(3072, 4, 1024)
        asum = area(5120, 2, 512)
        qx = area(6144, 4, T)
        gr = area(7168, 8, T)
        dq = area(9216, 8, T)
        dk = area(11264, 8, 2, T)
        dv = area(15360, 4, 1024)
        bufs = [area(19456 + 2056 * d, 4, 2, 257) for d in range(2)]
        KC = 23568
        zb = area(KC, 4, 512)
        ztmp = area(KC + 2048, 2048)
        smem = area(29200, 8, 128)
        kst = area(9216, 2, 2, T)
        pd = [carea(0, GC, 8, GC), carea(2048, GC, 8, GC)]
        yg = area(1024, 8, T)
        ga = rstd[0:32, 0, :]
        dp = area(KC, 4, 512)
        dsq = area(KC, 2, 512)
        dmul = area(KC + 1024, 2, 512)
        daT = [area(KC + 2048 + 1024 * b, 4, T) for b in range(2)]
        mT = area(11264, KD, T)
        gsb = [area(24000 + 1024 * b, 4, T) for b in range(2)]
        x1 = area(19456, KD, T)
        x0 = area(15360, KD, T)
        fh = area(0, KF, T)
        ftap = [area(11264 + 1024 * b, 4, T) for b in range(2)]
        fexp = area(13312, 4, T)
        memnat = area(23552, 2, D)
        sq2 = area(0, KD, T)
        cq = area(0, 4, T)
        ckv = area(1024, 4, T)
        kpe = area(2048, T)
        zT = area(2304, 16, T)
        qn = area(6400, 8, T)
        kcT = area(8448, 2, T)
        vcT = area(8960, T)
        ksT = area(9216, 2, T)
        kwT = area(9728, 2, T)
        vs = area(10240, 2, P)
        vw = area(10496, 2, P)
        gn = area(10752, T)
        qm = area(11008, 4, T)
        mqn = area(12032, 8, T)
        mqr = area(14080, 4, T)
        mkn = area(15104, 8, T)
        mv = area(17152, 2, 1024)
        causal = area(19200, 256)
        obuf = area(23552, 24, T)
        km = carea(0, 4, T)
        vm = carea(1024, 2, 512)
        ssb = carea(2048, 2, T)
        prob = carea(2560, 2, T)
        aT = [carea(3072 + 512 * b, 2, T) for b in range(2)]
        kcp = larea(0, 2, 32, NCMP)
        vcp = larea(960, 32, NCMP)
        hidk = larea(1440, 2, 16)
        hidv = larea(1472, 16)
        hexp = larea(1488, 48)
        kcmp = larea(1536, 2, 16)
        vcmp = larea(1568, 128)
        w2k = larea(1696, 2, 192)
        w2v = larea(2080, 128)
        pek = larea(2208, 192)
        pev = larea(2400, 128)
        peT = larea(2528, 3, 32)
        rtmp = larea(2624, 2, 512)
        rtmpsq = [area(23552 + 1024 * b, 4, T) for b in range(2)]
        onat = area(0, 2, D)

        block = ctx.enter_context(nc.Block())

        @block.sync
        def _(sp):
            def load(name, i, c, j):
                w, row0, kt, kp, col, width, step = c
                s = st.slot(name, j)
                sp.wait_ge(S("chunks_multiplied"), st.slot_free(name, i, j))
                a = col + i * step
                rows = dram[w][row0:row0 + kt * kp, :].rearrange("(k p) n -> p k n", p=kp)
                sp.dma_start(ring[0:kp, s, 0:kt * width].rearrange("p (k n) -> p k n", k=kt),
                             rows[:, :, bass.ds(a, width)] if st.iters(name) > 1 else rows[:, :, a:a + width]
                             ).then_inc(S(f"slot_loaded{s}"), 16)

            for name in st.phases:
                chunks = st.chunks(name)
                if st.iters(name) > 1:
                    with sp.Fori(0, st.iters(name)) as i:
                        for j, c in enumerate(chunks):
                            load(name, i, c, j)
                else:
                    for j, c in enumerate(chunks):
                        load(name, 0, c, j)
            for t in range(2):
                sp.wait_ge(S("out_copied"), 4 * (t + 1))
                sp.dma_start(out_dram[0, t * P:(t + 1) * P, :], onat[:, t, :]).then_inc(S("out_stored"), 16)
            sp.wait_ge(S("out_stored"), 32)

        @block.gpsimd
        def _(pool):
            pool.dma_start(cst[:, :], dram["consts"][:, 0:NCONST1]).then_inc(S("consts_loaded"), 16)
            pool.memset(csil[:, :, :], 0.0).then_inc(S("csil_cleared"), 1)
            nvec = 0

            def rows_in(row, n, view):
                nonlocal nvec
                done = 0
                while done < n:
                    k = min(n - done, P - (row + done) % P)
                    r = row + done
                    pool.dma_start(vstage[r % P:r % P + k, r // P, :], view[done:done + k, :]
                                   ).then_inc(S("vectors_loaded"), 16)
                    nvec += 1
                    done += k

            for name, n in VECTORS:
                ap = dram[name]
                if name == "c_ctx":
                    ap = ap.rearrange("(t p) -> t p", p=P)
                elif name == "final_norm_g_2":
                    ap = ap.rearrange("(t p) -> t p", p=P)
                elif name == "conv_w":
                    ap = ap.rearrange("j (t p) -> (j t) p", p=P)
                else:
                    ap = ap.rearrange("a (t p) -> (a t) p", p=P)
                rows_in(VROW[name], n, ap)
            for a, b in HALF_ROWS:
                for h, name in enumerate((a, b)):
                    r = VROW[a]
                    pool.dma_start(vstage[r % P:r % P + 1, r // P, 64 * h:64 * h + 64], dram[name]
                                   ).then_inc(S("vectors_loaded"), 16)
                    nvec += 1
            assert nvec == NVEC_DMAS, nvec
            for t in range(2):
                pool.dma_start(nat[:, t, :], dram["x"][0, t * P:(t + 1) * P, :]).then_inc(S(f"tokens_loaded{t}"), 16)
            for t in range(2):
                pool.dma_start(nat[:, 2 + t, :], dram["ctx"][0, t * P:(t + 1) * P, :]
                               ).then_inc(S(f"tokens_loaded{2 + t}"), 16)
            pool.memset(wup[:, :, :], 0.0).then_inc(S("wup_cleared"), 1)
            pool.wait_ge(S("wup_cleared"), 1)
            pool.dma_start(wup[0:16, 0, :], dram["w_a_up_f"]).then_inc(S("wup_loaded"), 16)
            pool.dma_start(wup[16:32, 1, :], dram["w_a_up_b"]).then_inc(S("wup_loaded"), 16)
            pool.wait_ge(S("x_transposed"), 8)
            pool.dma_start(x_spill, xT0[:, :, :]).then_inc(S("x_spilled"), 16)
            pool.wait_ge(S("gates_summed"), 2)
            pool.memset(area(KC, 5632), 0.0).then_inc(S("kc_cleared"), 1)
            pool.wait_ge(S("diff_pv_done"), 8)
            pool.dma_start(x0[:, :, :], x_spill).then_inc(S("x_back"), 16)
            for s in range(2):
                pool.wait_ge(S(f"set_read{s}"), st.set_uses("up", 0, s, s))
            pool.dma_start(shared[:, :, :].rearrange("p a b -> p (a b)"), dram["consts"][:, NCONST1:NCONST]
                           ).then_inc(S("consts2_loaded"), 16)
            for t in range(2):
                pool.dma_start(memnat[:, t, :], dram["mem_2"][0, t * P:(t + 1) * P, :]).then_inc(S("mem_loaded"), 16)
            pool.wait_ge(S("chunks_multiplied"), st.done("in2", 0, len(IN2) - 1))
            pool.dma_start(w2k[0:96, :, :], dram["cmp_w2k_2"].rearrange("(h p) n -> p h n", p=96)
                           ).then_inc(S("cmp_loaded"), 16)
            pool.dma_start(w2v[:, :], dram["cmp_w2v_2"]).then_inc(S("cmp_loaded"), 16)
            pool.dma_start(pek[0:32, :], dram["cmp_pe_k_2"]).then_inc(S("cmp_loaded"), 16)
            pool.dma_start(pev[0:32, :], dram["cmp_pe_v_2"]).then_inc(S("cmp_loaded"), 16)
            pool.wait_ge(S("x_spilled"), 16)

        def kc(d, b):
            if d == 0:
                at, n, tok = ((b - 1) * 128, 128, 0) if b <= 8 else (1024 + (b - 9) * 256, 256, 0)
            else:
                at, n, tok = (2816 + b * 256, 256, 0) if b <= 6 else (2816 + 1792 + (b - 7) * 128, 128, 128)
            return big[:, KC + at:KC + at + n], tok

        def key_range(d, b):
            return (0, GC * b) if d == 0 else (GC * (b + 1), T)

        BLOCKS = [range(1, NB), range(0, NB - 1)]

        OUTS = [("mla", h, h) for h in range(8)]
        OUTS += [(k, 8 + 3 * h + n, h) for h in range(4) for n, k in enumerate(("cmp", "slc", "win"))]
        OUTS += [("mem", 20 + h, h) for h in range(4)]

        def keys_seen(kind, qt):
            return NCMP if kind == "cmp" else T if kind == "mem" else P * (qt + 1)

        @block.tensor
        def _(pe):
            mm = nc.tensor.matmul

            def gemm(name, i, job, products):
                chunks, sets = st.phases[name][1][job]
                started, k0, j0 = set(), 0, st.first(name, job)
                for q, (_, _, kt, kp, _, width, _) in enumerate(chunks):
                    s = st.slot(name, j0 + q)
                    pe.wait_ge(S(f"slot_loaded{s}"), st.landed(name, i, j0 + q))
                    if q == 0:
                        for k in sets:
                            pe.wait_ge(S(f"set_read{k}"), st.set_uses(name, i, job, k))
                    slot = ring[0:kp, s, 0:kt * width].rearrange("p (k n) -> p k n", k=kt)
                    todo = [products(k0 + k, slot[:, k, :]) for k in range(kt)]
                    for m in range(len(todo[0])):
                        for k in range(kt):
                            out, b, lhsT, rhs = todo[k][m]
                            last = mm(out, lhsT, rhs, start=b not in started,
                                      stop=q == len(chunks) - 1 and k == kt - 1, skip_group_check=True)
                            started.add(b)
                    k0 += kt
                    last.then_inc(S("chunks_multiplied"), 1)

            def features(s, act, width=512, m=P):
                def products(k, w):
                    return [(set_of(s)[0:min(m, width - c), n * T:(n + 1) * T], (s, n // 2),
                             w[:, c:min(c + m, width)], act[:, k, :])
                            for n, c in enumerate(range(0, width, m))]
                return products

            def tokens(s, act, width=512):
                def products(k, w):
                    return [(set_of(s)[:, t * 512:t * 512 + width], (s, t), act[:, k, t * P:(t + 1) * P], w)
                            for t in range(2)]
                return products

            def both(a, b):
                return lambda k, w: a(k, w) + b(k, w)

            def transposed(out, in_):
                n = in_.shape[0]
                return nc.tensor.transpose(out, in_, C("ident", n)[:, 0:n])

            def sums(out, weights, sq, tiles):
                for k in range(tiles):
                    last = mm(out, weights, sq[:, k, :], start=k == 0, stop=k == tiles - 1)
                return last

            pe.sem_inc(S("chunks_multiplied"), SLOTS)
            for s in range(2):
                pe.sem_inc(S(f"set_read{s}"), 1)
            pe.wait_ge(S("consts_loaded"), 16)
            pe.wait_ge(S("vectors_loaded"), 16 * NVEC_DMAS)
            for n in range(5):
                rows = min(P, NVEC - n * P)
                last = transposed(bank(6 + n // 4, (n % 4) * P, rows), vstage[0:rows, n, :])
            last.then_inc(S("vectors_transposed"), 1)
            for n in range(16):
                t, g = n // 4, n % 4
                pe.wait_ge(S(f"tokens_loaded{t}"), 16)
                if n >= 2:
                    pe.wait_ge(S("x_transposed"), n - 1)
                for k in range(4):
                    last = transposed(bank(4 + n % 2, k * P, P), nat[:, t, (4 * g + k) * P:(4 * g + k + 1) * P])
                last.then_inc(S("x_in_psum"), 1)
            pe.wait_ge(S("vectors_copied"), 1)
            for n, sq in enumerate((hL, hC)):
                pe.wait_ge(S("x_squared"), n + 1)
                sums(bank(6 + n, 0, T), C("ones"), sq, KD).then_inc(S("x_summed"), 1)

            def ada_rows(name, i, job):
                s = job % 2
                gemm(name, i, job, lambda k, w: [
                    (bank(2 * s)[32 * (k % 4):32 * (k % 4) + 32, :], (s, k % 4), csil[:, k, :], w)])

            def ada_fold(s, rows, n):
                pe.wait_ge(S("ada_rows_copied"), n)
                for m in range(4):
                    last = mm(bank(2 * s + 1, 2 * m, 2), rows[:, s, m * P:(m + 1) * P], C("rowsel"),
                              start=True, stop=True)
                last.then_inc(S("ada_folded"), 1)

            def ada_late(first, last):
                for n in range(first, last):
                    ada_rows("ada_late", 0, n)
                    if n:
                        ada_fold((n - 1) % 2, shared, 8 + n)
                if last == ADA_LATE:
                    ada_fold((ADA_LATE - 1) % 2, shared, 8 + ADA_LATE)

            pe.wait_ge(S("c_activated"), 1)
            with pe.Fori(0, st.iters("ada_early")) as i:
                for job in range(2):
                    ada_rows("ada_early", i, job)
                for job in range(2):
                    ada_fold(job, rows_early, i * 2 + (job + 1))
            pe.wait_ge(S("h_ready"), 2)
            gemm("gla_in", 0, 0, both(features(0, hL), features(1, hC)))
            gemm("gla_in", 0, 1, both(tokens(0, hL), tokens(1, hC)))
            gemm("gla_in", 0, 2, both(tokens(0, hL), tokens(1, hC)))
            gemm("gla_in", 0, 3, both(features(0, hL, 32), features(1, hC, 32)))
            gemm("gla_in", 0, 4, features(0, hL))
            pe.wait_ge(S("set_read0"), st.set_uses("gla_in", 0, 4, 0))
            pe.wait_ge(S("set_read1"), st.set_uses("dk_in", 0, 0, 1))
            pe.wait_ge(S("wup_loaded"), 32)
            for n in range(8):
                if n >= 4:
                    pe.wait_ge(S("z_read"), n - 3)
                mm(bank(4 + n % 4), wup[:, n // 4, (n % 4) * P:(n % 4 + 1) * P], ga, start=True, stop=True
                   ).then_inc(S("z_ready"), 1)
            for job in range(2):
                gemm("dk_in", 0, job, both(features(0, hL), features(1, hC)))
            pe.wait_ge(S("z_read"), 8)
            for n in range(8):
                pe.wait_ge(S("ctx_keys_scaled"), n + 1)
                if n:
                    pe.wait_ge(S("ctx_keys_copied"), n)
                for t in range(2):
                    last = transposed(bank(6, t * P, P), kst[:, n % 2, 0, t * P:(t + 1) * P])
                last.then_inc(S("ctx_keys_transposed"), 1)
                pe.wait_ge(S("ctx_keys_copied"), n + 1)
                if n:
                    pe.wait_ge(S("states_copied"), n)
                for h in range(2):
                    head = 2 * (n // 2) + h
                    for t in range(2):
                        last = mm(bank(7, 0, P)[64 * h:64 * h + 64, :], kst[:, n % 2, 1, t * P + 64 * h:t * P + 64 * h + 64],
                                  gv[:, 2 + t, head * P:(head + 1) * P], start=t == 0, stop=t == 1)
                last.then_inc(S("states_ready"), 1)
            for job in range(2):
                gemm("dv_in", 0, job, both(tokens(0, hL), tokens(1, hC)))

            def gla_diagonals(p, first):
                if p and not first:
                    pe.wait_ge(S("gla_normed"), p)
                for e in (first, first + 1):
                    pe.wait_ge(S("gla_diag_ready"), 4 * p + e + 1)
                    for io in range(GC):
                        last = mm(bank(6, (e * GC + io) * 2, 2), pd[e % 2][:, io, :, :].rearrange("p b j -> p (b j)"),
                                  C("headind"), start=True, stop=True)
                    last.then_inc(S("gla_diag_summed"), 1)

            def gla_pair(p):
                pe.wait_ge(S("gla_operands_ready"), p + 1)
                if p:
                    pe.wait_ge(S("gla_normed"), p)
                else:
                    pe.wait_ge(S("states_copied"), 8)
                for h in range(2):
                    first = True
                    for d in range(2):
                        for b in BLOCKS[d]:
                            keys, tok = kc(d, b)
                            lo, hi = key_range(d, b)
                            for t in range(2):
                                if hi > t * P and lo < (t + 1) * P:
                                    last = mm(bank(4 + h, t * T + GC * b, GC),
                                              keys[64 * h:64 * h + 64, t * P - tok:(t + 1) * P - tok],
                                              qx[64 * h:64 * h + 64, 2 + d, GC * b:GC * (b + 1)],
                                              start=first, stop=True, skip_group_check=True)
                                    first = False
                last.then_inc(S("gla_blocks_done"), 1)
                gla_diagonals(p, 2)
                pe.wait_ge(S("gla_scores_ready"), 2 * p + 2)
                for h in range(2):
                    head = 2 * p + h
                    for t in range(2):
                        mm(bank(6 + h, 0, T), gv[:, t, head * P:(head + 1) * P], asum[:, h, t * T:(t + 1) * T],
                           start=t == 0, stop=False)
                    for d in range(2):
                        last = mm(bank(6 + h, 0, T), smem[64 * h:64 * h + 64, 2 * p + d, :],
                                  qx[64 * h:64 * h + 64, d, :], start=False, stop=d == 1)
                last.then_inc(S("gla_out_ready"), 1)
                pe.wait_ge(S("gla_squared"), p + 1)
                mm(bank(4), C("ones"), rstd[:, 1, :], start=True, stop=True).then_inc(S("gla_summed"), 1)

            for pair in range(4):
                for half in range(2):
                    if pair < 2:
                        gemm("dq_in", 0, 2 * pair + half, features(half, hL))
                    else:
                        ada_late(6 * (pair - 2) + 3 * half, 6 * (pair - 2) + 3 * half + 3)
                    if half == 0:
                        gla_diagonals(pair, 0)
                gla_pair(pair)

            pe.wait_ge(S("gla_normed"), 4)
            for g in range(12):
                if g % 3 == 0:
                    ada_late(12 + g // 3, 13 + g // 3)
                pe.wait_ge(S("qk_squared"), g + 1)
                mm(bank(4 + g % 2), C("blk64"), dsq[:, g % 2, :], start=True, stop=True).then_inc(S("qk_summed"), 1)
                pe.wait_ge(S("qk_normed"), g + 1)
                n = 512 if g < 4 else T
                src = dq[:, 2 * g:2 * g + 2, :].rearrange("p a b -> p (a b)") if g < 4 else dk[:, g - 4, 0, :]
                mm(bank(6 + g % 2, 0, n), C("rot16"), src, start=True, stop=True).then_inc(S("qk_rotated"), 1)
            pe.wait_ge(S("lambda_products"), 1)
            pe.wait_ge(S("qk_done"), 12)
            for h in range(2):
                last = mm(bank(6 + h, 0, 1), C("ones")[64 * h:64 * h + 64, :], small[64 * h:64 * h + 64, 0:1],
                          start=True, stop=True)
            last.then_inc(S("lambda_summed"), 1)
            pe.wait_ge(S("lambda_done"), 1)

            def diff_scores(n):
                h, qt, m = n // 4, (n // 2) % 2, n % 2
                if n >= 2:
                    pe.wait_ge(S("diff_exps"), n - 1)
                mm(bank(4 + m), dq[64 * m:64 * m + 64, h, qt * P:(qt + 1) * P],
                   dk[64 * m:64 * m + 64, h, :, :].rearrange("p a b -> p (a b)"), start=True, stop=True
                   ).then_inc(S("diff_scores_ready"), 1)

            def diff_values(u):
                h, qt = u // 2, u % 2
                pe.wait_ge(S("diff_probs_ready"), u + 1)
                if u:
                    pe.wait_ge(S("diff_probs_copied"), u)
                for k in range(4):
                    last = transposed(bank(6, k * P, P), dp[:, 2 * (u % 2), k * P:(k + 1) * P])
                last.then_inc(S("diff_probs_transposed"), 1)
                if qt == 1:
                    pe.wait_ge(S("diff_probs_copied"), u + 1)
                    if h:
                        pe.wait_ge(S("diff_out_copied"), h)
                    for k in range(4):
                        last = mm(bank(7, 0, T), dv[:, k, h * P:(h + 1) * P], daT[h % 2][:, k, :],
                                  start=k == 0, stop=k == 3)
                    last.then_inc(S("diff_pv_done"), 1)

            for u in range(16):
                diff_scores(2 * u)
                diff_scores(2 * u + 1)
                if u:
                    diff_values(u - 1)
            diff_values(15)
            for g in range(4):
                pe.wait_ge(S("diff_squared"), g + 1)
                if g >= 2:
                    pe.wait_ge(S("diff_normed"), g - 1)
                mm(bank(4 + g % 2), C("ones"), dsq[:, g % 2, :], start=True, stop=True).then_inc(S("diff_summed"), 1)

            pe.wait_ge(S("gla_gated"), 1)
            pe.wait_ge(S("diff_normed"), 4)
            with pe.Fori(0, st.iters("merge")) as i:
                gemm("merge", i, 0, features(0, hL))
                gemm("merge", i, 1, features(1, yg))
                gemm("merge", i, 2, features(0, hL))
                gemm("merge", i, 3, features(1, dq))
            pe.wait_ge(S("merged"), st.iters("merge") + 1)
            with pe.Fori(0, st.iters("out")) as i:
                for job in range(2):
                    gemm("out", i, job, features(job, mT))
            pe.wait_ge(S("x1_squared"), 1)
            sums(bank(4, 0, T), C("ones"), hC, KD).then_inc(S("x1_summed"), 1)
            pe.wait_ge(S("h2_ready"), 1)
            with pe.Fori(0, st.iters("up")) as i:
                for job in range(2):
                    gemm("up", i, job, features(job, hL))
            pe.wait_ge(S("ffn_hidden"), st.iters("up") + 1)
            with pe.Fori(0, st.iters("down")) as i:
                for job in range(2):
                    gemm("down", i, job, features(job, fh))

            for n in range(8):
                t, g = n // 4, n % 4
                if n == 0:
                    pe.wait_ge(S("mem_loaded"), 32)
                if n >= 2:
                    pe.wait_ge(S("mem_transposed"), n - 1)
                for k in range(4):
                    last = transposed(bank(4 + n % 2, k * P, P), memnat[:, t, (4 * g + k) * P:(4 * g + k + 1) * P])
                last.then_inc(S("mem_in_psum"), 1)
            pe.wait_ge(S("mem_squared"), 1)
            sums(bank(6, 0, T), C("ones"), sq2, KD).then_inc(S("mem_summed"), 1)
            pe.wait_ge(S("x2_squared"), 1)
            sums(bank(7, 0, T), C("ones"), hL, KD).then_inc(S("x2_summed"), 1)
            pe.wait_ge(S("mem_ready"), 1)
            gemm("mem", 0, 0, features(0, hC))
            gemm("mem", 0, 1, tokens(1, hC))
            pe.wait_ge(S("h3_ready"), 1)
            for n, (name, _, width) in enumerate(IN2):
                s = n % 2
                if name in ("vs", "vw"):
                    gemm("in2", 0, n, tokens(s, hL, width))
                elif name == "krope":
                    def twice(k, w, s=s):
                        return [(set_of(s)[64 * b:64 * b + 64, 0:T], (s, 0, b), w, hL[:, k, :]) for b in range(2)]
                    gemm("in2", 0, n, twice)
                else:
                    gemm("in2", 0, n, features(s, hL, width, 96 if name in ("qn0", "qn1", "kc", "ks", "kw") else P))
                if name == "ckv":
                    for v in range(2):
                        pe.wait_ge(S("lowrank_squared"), v + 1)
                        sums(bank(4 + v, 0, T), C("ones"), rtmpsq[v], 4).then_inc(S("lowrank_summed"), 1)
            for n in range(4):
                s = n % 2
                pe.wait_ge(S("cq_normed"), 1)

                def query_pair(k, w, s=s):
                    return [(set_of(s)[:, 0:T], (s, 0), w[:, 0:P], cq[:, k, :]),
                            (set_of(s)[:, T:2 * T], (s, 0), w[:, 192:192 + P], cq[:, k, :]),
                            (set_of(s)[0:64, 2 * T:3 * T], (s, 1, 0), w[:, P:192], cq[:, k, :]),
                            (set_of(s)[64:P, 2 * T:3 * T], (s, 1, 1), w[:, 192 + P:384], cq[:, k, :])]
                gemm("uq", 0, n, query_pair)
            for n in range(4):
                s = n % 2
                pe.wait_ge(S("ckv_normed"), 1)

                def key_pair(k, w, s=s):
                    values = w.rearrange("p (h c) -> p h c", h=2)[:, :, P:2 * P]
                    return [(set_of(s)[:, 0:T], (s, 0), w[:, 0:P], ckv[:, k, :]),
                            (set_of(s)[:, T:2 * T], (s, 0), w[:, 2 * P:3 * P], ckv[:, k, :]),
                            (set_of(s)[:, 2 * T:3 * T], (s, 1), ckv[:, k, 0:P], values),
                            (set_of(s)[:, 3 * T:4 * T], (s, 1), ckv[:, k, P:2 * P], values)]
                gemm("ukv", 0, n, key_pair)
            for n in range(5):
                if n == 0:
                    for s in range(2):
                        pe.wait_ge(S(f"set_read{s}"), st.set_uses("ukv", 0, s, s))
                if n >= 2:
                    pe.wait_ge(S("rope_done"), n - 1)
                src = mqr[:, n, :] if n < 4 else kpe
                mm(bank(4 + n % 2, 0, T), C("rot32"), src, start=True, stop=True).then_inc(S("rope_rotated"), 1)
            pe.wait_ge(S("cmp_loaded"), 64)
            pe.wait_ge(S("rope_done"), 5)
            for h in range(2):
                transposed(bank(6, 32 * h, 32)[0:96, :], pek[0:32, 96 * h:96 * h + 96])
            transposed(bank(6, 64, 32), pev[0:32, :]).then_inc(S("pe_transposed"), 1)
            pe.wait_ge(S("cmp_blocks_ready"), 1)
            gemm("cmp", 0, 0, lambda k, w: [
                (set_of(0)[0:96, m * 16:m * 16 + NCMP], (0, 0), w[:, 96 * m:96 * m + 96], kcp[0:96, k % 2, k // 2, :])
                for m in range(2)])
            gemm("cmp", 0, 1, lambda k, w: [(set_of(1)[:, 0:NCMP], (1, 0), w, vcp[:, k, :])])
            for s in range(2):
                pe.wait_ge(S(f"set_read{s}"), st.set_uses("out2", 0, s, s))
            for m in range(2):
                for k in range(2):
                    mm(bank(6, 16 * m, NCMP)[0:96, :], w2k[0:96, k, 96 * m:96 * m + 96], hidk[0:96, k, 0:NCMP],
                       start=k == 0 and m == 0, stop=k == 1, skip_group_check=True)
            mm(bank(7, 0, P)[0:NCMP, :], hidv[:, 0:NCMP], w2v[:, :], start=True, stop=True
               ).then_inc(S("cmp_projected"), 1)
            pe.wait_ge(S("cmp_done"), 1)

            def scores2(u):
                kind, o, h = OUTS[u // 2]
                qt = u % 2
                q = slice(qt * P, (qt + 1) * P)
                n = keys_seen(kind, qt)
                out = bank(4 + u % 2, 0, n)
                if u >= 2:
                    pe.wait_ge(S("exps2"), u - 1)
                if kind == "mla":
                    r = slice(64 * (h % 2), 64 * (h % 2) + 64)
                    terms = [(mqn[:, h, q], mkn[:, h, 0:n]), (mqr[r, h // 2, q], kpe[r, 0:n])]
                elif kind == "mem":
                    terms = [(qm[:, h, q], km[:, h, 0:n])]
                else:
                    keys = {"cmp": kcmp, "slc": ksT, "win": kwT}[kind]
                    terms = [(qn[0:96, 2 * h + k, q], keys[0:96, k, 0:n]) for k in range(2)]
                for k, (lhsT, rhs) in enumerate(terms):
                    last = mm(out, lhsT, rhs, start=k == 0, stop=k == len(terms) - 1)
                last.then_inc(S("scores2_ready"), 1)

            def values2(u):
                kind, o, h = OUTS[u // 2]
                qt = u % 2
                n = keys_seen(kind, qt)
                pe.wait_ge(S("probs2_ready"), u + 1)
                if u:
                    pe.wait_ge(S("probs2_copied"), u)
                for k in range((n + P - 1) // P):
                    w = min(P, n - k * P)
                    last = transposed(bank(6, k * P, P)[0:w, :], prob[:, u % 2, k * P:k * P + w])
                last.then_inc(S("probs2_transposed"), 1)
                if qt == 0:
                    return
                pe.wait_ge(S("probs2_copied"), u + 1)
                if u > 1:
                    pe.wait_ge(S("out2_copied"), u // 2)
                a = aT[(u // 2) % 2]
                if kind == "cmp":
                    terms = [(vcmp[0:NCMP, :], a[0:NCMP, 0, :], 0)]
                elif kind == "mem":
                    terms = [(vm[:, k, h * P:(h + 1) * P], a[:, k, :], 0) for k in range(2)]
                else:
                    v = [mv[:, k, h * P:(h + 1) * P] if kind == "mla" else (vs if kind == "slc" else vw)[:, k, :]
                         for k in range(2)]
                    terms = [(v[0], a[:, 0, :], 0), (v[1], a[:, 1, P:T], P)]
                for k, (lhsT, rhs, c) in enumerate(terms):
                    last = mm(bank(7, c, T - c), lhsT, rhs, start=k == 0, stop=k == len(terms) - 1,
                              skip_group_check=True)
                last.then_inc(S("out2_ready"), 1)

            for u in range(2 * len(OUTS)):
                scores2(u)
                if u:
                    values2(u - 1)
            values2(2 * len(OUTS) - 1)
            for n in range(12):
                if n == 0:
                    pe.wait_ge(S("nsa_gates_ready"), 1)
                    pe.wait_ge(S("out2_copied"), len(OUTS))
                if n >= 2:
                    pe.wait_ge(S("nsa_gated"), n - 1)
                mm(bank(4 + n % 2, 0, T), C("ident", 12)[:, n:n + 1].to_broadcast([12, P]), gn[0:12, :],
                   start=True, stop=True).then_inc(S("nsa_gate_rows"), 1)
            pe.wait_ge(S("mixed2"), 1)
            with pe.Fori(0, st.iters("out2")) as i:
                for job in range(2):
                    gemm("out2", i, job, features(job, zT))
            pe.wait_ge(S("x3_squared"), 1)
            sums(bank(4, 0, T), C("ones"), hC, KD).then_inc(S("x3_summed"), 1)
            pe.wait_ge(S("x3_normed"), 1)
            for n in range(8):
                t, g = n // 4, n % 4
                if n >= 2:
                    pe.wait_ge(S("out_copied"), n - 1)
                for k in range(4):
                    last = transposed(bank(6 + n % 2, k * P, P), hL[:, 4 * g + k, t * P:(t + 1) * P])
                last.then_inc(S("out_transposed"), 1)

        @block.scalar
        def _(act):
            A = nc.scalar.activation
            roots = 0

            def copy(out, in_, scale=1.0):
                return A(out, in_, ACT.Copy, scale=scale)

            def job_done(name, i, job):
                act.wait_ge(S("chunks_multiplied"), st.done(name, i, job))

            def rsqrt(v):
                nonlocal roots
                roots += 1
                act.wait_ge(S("variance_ready"), roots)
                A(v, v, ACT.Ln)
                act.drain()
                A(v, v, ACT.Exp, scale=-0.5).then_inc(S("rsqrt_done"), 1)

            def ada_copy_rows(name, i, job, rows):
                s = job % 2
                job_done(name, i, job)
                copy(rows[:, s, :], bank(2 * s)).then_inc(S("ada_rows_copied"), 1)

            def ada_keep(s, n, tile):
                act.wait_ge(S("ada_folded"), n)
                copy(ada[:, tile, :], bank(2 * s + 1, 0, 8).rearrange("p (a b) -> p a b", a=4)
                     ).then_inc(S(f"set_read{s}"), 1)

            def ada_late(n):
                if n < ADA_LATE:
                    ada_copy_rows("ada_late", 0, n, shared)
                if n:
                    ada_keep((n - 1) % 2, 8 + n, slice(28 + 4 * n, 32 + 4 * n))

            act.wait_ge(S("vectors_copied"), 1)
            A(ctmp[:, :], V("c", 0, 32), ACT.Exp, scale=-1.0).then_inc(S("c_exp"), 1)
            for n in range(16):
                t, g = n // 4, n % 4
                act.wait_ge(S("x_in_psum"), n + 1)
                dst = xT0 if t < 2 else cT0
                copy(dst[:, 4 * g:4 * g + 4, (t % 2) * P:(t % 2 + 1) * P],
                     bank(4 + n % 2).rearrange("p (a b) -> p a b", a=4)).then_inc(S("x_transposed"), 1)
            act.drain()
            A(hL[:, :, :], xT0, ACT.Square).then_inc(S("x_squared"), 1)
            A(hC[:, :, :], cT0, ACT.Square).then_inc(S("x_squared"), 1)
            rsqrt(rstd[:, 0, 0:T])
            rsqrt(rstd[:, 1, 0:T])
            with act.Fori(0, st.iters("ada_early")) as i:
                for job in range(2):
                    ada_copy_rows("ada_early", i, job, rows_early)
                for job in range(2):
                    ada_keep(job, i * 2 + (job + 1), bass.ds(i * 8 + 4 * job, 4))
            act.wait_ge(S("h_scaled"), 2)
            act.wait_ge(S("amod_ready"), 1)
            for n, h in enumerate((hL, hC)):
                for k in range(KD):
                    last = A(h[:, k, :], h[:, k, :], ACT.Identity, bias=ada[:, k, n:n + 1],
                             scale=amod[:, n, k:k + 1])
                last.then_inc(S("h_ready"), 1)

            def feature_tiles(dst, s, scale=1.0, n=4, m=P):
                return copy(dst, set_of(s)[0:m, 0:n * T].rearrange("p (a b) -> p a b", a=n), scale)

            act.wait_ge(S("x_spilled"), 16)
            job_done("gla_in", 0, 0)
            for s in range(2):
                feature_tiles(gk[:, :, s, :], s).then_inc(S(f"set_read{s}"), 1)
            for job in (1, 2):
                job_done("gla_in", 0, job)
                for s in range(2):
                    copy(gv[:, 2 * s:2 * s + 2, (job - 1) * 512:job * 512],
                         set_of(s).rearrange("p (a b) -> p a b", a=2)).then_inc(S(f"set_read{s}"), 1)
            job_done("gla_in", 0, 3)
            for s in range(2):
                copy(ga[:, s * T:(s + 1) * T], set_of(s)[0:32, 0:T]).then_inc(S(f"set_read{s}"), 1)
            job_done("gla_in", 0, 4)
            feature_tiles(gq, 0, 0.125).then_inc(S("set_read0"), 1)
            for d in range(2):
                if d:
                    act.wait_ge(S("gates_summed"), 1)
                for p in range(4):
                    n = 4 * d + p
                    act.wait_ge(S("z_ready"), n + 1)
                    A(zb[:, p, :], bank(4 + n % 4), ACT.Identity, bias=V(("b_a_f", "b_a_b")[d], p)
                      ).then_inc(S("z_read"), 1)
                act.drain()
                A(ztmp, area(KC, 2048), ACT.Abs)
                act.drain()
                A(ztmp, ztmp, ACT.Exp, scale=-1.0)
                act.drain()
                A(ztmp, ztmp, ACT.Ln, bias=1.0).then_inc(S("z_log"), 1)
            for job in range(2):
                job_done("dk_in", 0, job)
                for s in range(2):
                    feature_tiles(dk[:, 4 * job:4 * job + 4, s, :], s).then_inc(S(f"set_read{s}"), 1)

            def ctx_decay(n):
                p, d = n // 2, n % 2
                if n >= 2:
                    act.wait_ge(S("ctx_keys_transposed"), n - 1)
                if d == 0:
                    A(kst[:, 0, 0, :], bufs[0][:, p, 1, 1:257], ACT.Exp, scale=-1 / TAU,
                      bias=refs[:, 0, 2 * p + 1, 16:17]).then_inc(S("ctx_decay"), 1)
                else:
                    A(kst[:, 1, 0, :], bufs[1][:, p, 1, 0:256], ACT.Exp, scale=1 / TAU).then_inc(S("ctx_decay"), 1)

            act.wait_ge(S("refs_ready"), 2)
            ctx_decay(0)
            for n in range(8):
                if n < 7:
                    ctx_decay(n + 1)
                act.wait_ge(S("ctx_keys_transposed"), n + 1)
                if n >= 2:
                    act.wait_ge(S("states_ready"), n - 1)
                copy(kst[:, n % 2, 1, :], bank(6, 0, T)).then_inc(S("ctx_keys_copied"), 1)
            for job in range(2):
                job_done("dv_in", 0, job)
                for s in range(2):
                    copy(dv[:, 2 * s:2 * s + 2, job * 512:(job + 1) * 512],
                         set_of(s).rearrange("p (a b) -> p a b", a=2)).then_inc(S(f"set_read{s}"), 1)

            def dq_tiles(job):
                s = job % 2
                job_done("dq_in", 0, job)
                dst = (dq, gr)[job // 2]
                feature_tiles(dst[:, 4 * s:4 * s + 4, :], s).then_inc(S(f"set_read{s}"), 1)

            def gla_prepare(p, beside):
                if p == 0:
                    act.wait_ge(S("states_ready"), 8)
                    act.wait_ge(S("kc_cleared"), 1)
                else:
                    act.wait_ge(S("gla_out_ready"), p)
                A(qx[:, 0, :], bufs[0][:, p, 0, 1:257], ACT.Exp, scale=1 / TAU)
                A(qx[:, 1, :], bufs[1][:, p, 0, 0:256], ACT.Exp, scale=-1 / TAU, bias=small[:, 8 + p:9 + p])
                act.wait_ge(S("q_gaps"), p + 1)
                A(qx[:, 2:4, :], qx[:, 2:4, :], ACT.Exp, scale=1 / TAU).then_inc(S("q_decay"), 1)
                for d in range(2):
                    for b in BLOCKS[d]:
                        keys, tok = kc(d, b)
                        lo, hi = key_range(d, b)
                        if d == 0:
                            src, sc, ref = bufs[0][:, p, 0, 1 + lo:1 + hi], -1 / TAU, refs[:, 0, 2 * p, b:b + 1]
                        else:
                            src, sc, ref = bufs[1][:, p, 0, lo:hi], 1 / TAU, refs[:, 1, 2 * p, b + 1:b + 2]
                        A(keys[:, lo - tok:hi - tok], src, ACT.Exp, scale=sc, bias=ref).then_inc(S("k_decay"), 1)
                        if b == 7:
                            beside(d)
                for e in range(4):
                    act.wait_ge(S("pair_gaps"), 4 * p + e + 1)
                    A(pd[e % 2], pd[e % 2], ACT.Exp, scale=1 / TAU).then_inc(S("pair_decay"), 1)
                    if e:
                        beside(1 + e)
                beside(5)

            def gla_finish(p):
                act.wait_ge(S("gla_out_ready"), p + 1)
                A(rstd[:, 1, :].rearrange("p (a b) -> p a b", a=2), two_banks(T), ACT.Square
                  ).then_inc(S("gla_squared"), 1)
                rsqrt(rstd[:, 0, :])

            for pair in range(4):
                def beside(n, pair=pair):
                    if pair >= 2:
                        ada_late(6 * (pair - 2) + n)
                    elif n in (3, 5):
                        dq_tiles(2 * pair + n // 4)
                gla_prepare(pair, beside)
                gla_finish(pair)
            A(ztmp, area(7168, 2048), ACT.Exp, scale=-1.0).then_inc(S("r_exp"), 1)

            for g in range(12):
                src = dq[:, 2 * g:2 * g + 2, :] if g < 4 else dk[:, g - 4, :, :]
                if g % 3 == 0:
                    ada_late(12 + g // 3)
                if g >= 2:
                    act.wait_ge(S("qk_summed"), g - 1)
                A(dsq[:, g % 2, :].rearrange("p (a b) -> p a b", a=2), src, ACT.Square).then_inc(S("qk_squared"), 1)
                rsqrt(rstd[:, g % 2, :])
            ada_late(ADA_LATE)
            act.wait_ge(S("lambda_summed"), 1)
            A(small[:, 2:4].unsqueeze(2), two_banks(1), ACT.Exp).then_inc(S("lambda_exps"), 1)

            def diff_exp(n):
                act.wait_ge(S("diff_max_ready"), n + 1)
                if n >= 4:
                    act.wait_ge(S("diff_probs_transposed"), (n - 4) // 2 + 1)
                A(dp[:, n % 4, :], bank(4 + n % 2), ACT.Exp, scale=0.125, bias=small[:, 20 + n % 4:21 + n % 4],
                  accum_out=small[:, 24 + n % 4:25 + n % 4]).then_inc(S("diff_exps"), 1)

            def diff_copy(u):
                h, qt = u // 2, u % 2
                act.wait_ge(S("diff_probs_transposed"), u + 1)
                if h >= 2 and qt == 0:
                    act.wait_ge(S("diff_pv_done"), h - 1)
                copy(daT[h % 2][:, :, qt * P:(qt + 1) * P], bank(6).rearrange("p (a b) -> p a b", a=4)
                     ).then_inc(S("diff_probs_copied"), 1)
                if qt == 1:
                    act.wait_ge(S("diff_pv_done"), h + 1)
                    copy(dq[:, h, :], bank(7, 0, T)).then_inc(S("diff_out_copied"), 1)

            for u in range(16):
                diff_exp(2 * u)
                diff_exp(2 * u + 1)
                if u:
                    diff_copy(u - 1)
            diff_copy(15)
            act.drain()
            for g in range(4):
                if g >= 2:
                    act.wait_ge(S("diff_summed"), g - 1)
                A(dsq[:, g % 2, :].rearrange("p (a b) -> p a b", a=2), dq[:, 2 * g:2 * g + 2, :], ACT.Square
                  ).then_inc(S("diff_squared"), 1)
                rsqrt(rstd[:, g % 2, :])

            with act.Fori(0, st.iters("merge")) as i:
                act.wait_ge(S("merged"), i + 1)
                for b in range(2):
                    job_done("merge", i, 2 * b)
                    for m in range(4):
                        f = i * 4 + (16 * b + m)
                        last = A(gsb[b][:, m, :], set_of(0)[:, m * T:(m + 1) * T], ACT.Exp, scale=-1.0,
                                 bias=nbgate[:, bass.ds(f, 1)])
                    last.then_inc(S("gate_exps"), 1)
            for s in range(2):
                act.wait_ge(S(f"set_read{s}"), st.set_uses("up", 0, s, s))
            A(hC[:, :, :], x1, ACT.Square).then_inc(S("x1_squared"), 1)
            rsqrt(rstd[:, 0, 0:T])
            act.wait_ge(S("h2_scaled"), 1)
            for k in range(KD):
                last = A(hL[:, k, :], hL[:, k, :], ACT.Identity, bias=ada[:, 48 + k, 0:1], scale=amod[:, 2, k:k + 1])
            last.then_inc(S("h2_ready"), 1)

            with act.Fori(0, st.iters("up")) as i:
                act.wait_ge(S("ffn_hidden"), i + 1)
                for s in range(2):
                    job_done("up", i, s)
                    for m in range(4):
                        f = i * 4 + (KF * s + m)
                        last = A(ftap[s][:, m, :], set_of(s)[:, m * T:(m + 1) * T], ACT.Identity,
                                 bias=vec[:, bass.ds(f + VROW["conv_b"], 1)],
                                 scale=vec[:, bass.ds(f + (VROW["conv_w"] + 2 * KF), 1)])
                    last.then_inc(S("taps_centred"), 1)
                act.wait_ge(S("set_read0"), st.set_uses("up", i, 1, 0))
                A(fexp, ftap[0], ACT.Exp, scale=-1.0).then_inc(S("ffn_exps"), 1)

            for n in range(8):
                t, g = n // 4, n % 4
                act.wait_ge(S("mem_in_psum"), n + 1)
                copy(hC[:, 4 * g:4 * g + 4, t * P:(t + 1) * P],
                     bank(4 + n % 2).rearrange("p (a b) -> p a b", a=4)).then_inc(S("mem_transposed"), 1)
            act.drain()
            A(sq2, hC[:, :, :], ACT.Square).then_inc(S("mem_squared"), 1)
            for s in range(2):
                act.wait_ge(S(f"set_read{s}"), st.set_uses("mem", 0, s, s))
            A(hL[:, :, :], x1, ACT.Square).then_inc(S("x2_squared"), 1)
            rsqrt(rstd[:, 0, 0:T])
            rsqrt(rstd[:, 1, 0:T])
            job_done("mem", 0, 1)
            feature_tiles(km, 0, ).then_inc(S("set_read0"), 1)
            copy(vm, set_of(1).rearrange("p (a b) -> p a b", a=2)).then_inc(S("set_read1"), 1)
            where = {"z0": zT[:, 0:4, :], "z1": zT[:, 4:8, :], "z2": zT[:, 8:12, :], "z3": zT[:, 12:16, :]}
            for n, (name, _, _) in enumerate(IN2):
                s = n % 2
                job_done("in2", 0, n)
                if name in ("cq", "ckv"):
                    A(rtmpsq[s], set_of(s).rearrange("p (a b) -> p a b", a=4), ACT.Square
                      ).then_inc(S("lowrank_squared"), 1)
                    last = feature_tiles((cq, ckv)[s], s)
                elif name == "krope":
                    last = copy(kpe, set_of(s)[:, 0:T])
                elif name in ("qn0", "qn1"):
                    last = feature_tiles(qn[0:96, 4 * (name == "qn1"):4 * (name == "qn1") + 4, :], s, NSA_SCALE, 4, 96)
                elif name in ("kc", "ks", "kw"):
                    last = feature_tiles({"kc": kcT, "ks": ksT, "kw": kwT}[name][0:96, :, :], s, 1.0, 2, 96)
                elif name == "vc":
                    last = copy(vcT, set_of(s)[:, 0:T])
                elif name in ("vs", "vw"):
                    last = copy({"vs": vs, "vw": vw}[name],
                                set_of(s).rearrange("p (a b) -> p a b", a=2)[:, :, 0:P])
                elif name == "gn":
                    A(gn[0:12, :], set_of(s)[0:12, 0:T], ACT.Exp, scale=-1.0).then_inc(S(f"set_read{s}"), 1)
                    continue
                elif name == "qm":
                    last = feature_tiles(qm, s, MEM_SCALE)
                else:
                    last = feature_tiles(where[name], s)
                last.then_inc(S(f"set_read{s}"), 1)
                if name == "ckv":
                    rsqrt(rstd[:, 0, 0:T])
                    rsqrt(rstd[:, 1, 0:T])
            for n in range(4):
                s = n % 2
                job_done("uq", 0, n)
                copy(mqn[:, 2 * n:2 * n + 2, :], set_of(s)[:, 0:2 * T].rearrange("p (a b) -> p a b", a=2), MLA_SCALE)
                copy(mqr[:, n, :], set_of(s)[:, 2 * T:3 * T], MLA_SCALE).then_inc(S(f"set_read{s}"), 1)
            for n in range(4):
                s = n % 2
                job_done("ukv", 0, n)
                copy(mkn[:, 2 * n:2 * n + 2, :], set_of(s)[:, 0:2 * T].rearrange("p (a b) -> p a b", a=2))
                copy(mv[:, :, 256 * n:256 * (n + 1)], set_of(s)[:, 2 * T:4 * T].rearrange("p (a b) -> p a b", a=2)
                     ).then_inc(S(f"set_read{s}"), 1)
            act.wait_ge(S("cmp_bounded"), 1)
            hk = hexp[0:96, 0:32].rearrange("p (a b) -> p a b", a=2)[:, :, 0:NCMP]
            A(hk, hk, ACT.Exp, scale=-1.0)
            A(hexp[:, 32:32 + NCMP], hexp[:, 32:32 + NCMP], ACT.Exp, scale=-1.0).then_inc(S("cmp_exps"), 1)

            def exp2(u):
                kind, o, h = OUTS[u // 2]
                n = keys_seen(kind, u % 2)
                act.wait_ge(S("max2_ready"), u + 1)
                if u >= 2:
                    act.wait_ge(S("probs2_transposed"), u - 1)
                src = bank(4 + u % 2, 0, n) if kind == "mem" else ssb[:, u % 2, 0:n]
                A(prob[:, u % 2, 0:n], src, ACT.Exp, bias=small[:, 36 + u % 2:37 + u % 2],
                  accum_out=small[:, 40 + u % 2:41 + u % 2]).then_inc(S("exps2"), 1)

            def copy2(u):
                kind, o, h = OUTS[u // 2]
                qt = u % 2
                n = keys_seen(kind, qt)
                act.wait_ge(S("probs2_transposed"), u + 1)
                if qt == 0 and u >= 4:
                    act.wait_ge(S("out2_ready"), u // 2 - 1)
                k, w = (n + P - 1) // P, min(n, P)
                copy(aT[(u // 2) % 2][0:w, 0:k, qt * P:(qt + 1) * P],
                     bank(6, 0, k * P)[0:w, :].rearrange("p (a b) -> p a b", a=k)).then_inc(S("probs2_copied"), 1)
                if qt == 1:
                    act.wait_ge(S("out2_ready"), u // 2 + 1)
                    copy(obuf[:, u // 2, :], bank(7, 0, T)).then_inc(S("out2_copied"), 1)

            for u in range(2 * len(OUTS)):
                exp2(u)
                if u:
                    copy2(u - 1)
            copy2(2 * len(OUTS) - 1)
            A(area(12032, 4096), area(2304, 4096), ACT.Exp, scale=-1.0).then_inc(S("z_exps"), 1)
            for s in range(2):
                act.wait_ge(S(f"set_read{s}"), st.set_uses("out2", 2, 0, 0) if s == 0 else st.set_uses("out2", 2, 0, 1))
            A(hC[:, :, :], x1, ACT.Square).then_inc(S("x3_squared"), 1)
            rsqrt(rstd[:, 0, 0:T])
            for n in range(8):
                t, g = n // 4, n % 4
                act.wait_ge(S("out_transposed"), n + 1)
                copy(onat[:, t, 512 * g:512 * (g + 1)], bank(6 + n % 2)).then_inc(S("out_copied"), 1)

        @block.vector
        def _(dve):
            v = nc.vector
            tt, ts, stt = v.tensor_tensor, v.tensor_scalar, v.scalar_tensor_tensor
            roots = 0

            def variance(out, sums, n):
                ts(out, sums, 1.0 / n, EPS, ALU.mult, ALU.add).then_inc(S("variance_ready"), 1)

            def rsqrt_wait():
                nonlocal roots
                roots += 1
                dve.wait_ge(S("rsqrt_done"), roots)

            def plus_one_over(x):
                ts(x, x, 1.0, None, ALU.add)
                dve.drain()
                v.reciprocal(x, x)
                dve.drain()

            for name in ("merged", "ffn_hidden"):
                dve.sem_inc(S(name), 1)
            def modulation_bias(a, b):
                tt(ada[:, a:b, :], ada[:, a:b, :], V("b_ada", a, b - a).unsqueeze(2).to_broadcast([P, b - a, 2]), ALU.add)
                dve.drain()

            dve.wait_ge(S("vectors_transposed"), 1)
            v.tensor_copy(vec[:, 0:512], bank(6))
            v.tensor_copy(vec[:, 512:NVEC], bank(7, 0, NVEC - 512)).then_inc(S("vectors_copied"), 1)
            dve.drain()
            ts(nbgate[:, :], V("b_gate", 0, 32), -1.0, None, ALU.mult)
            ts(small[:, 5:6], V("diff_onorm_w"), 1.0 - LAM_INIT, None, ALU.mult)
            tt(small[:, 0:1], V("lambda_q1"), V("lambda_k1"), ALU.mult).then_inc(S("lambda_products"), 1)
            dve.wait_ge(S("c_exp"), 1)
            plus_one_over(ctmp[:, :])
            dve.wait_ge(S("csil_cleared"), 1)
            tt(csil[:, :, 0:2].rearrange("p k w -> p w k"), V("c", 0, 32).rearrange("p (w k) -> p w k", w=2),
               ctmp[:, :].rearrange("p (w k) -> p w k", w=2), ALU.mult).then_inc(S("c_activated"), 1)
            for n in range(2):
                dve.wait_ge(S("x_summed"), n + 1)
                variance(rstd[:, n, 0:T], bank(6 + n, 0, T), D)
            for n, (h, x) in enumerate(((hL, xT0), (hC, cT0))):
                rsqrt_wait()
                tt(h[:, :, :], x, rstd[:, n, 0:T].unsqueeze(1).to_broadcast([P, KD, T]), ALU.mult
                   ).then_inc(S("h_scaled"), 1)
            for s in range(2):
                dve.wait_ge(S(f"set_read{s}"), st.set_uses("gla_in", 0, 0, s))
            modulation_bias(0, 32)
            for n in range(2):
                last = stt(amod[:, n, :], ada[:, 16:32, n], 1.0, V("norm1_w", 0, 16), ALU.add, ALU.mult)
            last.then_inc(S("amod_ready"), 1)

            for d in range(2):
                dve.wait_ge(S("z_read"), 4 * (d + 1))
                v.memset(bufs[d][:, :, :, 0:1], 0.0)
                dve.wait_ge(S("z_log"), d + 1)
                stt(area(KC, 2048), area(KC, 2048), 0.0, ztmp, ALU.min, ALU.subtract)
                dve.drain()
                for p in range(4):
                    for half in range(2):
                        last = v.tensor_tensor_scan(bufs[d][:, p, half, 1:257], C("ones")[:, 0:1].to_broadcast([P, T]),
                                                    zb[:, p, half * T:(half + 1) * T], 0.0, ALU.mult, ALU.add)
                last.then_inc(S("gates_summed"), 1)
                dve.drain()
                if d:
                    ts(small[:, 8:12], bufs[1][:, :, 0, 256], 1 / TAU, None, ALU.mult)
                ts(refs[:, d, :, :], bufs[d].rearrange("p a b c -> p (a b) c")[:, :, 0:257:16], (1 - 2 * d) / TAU, None,
                   ALU.mult).then_inc(S("refs_ready"), 1)

            def scale_ctx_keys(n):
                dve.wait_ge(S("ctx_decay"), n + 1)
                tt(kst[:, n % 2, 0, :], kst[:, n % 2, 0, :], gk[:, n // 2, 1, :], ALU.mult
                   ).then_inc(S("ctx_keys_scaled"), 1)

            scale_ctx_keys(0)
            for n in range(8):
                if n < 7:
                    scale_ctx_keys(n + 1)
                dve.wait_ge(S("states_ready"), n + 1)
                v.tensor_copy(smem[:, n, :], bank(7, 0, P)).then_inc(S("states_copied"), 1)

            def blocks(flat):
                return flat.rearrange("p (b i) -> p b i", i=GC)

            def gla_prepare(p):
                if p == 0:
                    dve.wait_ge(S("states_ready"), 8)
                else:
                    dve.wait_ge(S("gla_out_ready"), p)
                f, b = bufs[0][:, p, 0, :], bufs[1][:, p, 0, :]
                tt(blocks(qx[:, 2, :]), blocks(f[:, 1:257]),
                   f[:, 0:256:GC].unsqueeze(2).to_broadcast([P, NB, GC]), ALU.subtract)
                tt(blocks(qx[:, 3, :]), b[:, GC:257:GC].unsqueeze(2).to_broadcast([P, NB, GC]),
                   blocks(b[:, 0:256]), ALU.subtract).then_inc(S("q_gaps"), 1)
                dve.wait_ge(S("q_decay"), p + 1)
                tt(qx, qx, gq[:, p, :].unsqueeze(1).to_broadcast([P, 4, T]), ALU.mult)
                n = 0
                for d in range(2):
                    for blk in BLOCKS[d]:
                        keys, tok = kc(d, blk)
                        lo, hi = key_range(d, blk)
                        n += 1
                        dve.wait_ge(S("k_decay"), 30 * p + n)
                        last = tt(keys[:, lo - tok:hi - tok], keys[:, lo - tok:hi - tok], gk[:, p, 0, lo:hi], ALU.mult)
                last.then_inc(S("gla_operands_ready"), 1)
                if p == 0:
                    dve.wait_ge(S("chunks_multiplied"), st.done("dv_in", 0, 1))

                def gaps(e):
                    d, t = e // 2, e % 2
                    if 4 * p + e >= 2:
                        dve.wait_ge(S("gla_diag_summed"), 4 * p + e - 1)
                    src = f[:, 1 + t * P:1 + (t + 1) * P] if d == 0 else b[:, t * P:(t + 1) * P]
                    i = src.rearrange("p (b i) -> p i b", i=GC).unsqueeze(3).to_broadcast([P, GC, 8, GC])
                    j = blocks(src).unsqueeze(1).to_broadcast([P, GC, 8, GC])
                    tt(pd[e % 2], i if d == 0 else j, j if d == 0 else i, ALU.subtract)
                    dve.drain()
                    flat = carea(2048 * (e % 2), 2048)
                    ts(flat, flat, 0.0, None, ALU.min).then_inc(S("pair_gaps"), 1)

                def pairs(e):
                    t = e % 2
                    dve.wait_ge(S("pair_decay"), 4 * p + e + 1)
                    k = blocks(gk[:, p, 0, t * P:(t + 1) * P]).unsqueeze(1).to_broadcast([P, GC, 8, GC])
                    q = gq[:, p, t * P:(t + 1) * P].rearrange("p (b i) -> p i b", i=GC).unsqueeze(3
                                                             ).to_broadcast([P, GC, 8, GC])
                    tt(pd[e % 2], pd[e % 2], k, ALU.mult)
                    dve.drain()
                    tt(pd[e % 2], pd[e % 2], q, ALU.mult).then_inc(S("gla_diag_ready"), 1)

                gaps(0)
                gaps(1)
                for e in range(4):
                    pairs(e)
                    if e < 2:
                        gaps(e + 2)

            def gla_finish(p):
                dve.wait_ge(S("gla_blocks_done"), p + 1)
                dve.wait_ge(S("gla_diag_summed"), 4 * p + 4)
                if p:
                    dve.wait_ge(S("gla_out_ready"), p)
                for h in range(2):
                    parts = []
                    for d, mask in enumerate(("mask_f", "mask_b")):
                        diag = bank(6, 64 * d, 64).rearrange("p (t i h) -> p t i h", t=2, i=GC)[:, :, :, h]
                        part = rstd[:, 1, d * T:(d + 1) * T].rearrange("p (t b i) -> p t b i", t=2, b=8)
                        tt(part, diag.unsqueeze(2).to_broadcast([P, 2, 8, GC]),
                           C(mask).rearrange("p (t b i) -> p t b i", t=2, b=8), ALU.mult)
                        parts.append(rstd[:, 1, d * T:(d + 1) * T])
                    v.tensor_copy(asum[:, h, :], bank(4 + h))
                    dve.drain()
                    quads = asum[:, h, :].rearrange("p (a b) -> p a b", a=4)[:, 0:4:3, :]
                    for d in range(2):
                        last = tt(quads, quads, parts[d].rearrange("p (a b) -> p a b", a=2), ALU.add)
                        if d == 0:
                            dve.drain()
                    last.then_inc(S("gla_scores_ready"), 1)
                    dve.drain()
                dve.wait_ge(S("gla_summed"), p + 1)
                variance(rstd[:, 0, :], bank(4), P)
                rsqrt_wait()
                stt(yg[:, 2 * p:2 * p + 2, :], two_banks(T), V("gla_onorm_w"),
                    rstd[:, 0, :].rearrange("p (a b) -> p a b", a=2), ALU.mult, ALU.mult).then_inc(S("gla_normed"), 1)

            for p in range(4):
                gla_prepare(p)
                gla_finish(p)
            dve.wait_ge(S("r_exp"), 1)
            plus_one_over(ztmp)
            grf, ygf = area(7168, 2048), area(1024, 2048)
            tt(grf, grf, ztmp, ALU.mult)
            dve.drain()
            tt(ygf, ygf, grf, ALU.mult).then_inc(S("gla_gated"), 1)

            for g in range(12):
                n = 512 if g < 4 else T
                src = (dq[:, 2 * g:2 * g + 2, :] if g < 4 else dk[:, g - 4, :, :]).rearrange("p a b -> p (a b)")
                rs = rstd[:, g % 2, :]
                dve.wait_ge(S("qk_summed"), g + 1)
                variance(rs, bank(4 + g % 2), 64)
                rsqrt_wait()
                stt(src, src, V("diff_qnorm_w" if g < 4 else "diff_knorm_w"), rs, ALU.mult, ALU.mult
                    ).then_inc(S("qk_normed"), 1)
                dve.drain()
                a = n // T

                def reps(flat):
                    return flat.rearrange("p (a b) -> p a b", a=a)

                def table(name):
                    return C(name).unsqueeze(1).to_broadcast([P, a, T])

                tt(reps(dmul[:, g % 2, 0:n]), reps(src[:, 0:n]), table("cos2d"), ALU.mult)
                dve.wait_ge(S("qk_rotated"), g + 1)
                tt(reps(rs[:, 0:n]), reps(bank(6 + g % 2, 0, n)), table("sin2d"), ALU.mult)
                dve.drain()
                tt(src[:, 0:n], dmul[:, g % 2, 0:n], rs[:, 0:n], ALU.add).then_inc(S("qk_done"), 1)
            dve.wait_ge(S("lambda_exps"), 1)
            tt(small[:, 4:5], small[:, 3:4], small[:, 2:3], ALU.subtract)
            dve.drain()
            ts(small[:, 4:5], small[:, 4:5], -LAM_INIT, None, ALU.add).then_inc(S("lambda_done"), 1)
            dve.drain()

            def diff_max(n):
                dve.wait_ge(S("diff_scores_ready"), n + 1)
                if n >= 4:
                    dve.wait_ge(S("diff_exps"), n - 3)
                v.reduce_max(small[:, 16 + n % 4:17 + n % 4], bank(4 + n % 2), AXX)
                dve.drain()
                ts(small[:, 20 + n % 4:21 + n % 4], small[:, 16 + n % 4:17 + n % 4], -0.125, None, ALU.mult
                   ).then_inc(S("diff_max_ready"), 1)

            def diff_combine(u):
                a = 2 * (u % 2)
                dve.wait_ge(S("diff_exps"), 2 * u + 2)
                v.reciprocal(small[:, 28 + a:30 + a], small[:, 24 + a:26 + a])
                dve.drain()
                tt(small[:, 29 + a:30 + a], small[:, 29 + a:30 + a], small[:, 4:5], ALU.mult)
                ts(dp[:, a, :], dp[:, a, :], small[:, 28 + a:29 + a], None, ALU.mult)
                dve.drain()
                stt(dp[:, a, :], dp[:, a + 1, :], small[:, 29 + a:30 + a], dp[:, a, :], ALU.mult, ALU.add
                    ).then_inc(S("diff_probs_ready"), 1)

            for u in range(16):
                diff_max(2 * u)
                diff_max(2 * u + 1)
                if u:
                    diff_combine(u - 1)
            diff_combine(15)
            for g in range(4):
                rs = rstd[:, g % 2, :]
                flat = dq[:, 2 * g:2 * g + 2, :].rearrange("p a b -> p (a b)")
                dve.wait_ge(S("diff_summed"), g + 1)
                variance(rs, bank(4 + g % 2), P)
                rsqrt_wait()
                stt(flat, flat, small[:, 5:6], rs, ALU.mult, ALU.mult).then_inc(S("diff_normed"), 1)

            with dve.Fori(0, st.iters("merge")) as i:
                for b in range(2):
                    dve.wait_ge(S("gate_exps"), i * 2 + (b + 1))
                    ts(gsb[b], gsb[b], 1.0, None, ALU.add).then_inc(S("set_read0"), 1)
                    dve.drain()
                    v.reciprocal(gsb[b], gsb[b])
                    dve.drain()
                    dve.wait_ge(S("chunks_multiplied"), st.done("merge", i, 2 * b + 1))
                    dst = mT[:, bass.ds(i * 4, 4), :]
                    proj = set_of(1).rearrange("p (a b) -> p a b", a=4)
                    if b == 0:
                        tt(dst, gsb[0], proj, ALU.mult).then_inc(S("set_read1"), 1)
                    else:
                        tt(gsb[1], gsb[1], proj, ALU.mult).then_inc(S("set_read1"), 1)
                        dve.drain()
                        tt(dst, dst, gsb[1], ALU.add).then_inc(S("merged"), 1)
            modulation_bias(32, 96)
            dve.wait_ge(S("x_back"), 16)
            with dve.Fori(0, st.iters("out")) as i:
                for job in range(2):
                    dve.wait_ge(S("chunks_multiplied"), st.done("out", i, job))
                    for m in range(4):
                        f = i * 8 + (4 * job + m)
                        last = stt(x1[:, bass.ds(f, 1), :].rearrange("p a b -> p (a b)"), set_of(job)[:, m * T:(m + 1) * T],
                                   ada[:, bass.ds(f + 32, 1), 0], x0[:, bass.ds(f, 1), :].rearrange("p a b -> p (a b)"),
                                   ALU.mult, ALU.add)
                    last.then_inc(S(f"set_read{job}"), 1)
            stt(amod[:, 2, :], ada[:, 64:80, 0], 1.0, V("norm2_w", 0, 16), ALU.add, ALU.mult)
            dve.wait_ge(S("x1_summed"), 1)
            variance(rstd[:, 0, 0:T], bank(4, 0, T), D)
            rsqrt_wait()
            tt(hL[:, :, :], x1, rstd[:, 0, 0:T].unsqueeze(1).to_broadcast([P, KD, T]), ALU.mult
               ).then_inc(S("h2_scaled"), 1)

            with dve.Fori(0, st.iters("up")) as i:
                for s in range(2):
                    dve.wait_ge(S("taps_centred"), i * 2 + (s + 1))
                    for tap in (0, 2):
                        for m in range(4):
                            f = i * 4 + (KF * s + m)
                            w = vec[:, bass.ds(f + (VROW["conv_w"] + 2 * KF * tap), 1)]
                            u = set_of(s)[:, m * T:(m + 1) * T]
                            y = ftap[s][:, m, :]
                            if tap == 0:
                                last = stt(y[:, 1:T], u[:, 0:T - 1], w, y[:, 1:T], ALU.mult, ALU.add)
                            else:
                                last = stt(y[:, 0:T - 1], u[:, 1:T], w, y[:, 0:T - 1], ALU.mult, ALU.add)
                        if tap == 0:
                            dve.drain()
                    last.then_inc(S(f"set_read{s}"), 1)
                dve.wait_ge(S("ffn_exps"), i + 1)
                plus_one_over(fexp)
                tt(ftap[0], ftap[0], fexp, ALU.mult)
                dve.drain()
                tt(fh[:, bass.ds(i * 4, 4), :], ftap[0], ftap[1], ALU.mult).then_inc(S("ffn_hidden"), 1)
            with dve.Fori(0, st.iters("down")) as i:
                for job in range(2):
                    dve.wait_ge(S("chunks_multiplied"), st.done("down", i, job))
                    for m in range(4):
                        f = i * 8 + (4 * job + m)
                        x = x1[:, bass.ds(f, 1), :].rearrange("p a b -> p (a b)")
                        last = stt(x, set_of(job)[:, m * T:(m + 1) * T], ada[:, bass.ds(f + 80, 1), 0], x,
                                   ALU.mult, ALU.add)
                    last.then_inc(S(f"set_read{job}"), 1)

            def gained(out, x, gain, rs, tiles):
                for k in range(tiles):
                    last = stt(out[:, k, :], x[:, k, :], V(gain, k), rs, ALU.mult, ALU.mult)
                return last

            dve.wait_ge(S("mem_summed"), 1)
            variance(rstd[:, 0, 0:T], bank(6, 0, T), D)
            dve.wait_ge(S("x2_summed"), 1)
            variance(rstd[:, 1, 0:T], bank(7, 0, T), D)
            rsqrt_wait()
            gained(hC, hC, "mem_norm_g_2", rstd[:, 0, 0:T], KD).then_inc(S("mem_ready"), 1)
            rsqrt_wait()
            gained(hL, x1, "norm_g_2", rstd[:, 1, 0:T], KD).then_inc(S("h3_ready"), 1)
            dve.wait_ge(S("consts2_loaded"), 16)
            ts(causal, C("rel")[:, T:2 * T], -1e20, MASKED, ALU.is_lt, ALU.mult)
            for n in range(2):
                dve.wait_ge(S("lowrank_summed"), n + 1)
                variance(rstd[:, n, 0:T], bank(4 + n, 0, T), 512)
            for n, (x, gain, done) in enumerate(((cq, "q_norm_g_2", "cq_normed"), (ckv, "kv_norm_g_2", "ckv_normed"))):
                rsqrt_wait()
                dve.wait_ge(S(f"set_read{n}"), st.set_uses("in2", 0, 2 + n, n))
                gained(x, x, gain, rstd[:, n, 0:T], 4).then_inc(S(done), 1)
            gate_job = [n for n, (name, _, _) in enumerate(IN2) if name == "gn"][0]
            dve.wait_ge(S(f"set_read{gate_job % 2}"), st.set_uses("in2", 0, gate_job, gate_job % 2) + 1)
            ts(gn[0:12, :], gn[0:12, :], 1.0, None, ALU.add)
            dve.drain()
            v.reciprocal(gn[0:12, :], gn[0:12, :]).then_inc(S("nsa_gates_ready"), 1)
            for n in range(5):
                dve.wait_ge(S("rope_rotated"), n + 1)
                dst = mqr[:, n, :] if n < 4 else kpe
                tt(rtmp[:, n % 2, 0:T], dst, C("cos1d"), ALU.mult)
                tt(rtmp[:, n % 2, T:2 * T], bank(4 + n % 2, 0, T), C("sin1d"), ALU.mult)
                dve.drain()
                tt(dst, rtmp[:, n % 2, 0:T], rtmp[:, n % 2, T:2 * T], ALU.add).then_inc(S("rope_done"), 1)
            dve.wait_ge(S("pe_transposed"), 1)
            v.tensor_copy(peT[0:96, 0:2, :], bank(6, 0, 64)[0:96, :].rearrange("p (a b) -> p a b", a=2))
            v.tensor_copy(peT[:, 2, :], bank(6, 64, 32))
            dve.drain()
            for a in range(2):
                for h in range(3):
                    n = 96 if h < 2 else P
                    src = (kcT[0:96, h, :] if h < 2 else vcT).rearrange("p (n b) -> p b n", b=16)[:, :, a:a + NCMP]
                    dst = (kcp[0:96, h, :, :] if h < 2 else vcp)[:, 16 * a:16 * a + 16, :]
                    last = tt(dst, src, peT[0:n, h, 16 * a:16 * a + 16].unsqueeze(2).to_broadcast([n, 16, NCMP]),
                              ALU.add)
            last.then_inc(S("cmp_blocks_ready"), 1)

            def pair(flat):
                return flat.rearrange("p (a b) -> p a b", a=2)[:, :, 0:NCMP]

            dve.wait_ge(S("chunks_multiplied"), st.done("cmp", 0, 1))
            ts(pair(hexp[0:96, 0:32]), pair(set_of(0)[0:96, 0:32]), -87.0, None, ALU.max)
            ts(hexp[:, 32:32 + NCMP], set_of(1)[:, 0:NCMP], -87.0, None, ALU.max).then_inc(S("cmp_bounded"), 1)
            dve.wait_ge(S("cmp_exps"), 1)

            plus_one_over(pair(hexp[0:96, 0:32]))
            plus_one_over(hexp[:, 32:32 + NCMP])
            tt(hidk[0:96, :, 0:NCMP], pair(hexp[0:96, 0:32]), pair(set_of(0)[0:96, 0:32]), ALU.mult
               ).then_inc(S("set_read0"), 1)
            tt(hidv[:, 0:NCMP], hexp[:, 32:32 + NCMP], set_of(1)[:, 0:NCMP], ALU.mult).then_inc(S("set_read1"), 1)
            dve.wait_ge(S("cmp_projected"), 1)
            v.tensor_copy(kcmp[0:96, :, 0:NCMP], pair(bank(6, 0, 32)[0:96, :]))
            v.tensor_copy(vcmp[0:NCMP, :], bank(7, 0, P)[0:NCMP, :]).then_inc(S("cmp_done"), 1)

            def max2(u):
                kind, o, h = OUTS[u // 2]
                qt = u % 2
                n = keys_seen(kind, qt)
                scores = bank(4 + u % 2, 0, n)
                dve.wait_ge(S("scores2_ready"), u + 1)
                if u >= 2:
                    dve.wait_ge(S("exps2"), u - 1)
                if kind != "mem":
                    out = ssb[:, u % 2, 0:n]
                    if kind == "mla":
                        tt(out, scores, causal[:, T - n:T], ALU.add)
                    else:
                        rel = C("cmprel")[:, qt * 16:qt * 16 + n] if kind == "cmp" else C("rel")[:, qt * T:qt * T + n]
                        stt(out, rel, 2.0 ** (-2.0 * (h + 1)), scores, ALU.mult, ALU.add)
                    dve.drain()
                    scores = out
                v.reduce_max(small[:, 32 + u % 2:33 + u % 2], scores, AXX)
                dve.drain()
                ts(small[:, 36 + u % 2:37 + u % 2], small[:, 32 + u % 2:33 + u % 2], -1.0, None, ALU.mult
                   ).then_inc(S("max2_ready"), 1)

            def norm2(u):
                kind, o, h = OUTS[u // 2]
                qt = u % 2
                n = keys_seen(kind, qt)
                probs, total = prob[:, u % 2, 0:n], small[:, 40 + u % 2:41 + u % 2]
                dve.wait_ge(S("exps2"), u + 1)
                if kind == "cmp":
                    tt(probs, probs, C("cmpmask")[:, qt * 16:qt * 16 + n], ALU.mult)
                    dve.drain()
                    v.reduce_sum(total, probs, AXX)
                    dve.drain()
                    ts(total, total, 1e-20, None, ALU.add)
                    dve.drain()
                v.reciprocal(small[:, 44 + u % 2:45 + u % 2], total)
                dve.drain()
                ts(probs, probs, small[:, 44 + u % 2:45 + u % 2], None, ALU.mult).then_inc(S("probs2_ready"), 1)

            for u in range(2 * len(OUTS)):
                max2(u)
                if u:
                    norm2(u - 1)
            norm2(2 * len(OUTS) - 1)
            for n in range(12):
                dve.wait_ge(S("nsa_gate_rows"), n + 1)
                tt(obuf[:, 8 + n, :], obuf[:, 8 + n, :], bank(4 + n % 2, 0, T), ALU.mult).then_inc(S("nsa_gated"), 1)
            for k in (1, 2):
                dve.drain()
                tt(obuf[:, 8:20:3, :], obuf[:, 8:20:3, :], obuf[:, 8 + k:20:3, :], ALU.add)
            dve.wait_ge(S("z_exps"), 1)
            plus_one_over(area(12032, 4096))
            tt(area(2304, 4096), area(2304, 4096), area(12032, 4096), ALU.mult)
            dve.drain()
            tt(zT[:, 0:8, :], zT[:, 0:8, :], obuf[:, 0:8, :], ALU.mult)
            tt(zT[:, 8:12, :], zT[:, 8:12, :], obuf[:, 8:20:3, :], ALU.mult)
            tt(zT[:, 12:16, :], zT[:, 12:16, :], obuf[:, 20:24, :], ALU.mult).then_inc(S("mixed2"), 1)
            with dve.Fori(0, st.iters("out2")) as i:
                for job in range(2):
                    dve.wait_ge(S("chunks_multiplied"), st.done("out2", i, job))
                    x = x1[:, bass.ds(i * 8 + 4 * job, 4), :]
                    tt(x, x, set_of(job).rearrange("p (a b) -> p a b", a=4), ALU.add
                       ).then_inc(S(f"set_read{job}"), 1)
            dve.wait_ge(S("x3_summed"), 1)
            variance(rstd[:, 0, 0:T], bank(4, 0, T), D)
            rsqrt_wait()
            gained(hL, x1, "final_norm_g_2", rstd[:, 0, 0:T], KD).then_inc(S("x3_normed"), 1)


_INS = ["x", "c", "ctx", "c_ctx", "w_ada", "b_ada", "norm1_w", "w_in", "w_a_up_f", "b_a_f", "w_a_up_b", "b_a_b",
        "gla_onorm_w", "diff_qnorm_w", "diff_knorm_w", "lambda_q1", "lambda_k1", "lambda_q2", "lambda_k2",
        "diff_onorm_w", "w_proj_gla", "w_proj_diff", "w_gate", "b_gate", "w_out", "norm2_w", "w_up", "conv_w",
        "conv_b", "w_down", "mem_2", "norm_g_2", "w_in_2", "q_norm_g_2", "w_uq_2", "kv_norm_g_2", "w_ukv_2",
        "cmp_pe_k_2", "cmp_pe_v_2", "cmp_w1k_2", "cmp_w2k_2", "cmp_w1v_2", "cmp_w2v_2", "mem_norm_g_2",
        "w_mem_kv_2", "w_out_2", "final_norm_g_2"]


def kernel(**inputs):
    import concourse.bacc as bacc
    from concourse.bass_utils import run_bass_kernel_spmd

    nc = bacc.Bacc("TRN2", target_bir_lowering=False, num_devices=1)
    arrays, dram = {}, {}
    for name in _INS:
        a = np.ascontiguousarray(inputs[name])
        arrays[f"in_{name}"] = a
        ap = nc.dram_tensor(f"in_{name}", a.shape, F32, kind="ExternalInput").ap()
        dram[name] = ap[0] if len(a.shape) == 3 and name not in ("x", "ctx", "mem_2") else ap
    arrays["in_consts"] = shape_constants()
    dram["consts"] = nc.dram_tensor("in_consts", arrays["in_consts"].shape, F32, kind="ExternalInput").ap()
    out = nc.dram_tensor("out", (1, T, D), F32, kind="ExternalOutput").ap()
    x_spill = nc.dram_tensor("x_spill", (P, KD, T), F32, kind="Internal").ap()
    build(nc, dram, out, x_spill)
    r = run_bass_kernel_spmd(nc, [arrays], core_ids=[0])
    return r.results[0]["out"]
```

```python
import math
from contextlib import ExitStack

import numpy as np

import concourse.bass as bass
from concourse import mybir

F32 = mybir.dt.float32
F32R = mybir.dt.float32r
ACT = mybir.ActivationFunctionType
ALU = mybir.AluOpType
AXX = mybir.AxisListType.X

P = 128
T = 256
D = 2048
KD = D // P
EPS = 1e-6
DFF = 5632
KF = DFF // P
GC = 16
NB = T // GC
TAU = 16.0
LAM_INIT = 0.8 - 0.6 * math.exp(0.0)
NSA_SCALE = 192 ** -0.5
MLA_SCALE = 192 ** -0.5
MEM_SCALE = 128 ** -0.5
NCMP = T // 16 - 1
MASKED = -1e30

VECTORS = [("b_ada", 96), ("norm1_w", 16), ("b_gate", 32), ("norm2_w", 16), ("conv_w", 264), ("conv_b", 88),
           ("norm_g_2", 16), ("q_norm_g_2", 4), ("kv_norm_g_2", 4), ("mem_norm_g_2", 16), ("final_norm_g_2", 16),
           ("b_a_f", 4), ("b_a_b", 4), ("gla_onorm_w", 1), ("diff_onorm_w", 1), ("c", 16), ("c_ctx", 16)]
HALF_ROWS = [("diff_qnorm_w", "diff_qnorm_w"), ("diff_knorm_w", "diff_knorm_w"),
             ("lambda_q1", "lambda_q2"), ("lambda_k1", "lambda_k2")]
VROW, _at = {}, 0
for _n, _c in VECTORS:
    VROW[_n] = _at
    _at += _c
for _a, _b in HALF_ROWS:
    VROW[_a] = _at
    _at += 1
NVEC = _at
NVEC_DMAS = sum((VROW[n] + c - 1) // P - VROW[n] // P + 1 for n, c in VECTORS) + 2 * len(HALF_ROWS)

CONSTS = [("ident", 128), ("ones", 128), ("blk64", 128), ("rot16", 128), ("rot32", 128), ("cos2d", T), ("sin2d", T),
          ("cmprel", 32), ("cmpmask", 32), ("mask_f", T), ("mask_b", T), ("headind", 2), ("rowsel", 2),
          ("cos1d", T), ("sin1d", T), ("rel", 2 * T)]
CCOL, _at = {}, 0
for _n, _c in CONSTS:
    CCOL[_n] = (_at, _c)
    _at += _c
NCONST = _at
NCONST1 = CCOL["cos1d"][0]


def shape_constants():
    c = np.zeros((P, NCONST), np.float32)

    def put(name, value):
        a, n = CCOL[name]
        c[:, a:a + n] = np.asarray(value, np.float32).reshape(P, n)

    p = np.arange(P)
    put("ident", np.eye(P))
    put("ones", np.ones((P, P)))
    put("blk64", (p[:, None] // 64 == p[None, :] // 64))

    def rotation(half):
        m = np.zeros((P, P), np.float32)
        for o in range(P):
            if (o // half) % 2 == 0:
                m[o + half, o] = -1.0
            else:
                m[o - half, o] = 1.0
        return m

    put("rot16", rotation(16))
    put("rot32", rotation(32))
    tok = np.arange(T)
    f16 = (np.float32(10000.0) ** (-(np.arange(16, dtype=np.float32)) / np.float32(16))).astype(np.float32)
    d = p % 64
    pos = np.where(d[:, None] < 32, (tok // 64)[None, :], (tok % 64)[None, :]).astype(np.float32)
    ang = pos * f16[d % 16][:, None]
    put("cos2d", np.cos(ang))
    put("sin2d", np.sin(ang))
    f32 = (np.float32(10000.0) ** (-(np.arange(0, 64, 2, dtype=np.float32)) / np.float32(64))).astype(np.float32)
    ang = tok.astype(np.float32)[None, :] * f32[d % 32][:, None]
    put("cos1d", np.cos(ang))
    put("sin1d", np.sin(ang))
    q = (np.arange(2)[None, :] * P + p[:, None]).astype(np.float32)
    rel = tok[None, None, :] - q[:, :, None]
    put("rel", np.where(rel <= 0, rel, MASKED))
    n = np.arange(16)
    end = n * 16 + 31
    ok = (end[None, None, :] <= q[:, :, None]) & (n < NCMP)[None, None, :]
    crel = (n * 16 + 15.5)[None, None, :] - q[:, :, None]
    put("cmprel", np.where(ok, crel, MASKED))
    put("cmpmask", ok)
    blk = p[:, None, None] // 16 == np.arange(8)[None, :, None]
    io = np.arange(16)[None, None, :]
    jo = p[:, None, None] % 16
    put("mask_f", np.tile((blk & (jo <= io)).reshape(P, 128), (1, 2)))
    put("mask_b", np.tile((blk & (jo >= io)).reshape(P, 128), (1, 2)))
    put("rowsel", p[:, None] % 32 == np.arange(2)[None, :])
    put("headind", p[:, None] // 64 == np.arange(2)[None, :])
    return c


SLOTS = 4
KFA = 24
ADA_LATE = 16
SLOT_WORDS = 2048
X_WEIGHTS = 31232


def panel(w, col, width=512, rows=D, kt=4, step=0, kp=P, row=0):
    n = rows // kp
    return [(w, row + r * kp, min(kt, n - r), kp, col, width, step) for r in range(0, n, kt)]


def phases():
    out = []

    def phase(name, iters, jobs):
        out.append((name, iters, jobs))

    phase("ada_early", 4, [(panel("w_ada", 0, step=1024), (0,)), (panel("w_ada", 512, step=1024), (1,))])
    phase("gla_in", 1, [(panel("w_in", 512), (0, 1)), (panel("w_in", 1024), (0, 1)), (panel("w_in", 1536), (0, 1)),
                        (panel("w_in", 3072, 32, kt=16), (0, 1)), (panel("w_in", 0), (0,))])
    phase("dk_in", 1, [(panel("w_in", 4128), (0, 1)), (panel("w_in", 4640), (0, 1))])
    phase("dv_in", 1, [(panel("w_in", 5152), (0, 1)), (panel("w_in", 5664), (0, 1))])
    phase("dq_in", 1, [(panel("w_in", 3104), (0,)), (panel("w_in", 3616), (1,)),
                       (panel("w_in", 2048), (0,)), (panel("w_in", 2560), (1,))])
    phase("ada_late", 1, [(panel("w_ada", 4096 + 512 * n), (n % 2,)) for n in range(ADA_LATE)])
    phase("merge", 4, [(panel("w_gate", 0, step=512), (0,)), (panel("w_proj_gla", 0, rows=1024, step=512), (1,)),
                       (panel("w_gate", D, step=512), (0,)), (panel("w_proj_diff", 0, rows=1024, step=512), (1,))])
    phase("out", 2, [(panel("w_out", 0, step=1024), (0,)), (panel("w_out", 512, step=1024), (1,))])
    phase("up0", KFA // 4, [(panel("w_up", 0, step=512), (0,)), (panel("w_up", DFF, step=512), (1,))])
    phase("down0", 2, [(panel("w_down", 512 * n, rows=KFA * P, step=1024), (n,)) for n in range(2)])
    c = KFA * P
    phase("up1", (KF - KFA) // 4, [(panel("w_up", c, step=512), (0,)), (panel("w_up", DFF + c, step=512), (1,))])
    phase("down1", 1, [(panel("w_down", 512 * n, rows=DFF - c, row=c), (n % 2,)) for n in range(4)])
    phase("mem", 1, [(panel("w_mem_kv_2", 0), (0,)), (panel("w_mem_kv_2", 512), (1,))])
    jobs = [(panel("w_in_2", c, w, kt=min(16, SLOT_WORDS // w)), (n % 2,)) for n, (_, c, w) in enumerate(IN2)]
    phase("in2", 1, jobs)
    phase("uq", 1, [(panel("w_uq_2", 384 * n, 384, rows=512), (n % 2,)) for n in range(4)])
    phase("ukv", 1, [(panel("w_ukv_2", 512 * n, 512, rows=512), (n % 2,)) for n in range(4)])
    phase("cmp", 1, [(panel("cmp_w1k_2", 0, 192, rows=6144, kt=8, kp=96), (0,)),
                     (panel("cmp_w1v_2", 0, 128, rows=4096, kt=16), (1,))])
    phase("out2", 1, [(panel("w_out_2", 512 * n), (n % 2,)) for n in range(4)])
    return out


IN2 = [("cq", 0, 512), ("ckv", 512, 512), ("krope", 1024, 128), ("z0", 1088, 512), ("z1", 1600, 512),
       ("qn0", 2112, 384), ("qn1", 2496, 384), ("kc", 2880, 192), ("vc", 3072, 128), ("ks", 3200, 192),
       ("vs", 3392, 128), ("kw", 3520, 192), ("vw", 3712, 128), ("gn", 3840, 128), ("z2", 3852, 512),
       ("qm", 4364, 512), ("z3", 4876, 512)]


SPLIT = ["up0", "down0", "up1", "down1", "in2", "out2"]


class Stream:

    def __init__(self):
        self.phases = {n: (it, jobs) for n, it, jobs in phases()}
        self.info, last_use, g = {}, {}, 0
        landed = [0] * SLOTS
        uses = [0, 0]
        start = 0
        self.start = {}
        for name, (iters, jobs) in self.phases.items():
            n = sum(len(ch) for ch, _ in jobs)
            self.start[name] = start
            near = [None] * n
            for i in range(iters):
                for j in range(n):
                    s = (start + j) % SLOTS
                    far = g + i * n + j - last_use.get(s, -10 ** 6)
                    near[j] = far if near[j] is None else min(near[j], far)
                    last_use[s] = g + i * n + j
            near = [min(x, SLOTS) for x in near]
            per_slot = [sum((start + j) % SLOTS == s for j in range(n)) for s in range(SLOTS)]
            per_set = [sum(k in sets for _, sets in jobs) for k in (0, 1)]
            self.info[name] = (g, n, near, list(landed), per_slot, list(uses), per_set)
            start = (start + n) % SLOTS
            g += iters * n
            landed = [a + iters * b for a, b in zip(landed, per_slot)]
            uses = [a + iters * b for a, b in zip(uses, per_set)]

    def chunks(self, name):
        return [c for ch, _ in self.phases[name][1] for c in ch]

    def iters(self, name):
        return self.phases[name][0]

    def slot(self, name, j):
        return (self.start[name] + j) % SLOTS

    def slot_free(self, name, i, j):
        g, n, near, _, _, _, _ = self.info[name]
        return i * n + (g + j - near[j] + SLOTS + 1)

    def landed(self, name, i, j):
        _, _, _, landed, per_slot, _, _ = self.info[name]
        s = self.slot(name, j)
        return i * (16 * per_slot[s]) + 16 * (landed[s] + j // SLOTS + 1)

    def split_count(self, g):
        n = 0
        for name in SPLIT:
            a = self.info[name][0]
            n += max(0, min(g - a, self.iters(name) * self.info[name][1]))
        return n

    def index(self, name, j=0, job=0):
        return self.info[name][0] + self.first(name, job) + j

    def first(self, name, job):
        return sum(len(ch) for ch, _ in self.phases[name][1][:job])

    def done(self, name, i, job):
        g, n = self.info[name][:2]
        return i * n + (g + self.first(name, job + 1) + SLOTS)

    def set_uses(self, name, i, job, s):
        _, _, _, _, _, uses, per_set = self.info[name]
        before = sum(s in sets for _, sets in self.phases[name][1][:job])
        return i * per_set[s] + (uses[s] + before + 1)


def build(nc, dram, out_dram, x_spill):
    st = Stream()
    ctx = ExitStack()
    with ctx:
        def sb(name, shape):
            return ctx.enter_context(nc.sbuf_tensor(name, shape, F32))

        sems = {}

        def S(name):
            if name not in sems:
                sems[name] = ctx.enter_context(nc.semaphore(name))
            return sems[name]

        ring = sb("ring", [P, SLOTS, SLOT_WORDS])
        cst = sb("cst", [P, NCONST1])
        vec = sb("vec", [P, NVEC])
        ada = sb("ada", [P, 96, 2])
        csil = sb("csil", [P, KD, 32])
        ctmp = sb("ctmp", [P, 32])
        amod = sb("amod", [P, 3, KD])
        nbgate = sb("nbgate", [P, 32])
        rstd = sb("rstd", [P, 2, 512])
        small = sb("small", [P, 64])
        refs = sb("refs", [P, 2, 8, 17])
        shared = sb("shared", [P, 2, 512])
        wup = shared[0:32, :, :]

        with ExitStack() as parts:
            def sbr(name, shape):
                return parts.enter_context(nc.sbuf_tensor(name, shape, F32R))

            fh = [sbr("fh_hi", [P, KFA, T]), sbr("fh_lo", [P, KFA, T])]
            hs = [sbr("h_hi", [P, KD, T]), sbr("h_lo", [P, KD, T])]
            gap = parts.enter_context(nc.sbuf_tensor("gap", [P, X_WEIGHTS - 2 * (KFA + KD) * T], F32))
            ws = [[sbr(f"w_{part}{b}", [P, SLOT_WORDS]) for b in range(2)] for part in ("hi", "lo")]
        hL = sb("hL", [P, KD, T])
        hC = sb("hC", [P, KD, T])
        big = sb("big", [P, X_WEIGHTS + 4 * SLOT_WORDS - 2 * KD * T])
        psum = ctx.enter_context(nc.psum_tensor("psum", [P, 8 * 512], F32))

        def bank(b, a=0, n=512):
            return psum[:, b * 512 + a:b * 512 + a + n]

        def two_banks(n):
            return psum[:, 6 * 512:8 * 512].rearrange("p (a b) -> p a b", a=2)[:, :, 0:n]

        def set_of(s):
            return psum[:, s * 1024:s * 1024 + 1024]

        def C(name, parts=P):
            a, n = CCOL[name]
            if a >= NCONST1:
                return shared[0:parts, :, :].rearrange("p a b -> p (a b)")[:, a - NCONST1:a - NCONST1 + n]
            return cst[0:parts, a:a + n]

        def V(name, k=0, n=1):
            return vec[:, VROW[name] + k:VROW[name] + k + n]

        def cut(flat, *shape):
            if len(shape) == 2:
                return flat.rearrange("p (a b) -> p a b", a=shape[0])
            if len(shape) == 3:
                return flat.rearrange("p (a b c) -> p a b c", a=shape[0], b=shape[1])
            return flat

        def area(at, *shape):
            return cut(big[:, at:at + int(np.prod(shape))], *shape)

        def carea(at, *shape):
            return cut(hC[:, :, :].rearrange("p a b -> p (a b)")[:, at:at + int(np.prod(shape))], *shape)

        def larea(at, *shape):
            return cut(hL[:, :, :].rearrange("p a b -> p (a b)")[:, at:at + int(np.prod(shape))], *shape)

        vstage = area(0, 5, P)
        nat = area(1024, 4, D)
        xT0 = area(9216, KD, T)
        cT0 = area(13312, KD, T)
        rows_early = area(17408, 2, 512)
        gq = area(0, 4, T)
        gk = area(1024, 4, 2, T)
        gv = area(3072, 4, 1024)
        asum = area(5120, 2, 512)
        qx = area(6144, 4, T)
        gr = area(7168, 8, T)
        dq = area(9216, 8, T)
        dk = area(11264, 8, 2, T)
        dv = area(15360, 4, 1024)
        bufs = [area(19456 + 2056 * d, 4, 2, 257) for d in range(2)]
        KC = 23568
        zb = area(KC, 4, 512)
        ztmp = area(KC + 2048, 2048)
        smem = area(29200, 8, 128)
        kst = area(9216, 2, 2, T)
        pd = [carea(0, GC, 8, GC), carea(2048, GC, 8, GC)]
        yg = area(1024, 8, T)
        ga = rstd[0:32, 0, :]
        dp = area(19456, 8, 512)
        dsq = area(KC, 2, 512)
        dmul = area(KC + 1024, 2, 512)
        daT = [area(KC + 2048 + 1024 * b, 4, T) for b in range(2)]
        mT = area(3072, KD, T)
        gsb = [area(24000 + 1024 * b, 4, T) for b in range(2)]
        x1 = area(18944, KD, T)
        x0 = area(14848, KD, T)
        ftap = [area(12288 + 1024 * b, 4, T) for b in range(2)]
        fexp = area(14336, 4, T)
        memnat = area(12288, 2, D)
        sq2 = area(0, KD, T)
        cq = area(0, 4, T)
        ckv = area(1024, 4, T)
        kpe = area(2048, T)
        kcT = area(2304, 2, T)
        vcT = area(2816, T)
        vs = area(3072, 2, P)
        vw = area(3328, 2, P)
        gn = area(3584, T)
        causal = area(3840, 256)
        zT = larea(0, 16, T)
        qn = area(12288, 8, T)
        ksT = area(14336, 2, T)
        kwT = area(14848, 2, T)
        qm = area(15360, 4, T)
        mqn = area(4096, 8, T)
        mqr = area(6144, 4, T)
        mkn = area(7168, 8, T)
        mv = area(9216, 2, 1024)
        rtmp = area(11264, 2, 512)
        zexp = area(24576, KD * T)
        obuf = area(23552, 24, T)
        km = carea(0, 4, T)
        vm = carea(1024, 2, 512)
        ssb = area(16384, 4, T)
        prob = area(29696, 4, T)
        aT = [carea(3072 + 512 * b, 2, T) for b in range(2)]
        kcp = area(16384, 2, 32, NCMP)
        vcp = area(17344, 32, NCMP)
        hidk = area(17824, 2, 16)
        hidv = area(17856, 16)
        hexp = area(17872, 48)
        kcmp = area(17920, 2, 16)
        vcmp = area(17952, 128)
        w2k = area(18080, 2, 192)
        w2v = area(18464, 128)
        peT = area(18592, 3, 32)
        pek = area(23552, 192)
        pev = area(23744, 128)
        rtmpsq = [area(16384, 4, T), area(17408, 4, T)]
        onat = area(0, 2, D)

        def chunk_and_part(g, s, part):
            if g != st.index("in2", job=[n for n, _, _ in IN2].index("krope")):
                return ring[:, s, :], part
            return (cut(ring[:, s, 0:KD * 64], KD, 64).unsqueeze(2).to_broadcast([P, KD, 2, 64]),
                    cut(part, KD, 2, 64))

        block = ctx.enter_context(nc.Block())

        @block.sync
        def _(sp):
            def load(name, i, c, j):
                w, row0, kt, kp, col, width, step = c
                s = st.slot(name, j)
                sp.wait_ge(S("chunks_multiplied"), st.slot_free(name, i, j))
                a = col + i * step
                rows = dram[w][row0:row0 + kt * kp, :].rearrange("(k p) n -> p k n", p=kp)
                if (name, col) == ("in2", 1024):
                    width = 64
                dst = ring[0:kp, s, 0:kt * width].rearrange("p (k n) -> p k n", k=kt)
                src = rows[:, :, bass.ds(a, width)] if st.iters(name) > 1 else rows[:, :, a:a + width]
                sp.dma_start(dst, src).then_inc(S(f"slot_loaded{s}"), 16)

            for name in st.phases:
                chunks = st.chunks(name)
                if st.iters(name) > 1:
                    with sp.Fori(0, st.iters(name)) as i:
                        for j, c in enumerate(chunks):
                            load(name, i, c, j)
                else:
                    for j, c in enumerate(chunks):
                        load(name, 0, c, j)
            for t in range(2):
                sp.wait_ge(S("out_copied"), 4 * (t + 1))
                sp.dma_start(out_dram[0, t * P:(t + 1) * P, :], onat[:, t, :]).then_inc(S("out_stored"), 16)
            sp.wait_ge(S("out_stored"), 32)

        @block.gpsimd
        def _(pool):
            pool.dma_start(cst[:, :], dram["consts"][:, 0:NCONST1]).then_inc(S("consts_loaded"), 16)
            pool.memset(csil[:, :, :], 0.0).then_inc(S("csil_cleared"), 1)
            nvec = 0

            def rows_in(row, n, view):
                nonlocal nvec
                done = 0
                while done < n:
                    k = min(n - done, P - (row + done) % P)
                    r = row + done
                    pool.dma_start(vstage[r % P:r % P + k, r // P, :], view[done:done + k, :]
                                   ).then_inc(S("vectors_loaded"), 16)
                    nvec += 1
                    done += k

            for name, n in VECTORS:
                ap = dram[name]
                if name == "c_ctx":
                    ap = ap.rearrange("(t p) -> t p", p=P)
                elif name == "final_norm_g_2":
                    ap = ap.rearrange("(t p) -> t p", p=P)
                elif name == "conv_w":
                    ap = ap.rearrange("j (t p) -> (j t) p", p=P)
                else:
                    ap = ap.rearrange("a (t p) -> (a t) p", p=P)
                rows_in(VROW[name], n, ap)
            for a, b in HALF_ROWS:
                for h, name in enumerate((a, b)):
                    r = VROW[a]
                    pool.dma_start(vstage[r % P:r % P + 1, r // P, 64 * h:64 * h + 64], dram[name]
                                   ).then_inc(S("vectors_loaded"), 16)
                    nvec += 1
            assert nvec == NVEC_DMAS, nvec
            for t in range(2):
                pool.dma_start(nat[:, t, :], dram["x"][0, t * P:(t + 1) * P, :]).then_inc(S(f"tokens_loaded{t}"), 16)
            for t in range(2):
                pool.dma_start(nat[:, 2 + t, :], dram["ctx"][0, t * P:(t + 1) * P, :]
                               ).then_inc(S(f"tokens_loaded{2 + t}"), 16)
            pool.memset(wup[:, :, :], 0.0).then_inc(S("wup_cleared"), 1)
            pool.wait_ge(S("wup_cleared"), 1)
            pool.dma_start(wup[0:16, 0, :], dram["w_a_up_f"]).then_inc(S("wup_loaded"), 16)
            pool.dma_start(wup[16:32, 1, :], dram["w_a_up_b"]).then_inc(S("wup_loaded"), 16)
            pool.wait_ge(S("x_transposed"), 8)
            pool.dma_start(x_spill, xT0[:, :, :]).then_inc(S("x_spilled"), 16)
            pool.wait_ge(S("gates_summed"), 2)
            pool.memset(area(KC, 5632), 0.0).then_inc(S("kc_cleared"), 1)
            pool.wait_ge(S("diff_pv_done"), 8)
            pool.dma_start(x0[:, :, :], x_spill).then_inc(S("x_back"), 16)
            pool.wait_ge(S("ffn_hidden"), KF // 4 + 1)
            pool.dma_start(shared[:, :, :].rearrange("p a b -> p (a b)"), dram["consts"][:, NCONST1:NCONST]
                           ).then_inc(S("consts2_loaded"), 16)
            for t in range(2):
                pool.dma_start(memnat[:, t, :], dram["mem_2"][0, t * P:(t + 1) * P, :]).then_inc(S("mem_loaded"), 16)
            pool.wait_ge(S("chunks_multiplied"), st.done("in2", 0, len(IN2) - 1))
            pool.dma_start(w2k[0:96, :, :], dram["cmp_w2k_2"].rearrange("(h p) n -> p h n", p=96)
                           ).then_inc(S("cmp_loaded"), 16)
            pool.dma_start(w2v[:, :], dram["cmp_w2v_2"]).then_inc(S("cmp_loaded"), 16)
            pool.dma_start(pek[0:32, :], dram["cmp_pe_k_2"]).then_inc(S("cmp_loaded"), 16)
            pool.dma_start(pev[0:32, :], dram["cmp_pe_v_2"]).then_inc(S("cmp_loaded"), 16)
            pool.wait_ge(S("x_spilled"), 16)

        def kc(d, b):
            if d == 0:
                at, n, tok = ((b - 1) * 128, 128, 0) if b <= 8 else (1024 + (b - 9) * 256, 256, 0)
            else:
                at, n, tok = (2816 + b * 256, 256, 0) if b <= 6 else (2816 + 1792 + (b - 7) * 128, 128, 128)
            return big[:, KC + at:KC + at + n], tok

        def key_range(d, b):
            return (0, GC * b) if d == 0 else (GC * (b + 1), T)

        BLOCKS = [range(1, NB), range(0, NB - 1)]

        OUTS = [("mla", h, h) for h in range(8)]
        OUTS += [(k, 8 + 3 * h + n, h) for h in range(4) for n, k in enumerate(("cmp", "slc", "win"))]
        OUTS += [("mem", 20 + h, h) for h in range(4)]

        def keys_seen(kind, qt):
            return NCMP if kind == "cmp" else T if kind == "mem" else P * (qt + 1)

        @block.tensor
        def _(pe):
            mm = nc.tensor.matmul

            def gemm(name, i, job, products, split=False, hidden=None):
                chunks, sets = st.phases[name][1][job]
                started, k0, j0 = set(), 0, st.first(name, job)
                for q, (_, _, kt, kp, _, width, _) in enumerate(chunks):
                    s = st.slot(name, j0 + q)
                    if not split:
                        pe.wait_ge(S(f"slot_loaded{s}"), st.landed(name, i, j0 + q))
                    if q == 0:
                        for k in sets:
                            pe.wait_ge(S(f"set_read{k}"), st.set_uses(name, i, job, k))
                    if hidden is not None:
                        pe.wait_ge(S("ffn_hidden"), hidden + q + 2)
                    if split:
                        g = st.index(name, j0 + q)
                        n = sum(len(ch) for ch, _ in st.phases[name][1])
                        pe.wait_ge(S("weights_split"), i * n + st.split_count(g) + 1)
                        hi, lo = (w[g % 2][:, 0:kt * width].rearrange("p (k n) -> p k n", k=kt) for w in ws)
                        todo = [products(k0 + k, w[:, k, :], part) for k in range(kt)
                                for w, part in ((hi, 0), (hi, 1), (lo, 0))]
                    else:
                        slot = ring[0:kp, s, 0:kt * width].rearrange("p (k n) -> p k n", k=kt)
                        todo = [products(k0 + k, slot[:, k, :]) for k in range(kt)]
                    for m in range(len(todo[0])):
                        for k in range(len(todo)):
                            out, b, lhsT, rhs = todo[k][m]
                            last = mm(out, lhsT, rhs, start=b not in started,
                                      stop=q == len(chunks) - 1 and k == len(todo) - 1, skip_group_check=True)
                            started.add(b)
                    k0 += kt
                    last.then_inc(S("chunks_multiplied"), 1)

            def features(s, act, width=512, m=P):
                def products(k, w, part=None):
                    a = act if part is None else act[part]
                    return [(set_of(s)[0:min(m, width - c), n * T:(n + 1) * T], (s, n // 2),
                             w[:, c:min(c + m, width)], a[:, k, :])
                            for n, c in enumerate(range(0, width, m))]
                return products

            def tokens(s, act, width=512):
                def products(k, w, part=None):
                    a = act if part is None else act[part]
                    return [(set_of(s)[:, t * 512:t * 512 + width], (s, t), a[:, k, t * P:(t + 1) * P], w)
                            for t in range(2)]
                return products

            def both(a, b):
                return lambda k, w: a(k, w) + b(k, w)

            def transposed(out, in_):
                n = in_.shape[0]
                return nc.tensor.transpose(out, in_, C("ident", n)[:, 0:n])

            def sums(out, weights, sq, tiles):
                for k in range(tiles):
                    last = mm(out, weights, sq[:, k, :], start=k == 0, stop=k == tiles - 1)
                return last

            pe.sem_inc(S("chunks_multiplied"), SLOTS)
            for s in range(2):
                pe.sem_inc(S(f"set_read{s}"), 1)
            pe.wait_ge(S("consts_loaded"), 16)
            pe.wait_ge(S("vectors_loaded"), 16 * NVEC_DMAS)
            for n in range(5):
                rows = min(P, NVEC - n * P)
                last = transposed(bank(6 + n // 4, (n % 4) * P, rows), vstage[0:rows, n, :])
            last.then_inc(S("vectors_transposed"), 1)
            for n in range(16):
                t, g = n // 4, n % 4
                pe.wait_ge(S(f"tokens_loaded{t}"), 16)
                if n >= 2:
                    pe.wait_ge(S("x_transposed"), n - 1)
                for k in range(4):
                    last = transposed(bank(4 + n % 2, k * P, P), nat[:, t, (4 * g + k) * P:(4 * g + k + 1) * P])
                last.then_inc(S("x_in_psum"), 1)
            pe.wait_ge(S("vectors_copied"), 1)
            for n, sq in enumerate((hL, hC)):
                pe.wait_ge(S("x_squared"), n + 1)
                sums(bank(6 + n, 0, T), C("ones"), sq, KD).then_inc(S("x_summed"), 1)

            def ada_rows(name, i, job):
                s = job % 2
                gemm(name, i, job, lambda k, w: [
                    (bank(2 * s)[32 * (k % 4):32 * (k % 4) + 32, :], (s, k % 4), csil[:, k, :], w)])

            def ada_fold(s, rows, n):
                pe.wait_ge(S("ada_rows_copied"), n)
                for m in range(4):
                    last = mm(bank(2 * s + 1, 2 * m, 2), rows[:, s, m * P:(m + 1) * P], C("rowsel"),
                              start=True, stop=True)
                last.then_inc(S("ada_folded"), 1)

            def ada_late(first, last):
                for n in range(first, last):
                    ada_rows("ada_late", 0, n)
                    if n:
                        ada_fold((n - 1) % 2, shared, 8 + n)
                if last == ADA_LATE:
                    ada_fold((ADA_LATE - 1) % 2, shared, 8 + ADA_LATE)

            pe.wait_ge(S("c_activated"), 1)
            with pe.Fori(0, st.iters("ada_early")) as i:
                for job in range(2):
                    ada_rows("ada_early", i, job)
                for job in range(2):
                    ada_fold(job, rows_early, i * 2 + (job + 1))
            pe.wait_ge(S("h_ready"), 2)
            gemm("gla_in", 0, 0, both(features(0, hL), features(1, hC)))
            gemm("gla_in", 0, 1, both(tokens(0, hL), tokens(1, hC)))
            gemm("gla_in", 0, 2, both(tokens(0, hL), tokens(1, hC)))
            gemm("gla_in", 0, 3, both(features(0, hL, 32), features(1, hC, 32)))
            gemm("gla_in", 0, 4, features(0, hL))
            pe.wait_ge(S("set_read0"), st.set_uses("gla_in", 0, 4, 0))
            pe.wait_ge(S("set_read1"), st.set_uses("dk_in", 0, 0, 1))
            pe.wait_ge(S("wup_loaded"), 32)
            for n in range(8):
                if n >= 4:
                    pe.wait_ge(S("z_read"), n - 3)
                mm(bank(4 + n % 4), wup[:, n // 4, (n % 4) * P:(n % 4 + 1) * P], ga, start=True, stop=True
                   ).then_inc(S("z_ready"), 1)
            for job in range(2):
                gemm("dk_in", 0, job, both(features(0, hL), features(1, hC)))
            pe.wait_ge(S("z_read"), 8)
            for n in range(8):
                pe.wait_ge(S("ctx_keys_scaled"), n + 1)
                if n:
                    pe.wait_ge(S("ctx_keys_copied"), n)
                for t in range(2):
                    last = transposed(bank(6, t * P, P), kst[:, n % 2, 0, t * P:(t + 1) * P])
                last.then_inc(S("ctx_keys_transposed"), 1)
                pe.wait_ge(S("ctx_keys_copied"), n + 1)
                if n:
                    pe.wait_ge(S("states_copied"), n)
                for h in range(2):
                    head = 2 * (n // 2) + h
                    for t in range(2):
                        last = mm(bank(7, 0, P)[64 * h:64 * h + 64, :], kst[:, n % 2, 1, t * P + 64 * h:t * P + 64 * h + 64],
                                  gv[:, 2 + t, head * P:(head + 1) * P], start=t == 0, stop=t == 1)
                last.then_inc(S("states_ready"), 1)
            for job in range(2):
                gemm("dv_in", 0, job, both(tokens(0, hL), tokens(1, hC)))

            def gla_diagonals(p, first):
                if p and not first:
                    pe.wait_ge(S("gla_normed"), p)
                for e in (first, first + 1):
                    pe.wait_ge(S("gla_diag_ready"), 4 * p + e + 1)
                    for io in range(GC):
                        last = mm(bank(6, (e * GC + io) * 2, 2), pd[e % 2][:, io, :, :].rearrange("p b j -> p (b j)"),
                                  C("headind"), start=True, stop=True)
                    last.then_inc(S("gla_diag_summed"), 1)

            def gla_pair(p):
                pe.wait_ge(S("gla_operands_ready"), p + 1)
                if p:
                    pe.wait_ge(S("gla_normed"), p)
                else:
                    pe.wait_ge(S("states_copied"), 8)
                for h in range(2):
                    first = True
                    for d in range(2):
                        for b in BLOCKS[d]:
                            keys, tok = kc(d, b)
                            lo, hi = key_range(d, b)
                            for t in range(2):
                                if hi > t * P and lo < (t + 1) * P:
                                    last = mm(bank(4 + h, t * T + GC * b, GC),
                                              keys[64 * h:64 * h + 64, t * P - tok:(t + 1) * P - tok],
                                              qx[64 * h:64 * h + 64, 2 + d, GC * b:GC * (b + 1)],
                                              start=first, stop=True, skip_group_check=True)
                                    first = False
                last.then_inc(S("gla_blocks_done"), 1)
                gla_diagonals(p, 2)
                pe.wait_ge(S("gla_scores_ready"), 2 * p + 2)
                for h in range(2):
                    head = 2 * p + h
                    for t in range(2):
                        mm(bank(6 + h, 0, T), gv[:, t, head * P:(head + 1) * P], asum[:, h, t * T:(t + 1) * T],
                           start=t == 0, stop=False)
                    for d in range(2):
                        last = mm(bank(6 + h, 0, T), smem[64 * h:64 * h + 64, 2 * p + d, :],
                                  qx[64 * h:64 * h + 64, d, :], start=False, stop=d == 1)
                last.then_inc(S("gla_out_ready"), 1)
                pe.wait_ge(S("gla_squared"), p + 1)
                mm(bank(4), C("ones"), rstd[:, 1, :], start=True, stop=True).then_inc(S("gla_summed"), 1)

            for pair in range(4):
                for half in range(2):
                    if pair < 2:
                        gemm("dq_in", 0, 2 * pair + half, features(half, hL))
                    else:
                        ada_late(6 * (pair - 2) + 3 * half, 6 * (pair - 2) + 3 * half + 3)
                    if half == 0:
                        gla_diagonals(pair, 0)
                gla_pair(pair)

            pe.wait_ge(S("gla_normed"), 4)
            for g in range(12):
                if g % 3 == 0:
                    ada_late(12 + g // 3, 13 + g // 3)
                pe.wait_ge(S("qk_squared"), g + 1)
                mm(bank(4 + g % 2), C("blk64"), dsq[:, g % 2, :], start=True, stop=True).then_inc(S("qk_summed"), 1)
                pe.wait_ge(S("qk_normed"), g + 1)
                n = 512 if g < 4 else T
                src = dq[:, 2 * g:2 * g + 2, :].rearrange("p a b -> p (a b)") if g < 4 else dk[:, g - 4, 0, :]
                mm(bank(6 + g % 2, 0, n), C("rot16"), src, start=True, stop=True).then_inc(S("qk_rotated"), 1)
            pe.wait_ge(S("lambda_products"), 1)
            pe.wait_ge(S("qk_done"), 12)
            for h in range(2):
                last = mm(bank(6 + h, 0, 1), C("ones")[64 * h:64 * h + 64, :], small[64 * h:64 * h + 64, 0:1],
                          start=True, stop=True)
            last.then_inc(S("lambda_summed"), 1)
            pe.wait_ge(S("lambda_done"), 1)

            def diff_scores(n):
                h, qt, m = n // 4, (n // 2) % 2, n % 2
                if n >= 4:
                    pe.wait_ge(S("diff_exps"), n - 3)
                mm(bank(2 + n % 4), dq[64 * m:64 * m + 64, h, qt * P:(qt + 1) * P],
                   dk[64 * m:64 * m + 64, h, :, :].rearrange("p a b -> p (a b)"), start=True, stop=True
                   ).then_inc(S("diff_scores_ready"), 1)

            def diff_transpose(u):
                pe.wait_ge(S("diff_probs_ready"), u + 1)
                if u >= 2:
                    pe.wait_ge(S("diff_probs_copied"), u - 1)
                for k in range(4):
                    last = transposed(bank((6, 1)[u % 2], k * P, P), dp[:, 2 * (u % 4), k * P:(k + 1) * P])
                last.then_inc(S("diff_probs_transposed"), 1)

            def diff_values(h):
                pe.wait_ge(S("diff_probs_copied"), 2 * h + 2)
                if h >= 2:
                    pe.wait_ge(S("diff_out_copied"), h - 1)
                for k in range(4):
                    last = mm(bank((7, 0)[h % 2], 0, T), dv[:, k, h * P:(h + 1) * P], daT[h % 2][:, k, :],
                              start=k == 0, stop=k == 3)
                last.then_inc(S("diff_pv_done"), 1)

            for s in range(2):
                pe.wait_ge(S(f"set_read{s}"), st.set_uses("merge", 0, 0, s))
            for u in range(16 + 3):
                if u < 16:
                    diff_scores(2 * u)
                    diff_scores(2 * u + 1)
                if 2 <= u < 16 + 2:
                    diff_transpose(u - 2)
                if u >= 3 and u % 2 == 0:
                    diff_values((u - 3) // 2)
            for g in range(4):
                pe.wait_ge(S("diff_squared"), g + 1)
                if g >= 2:
                    pe.wait_ge(S("diff_normed"), g - 1)
                mm(bank(4 + g % 2), C("ones"), dsq[:, g % 2, :], start=True, stop=True).then_inc(S("diff_summed"), 1)

            pe.wait_ge(S("gla_gated"), 1)
            pe.wait_ge(S("diff_normed"), 4)
            with pe.Fori(0, st.iters("merge")) as i:
                gemm("merge", i, 0, features(0, hL))
                gemm("merge", i, 1, features(1, yg))
                gemm("merge", i, 2, features(0, hL))
                gemm("merge", i, 3, features(1, dq))
            pe.wait_ge(S("merged"), st.iters("merge") + 1)
            with pe.Fori(0, st.iters("out")) as i:
                for job in range(2):
                    gemm("out", i, job, features(job, mT))
            pe.wait_ge(S("x1_squared"), 1)
            sums(bank(4, 0, T), C("ones"), hC, KD).then_inc(S("x1_summed"), 1)
            pe.wait_ge(S("h2_ready"), 1)
            for part in range(2):
                with pe.Fori(0, st.iters(f"up{part}")) as i:
                    for job in range(2):
                        gemm(f"up{part}", i, job, features(job, hs), split=True)
                if part == 0:
                    with pe.Fori(0, 2) as i:
                        for job in range(2):
                            gemm("down0", i, job, features(job, fh), split=True, hidden=0 if job == 0 else None)
                else:
                    for job in range(4):
                        gemm("down1", 0, job, features(job % 2, fh), split=True,
                                 hidden=KFA // 4 if job == 0 else None)

            for n in range(8):
                t, g = n // 4, n % 4
                if n == 0:
                    pe.wait_ge(S("mem_loaded"), 32)
                if n >= 2:
                    pe.wait_ge(S("mem_transposed"), n - 1)
                for k in range(4):
                    last = transposed(bank(4 + n % 2, k * P, P), memnat[:, t, (4 * g + k) * P:(4 * g + k + 1) * P])
                last.then_inc(S("mem_in_psum"), 1)
            pe.wait_ge(S("mem_squared"), 1)
            sums(bank(6, 0, T), C("ones"), sq2, KD).then_inc(S("mem_summed"), 1)
            pe.wait_ge(S("x2_squared"), 1)
            sums(bank(7, 0, T), C("ones"), hL, KD).then_inc(S("x2_summed"), 1)
            pe.wait_ge(S("mem_ready"), 1)
            gemm("mem", 0, 0, features(0, hC))
            gemm("mem", 0, 1, tokens(1, hC))
            pe.wait_ge(S("h3_ready"), 1)
            for n, (name, _, width) in enumerate(IN2):
                s = n % 2
                if name in ("vs", "vw"):
                    gemm("in2", 0, n, tokens(s, hs, width), split=True)
                else:
                    m = 96 if name in ("qn0", "qn1", "kc", "ks", "kw") else P
                    gemm("in2", 0, n, features(s, hs, width, m), split=True)
                if name == "ckv":
                    for v in range(2):
                        pe.wait_ge(S("lowrank_squared"), v + 1)
                        sums(bank(4 + v, 0, T), C("ones"), rtmpsq[v], 4).then_inc(S("lowrank_summed"), 1)
            for n in range(4):
                s = n % 2
                pe.wait_ge(S("cq_normed"), 1)

                def query_pair(k, w, s=s):
                    return [(set_of(s)[:, 0:T], (s, 0), w[:, 0:P], cq[:, k, :]),
                            (set_of(s)[:, T:2 * T], (s, 0), w[:, 192:192 + P], cq[:, k, :]),
                            (set_of(s)[0:64, 2 * T:3 * T], (s, 1, 0), w[:, P:192], cq[:, k, :]),
                            (set_of(s)[64:P, 2 * T:3 * T], (s, 1, 1), w[:, 192 + P:384], cq[:, k, :])]
                gemm("uq", 0, n, query_pair)
            for n in range(4):
                s = n % 2
                pe.wait_ge(S("ckv_normed"), 1)

                def key_pair(k, w, s=s):
                    values = w.rearrange("p (h c) -> p h c", h=2)[:, :, P:2 * P]
                    return [(set_of(s)[:, 0:T], (s, 0), w[:, 0:P], ckv[:, k, :]),
                            (set_of(s)[:, T:2 * T], (s, 0), w[:, 2 * P:3 * P], ckv[:, k, :]),
                            (set_of(s)[:, 2 * T:3 * T], (s, 1), ckv[:, k, 0:P], values),
                            (set_of(s)[:, 3 * T:4 * T], (s, 1), ckv[:, k, P:2 * P], values)]
                gemm("ukv", 0, n, key_pair)
            for n in range(5):
                if n == 0:
                    for s in range(2):
                        pe.wait_ge(S(f"set_read{s}"), st.set_uses("ukv", 0, s, s))
                if n >= 2:
                    pe.wait_ge(S("rope_done"), n - 1)
                src = mqr[:, n, :] if n < 4 else kpe
                mm(bank(4 + n % 2, 0, T), C("rot32"), src, start=True, stop=True).then_inc(S("rope_rotated"), 1)
            pe.wait_ge(S("cmp_loaded"), 64)
            pe.wait_ge(S("rope_done"), 5)
            for h in range(2):
                transposed(bank(6, 32 * h, 32)[0:96, :], pek[0:32, 96 * h:96 * h + 96])
            transposed(bank(6, 64, 32), pev[0:32, :]).then_inc(S("pe_transposed"), 1)
            pe.wait_ge(S("cmp_blocks_ready"), 1)
            gemm("cmp", 0, 0, lambda k, w: [
                (set_of(0)[0:96, m * 16:m * 16 + NCMP], (0, 0), w[:, 96 * m:96 * m + 96], kcp[0:96, k % 2, k // 2, :])
                for m in range(2)])
            gemm("cmp", 0, 1, lambda k, w: [(set_of(1)[:, 0:NCMP], (1, 0), w, vcp[:, k, :])])
            for s in range(2):
                pe.wait_ge(S(f"set_read{s}"), st.set_uses("out2", 0, s, s))
            for m in range(2):
                for k in range(2):
                    mm(bank(6, 16 * m, NCMP)[0:96, :], w2k[0:96, k, 96 * m:96 * m + 96], hidk[0:96, k, 0:NCMP],
                       start=k == 0 and m == 0, stop=k == 1, skip_group_check=True)
            mm(bank(7, 0, P)[0:NCMP, :], hidv[:, 0:NCMP], w2v[:, :], start=True, stop=True
               ).then_inc(S("cmp_projected"), 1)
            pe.wait_ge(S("cmp_done"), 1)

            def scores2(u):
                kind, o, h = OUTS[u // 2]
                qt = u % 2
                q = slice(qt * P, (qt + 1) * P)
                n = keys_seen(kind, qt)
                out = bank(2 + u % 4, 0, n)
                if u >= 4:
                    pe.wait_ge(S("exps2"), u - 3)
                if kind == "mla":
                    r = slice(64 * (h % 2), 64 * (h % 2) + 64)
                    terms = [(mqn[:, h, q], mkn[:, h, 0:n]), (mqr[r, h // 2, q], kpe[r, 0:n])]
                elif kind == "mem":
                    terms = [(qm[:, h, q], km[:, h, 0:n])]
                else:
                    keys = {"cmp": kcmp, "slc": ksT, "win": kwT}[kind]
                    terms = [(qn[0:96, 2 * h + k, q], keys[0:96, k, 0:n]) for k in range(2)]
                for k, (lhsT, rhs) in enumerate(terms):
                    last = mm(out, lhsT, rhs, start=k == 0, stop=k == len(terms) - 1)
                last.then_inc(S("scores2_ready"), 1)

            def transpose2(u):
                kind, o, h = OUTS[u // 2]
                n = keys_seen(kind, u % 2)
                pe.wait_ge(S("probs2_ready"), u + 1)
                if u >= 2:
                    pe.wait_ge(S("probs2_copied"), u - 1)
                for k in range((n + P - 1) // P):
                    w = min(P, n - k * P)
                    last = transposed(bank((6, 1)[u % 2], k * P, P)[0:w, :], prob[:, u % 4, k * P:k * P + w])
                last.then_inc(S("probs2_transposed"), 1)

            def values2(u):
                kind, o, h = OUTS[u // 2]
                pe.wait_ge(S("probs2_copied"), u + 1)
                if u >= 4:
                    pe.wait_ge(S("out2_copied"), u // 2 - 1)
                a = aT[(u // 2) % 2]
                if kind == "cmp":
                    terms = [(vcmp[0:NCMP, :], a[0:NCMP, 0, :], 0)]
                elif kind == "mem":
                    terms = [(vm[:, k, h * P:(h + 1) * P], a[:, k, :], 0) for k in range(2)]
                else:
                    v = [mv[:, k, h * P:(h + 1) * P] if kind == "mla" else (vs if kind == "slc" else vw)[:, k, :]
                         for k in range(2)]
                    terms = [(v[0], a[:, 0, :], 0), (v[1], a[:, 1, P:T], P)]
                for k, (lhsT, rhs, c) in enumerate(terms):
                    last = mm(bank((7, 0)[u // 2 % 2], c, T - c), lhsT, rhs, start=k == 0, stop=k == len(terms) - 1,
                              skip_group_check=True)
                last.then_inc(S("out2_ready"), 1)

            units = 2 * len(OUTS)
            for u in range(units + 3):
                if u < units:
                    scores2(u)
                if 2 <= u < units + 2:
                    transpose2(u - 2)
                if u >= 3 and u % 2 == 0:
                    values2(u - 3)
            for n in range(12):
                if n == 0:
                    pe.wait_ge(S("nsa_gates_ready"), 1)
                    pe.wait_ge(S("out2_copied"), len(OUTS))
                if n >= 2:
                    pe.wait_ge(S("nsa_gated"), n - 1)
                mm(bank(4 + n % 2, 0, T), C("ident", 12)[:, n:n + 1].to_broadcast([12, P]), gn[0:12, :],
                   start=True, stop=True).then_inc(S("nsa_gate_rows"), 1)
            pe.wait_ge(S("mixed2"), 1)
            for job in range(4):
                gemm("out2", 0, job, features(job % 2, hs), split=True)
            pe.wait_ge(S("x3_squared"), 1)
            sums(bank(4, 0, T), C("ones"), hC, KD).then_inc(S("x3_summed"), 1)
            pe.wait_ge(S("x3_normed"), 1)
            for n in range(8):
                t, g = n // 4, n % 4
                if n >= 2:
                    pe.wait_ge(S("out_copied"), n - 1)
                for k in range(4):
                    last = transposed(bank(6 + n % 2, k * P, P), hL[:, 4 * g + k, t * P:(t + 1) * P])
                last.then_inc(S("out_transposed"), 1)

        @block.scalar
        def _(act):
            A = nc.scalar.activation
            roots = 0

            def copy(out, in_, scale=1.0):
                return A(out, in_, ACT.Copy, scale=scale)

            def job_done(name, i, job):
                act.wait_ge(S("chunks_multiplied"), st.done(name, i, job))

            def split_hi(g, i=0, n=0):
                s = g % SLOTS
                act.wait_ge(S(f"slot_loaded{s}"), i * (4 * n) + 16 * (g // SLOTS + 1))
                act.wait_ge(S("chunks_multiplied"), i * n + (g - 1 + SLOTS))
                chunk, hi = chunk_and_part(g, s, ws[0][g % 2][:, :])
                copy(hi, chunk).then_inc(S("weights_rounded"), 1)

            def rsqrt(v):
                nonlocal roots
                roots += 1
                act.wait_ge(S("variance_ready"), roots)
                A(v, v, ACT.Ln)
                act.drain()
                A(v, v, ACT.Exp, scale=-0.5).then_inc(S("rsqrt_done"), 1)

            def ada_copy_rows(name, i, job, rows):
                s = job % 2
                job_done(name, i, job)
                copy(rows[:, s, :], bank(2 * s)).then_inc(S("ada_rows_copied"), 1)

            def ada_keep(s, n, tile):
                act.wait_ge(S("ada_folded"), n)
                copy(ada[:, tile, :], bank(2 * s + 1, 0, 8).rearrange("p (a b) -> p a b", a=4)
                     ).then_inc(S(f"set_read{s}"), 1)

            def ada_late(n):
                if n < ADA_LATE:
                    ada_copy_rows("ada_late", 0, n, shared)
                if n:
                    ada_keep((n - 1) % 2, 8 + n, slice(28 + 4 * n, 32 + 4 * n))

            act.wait_ge(S("vectors_copied"), 1)
            A(ctmp[:, :], V("c", 0, 32), ACT.Exp, scale=-1.0).then_inc(S("c_exp"), 1)
            for n in range(16):
                t, g = n // 4, n % 4
                act.wait_ge(S("x_in_psum"), n + 1)
                dst = xT0 if t < 2 else cT0
                copy(dst[:, 4 * g:4 * g + 4, (t % 2) * P:(t % 2 + 1) * P],
                     bank(4 + n % 2).rearrange("p (a b) -> p a b", a=4)).then_inc(S("x_transposed"), 1)
            act.drain()
            A(hL[:, :, :], xT0, ACT.Square).then_inc(S("x_squared"), 1)
            A(hC[:, :, :], cT0, ACT.Square).then_inc(S("x_squared"), 1)
            rsqrt(rstd[:, 0, 0:T])
            rsqrt(rstd[:, 1, 0:T])
            with act.Fori(0, st.iters("ada_early")) as i:
                for job in range(2):
                    ada_copy_rows("ada_early", i, job, rows_early)
                for job in range(2):
                    ada_keep(job, i * 2 + (job + 1), bass.ds(i * 8 + 4 * job, 4))
            act.wait_ge(S("h_scaled"), 2)
            act.wait_ge(S("amod_ready"), 1)
            for n, h in enumerate((hL, hC)):
                for k in range(KD):
                    last = A(h[:, k, :], h[:, k, :], ACT.Identity, bias=ada[:, k, n:n + 1],
                             scale=amod[:, n, k:k + 1])
                last.then_inc(S("h_ready"), 1)

            def feature_tiles(dst, s, scale=1.0, n=4, m=P):
                return copy(dst, set_of(s)[0:m, 0:n * T].rearrange("p (a b) -> p a b", a=n), scale)

            act.wait_ge(S("x_spilled"), 16)
            job_done("gla_in", 0, 0)
            for s in range(2):
                feature_tiles(gk[:, :, s, :], s).then_inc(S(f"set_read{s}"), 1)
            for job in (1, 2):
                job_done("gla_in", 0, job)
                for s in range(2):
                    copy(gv[:, 2 * s:2 * s + 2, (job - 1) * 512:job * 512],
                         set_of(s).rearrange("p (a b) -> p a b", a=2)).then_inc(S(f"set_read{s}"), 1)
            job_done("gla_in", 0, 3)
            for s in range(2):
                copy(ga[:, s * T:(s + 1) * T], set_of(s)[0:32, 0:T]).then_inc(S(f"set_read{s}"), 1)
            job_done("gla_in", 0, 4)
            feature_tiles(gq, 0, 0.125).then_inc(S("set_read0"), 1)
            for d in range(2):
                if d:
                    act.wait_ge(S("gates_summed"), 1)
                for p in range(4):
                    n = 4 * d + p
                    act.wait_ge(S("z_ready"), n + 1)
                    A(zb[:, p, :], bank(4 + n % 4), ACT.Identity, bias=V(("b_a_f", "b_a_b")[d], p)
                      ).then_inc(S("z_read"), 1)
                act.drain()
                A(ztmp, area(KC, 2048), ACT.Abs)
                act.drain()
                A(ztmp, ztmp, ACT.Exp, scale=-1.0)
                act.drain()
                A(ztmp, ztmp, ACT.Ln, bias=1.0).then_inc(S("z_log"), 1)
            for job in range(2):
                job_done("dk_in", 0, job)
                for s in range(2):
                    feature_tiles(dk[:, 4 * job:4 * job + 4, s, :], s).then_inc(S(f"set_read{s}"), 1)

            def ctx_decay(n):
                p, d = n // 2, n % 2
                if n >= 2:
                    act.wait_ge(S("ctx_keys_transposed"), n - 1)
                if d == 0:
                    A(kst[:, 0, 0, :], bufs[0][:, p, 1, 1:257], ACT.Exp, scale=-1 / TAU,
                      bias=refs[:, 0, 2 * p + 1, 16:17]).then_inc(S("ctx_decay"), 1)
                else:
                    A(kst[:, 1, 0, :], bufs[1][:, p, 1, 0:256], ACT.Exp, scale=1 / TAU).then_inc(S("ctx_decay"), 1)

            act.wait_ge(S("refs_ready"), 2)
            ctx_decay(0)
            for n in range(8):
                if n < 7:
                    ctx_decay(n + 1)
                act.wait_ge(S("ctx_keys_transposed"), n + 1)
                if n >= 2:
                    act.wait_ge(S("states_ready"), n - 1)
                copy(kst[:, n % 2, 1, :], bank(6, 0, T)).then_inc(S("ctx_keys_copied"), 1)
            for job in range(2):
                job_done("dv_in", 0, job)
                for s in range(2):
                    copy(dv[:, 2 * s:2 * s + 2, job * 512:(job + 1) * 512],
                         set_of(s).rearrange("p (a b) -> p a b", a=2)).then_inc(S(f"set_read{s}"), 1)

            def dq_tiles(job):
                s = job % 2
                job_done("dq_in", 0, job)
                dst = (dq, gr)[job // 2]
                feature_tiles(dst[:, 4 * s:4 * s + 4, :], s).then_inc(S(f"set_read{s}"), 1)

            def gla_prepare(p, beside):
                if p == 0:
                    act.wait_ge(S("states_ready"), 8)
                    act.wait_ge(S("kc_cleared"), 1)
                else:
                    act.wait_ge(S("gla_out_ready"), p)
                A(qx[:, 0, :], bufs[0][:, p, 0, 1:257], ACT.Exp, scale=1 / TAU)
                A(qx[:, 1, :], bufs[1][:, p, 0, 0:256], ACT.Exp, scale=-1 / TAU, bias=small[:, 8 + p:9 + p])
                act.wait_ge(S("q_gaps"), p + 1)
                A(qx[:, 2:4, :], qx[:, 2:4, :], ACT.Exp, scale=1 / TAU).then_inc(S("q_decay"), 1)
                for d in range(2):
                    for b in BLOCKS[d]:
                        keys, tok = kc(d, b)
                        lo, hi = key_range(d, b)
                        if d == 0:
                            src, sc, ref = bufs[0][:, p, 0, 1 + lo:1 + hi], -1 / TAU, refs[:, 0, 2 * p, b:b + 1]
                        else:
                            src, sc, ref = bufs[1][:, p, 0, lo:hi], 1 / TAU, refs[:, 1, 2 * p, b + 1:b + 2]
                        A(keys[:, lo - tok:hi - tok], src, ACT.Exp, scale=sc, bias=ref).then_inc(S("k_decay"), 1)
                        if b == 7:
                            beside(d)
                for e in range(4):
                    act.wait_ge(S("pair_gaps"), 4 * p + e + 1)
                    A(pd[e % 2], pd[e % 2], ACT.Exp, scale=1 / TAU).then_inc(S("pair_decay"), 1)
                    if e:
                        beside(1 + e)
                beside(5)

            def gla_finish(p):
                act.wait_ge(S("gla_out_ready"), p + 1)
                A(rstd[:, 1, :].rearrange("p (a b) -> p a b", a=2), two_banks(T), ACT.Square
                  ).then_inc(S("gla_squared"), 1)
                rsqrt(rstd[:, 0, :])

            for pair in range(4):
                def beside(n, pair=pair):
                    if pair >= 2:
                        ada_late(6 * (pair - 2) + n)
                    elif n in (3, 5):
                        dq_tiles(2 * pair + n // 4)
                gla_prepare(pair, beside)
                gla_finish(pair)
            A(ztmp, area(7168, 2048), ACT.Exp, scale=-1.0).then_inc(S("r_exp"), 1)

            for g in range(12):
                src = dq[:, 2 * g:2 * g + 2, :] if g < 4 else dk[:, g - 4, :, :]
                if g % 3 == 0:
                    ada_late(12 + g // 3)
                if g >= 2:
                    act.wait_ge(S("qk_summed"), g - 1)
                A(dsq[:, g % 2, :].rearrange("p (a b) -> p a b", a=2), src, ACT.Square).then_inc(S("qk_squared"), 1)
                rsqrt(rstd[:, g % 2, :])
            ada_late(ADA_LATE)
            act.wait_ge(S("lambda_summed"), 1)
            A(small[:, 2:4].unsqueeze(2), two_banks(1), ACT.Exp).then_inc(S("lambda_exps"), 1)

            def diff_exp(n):
                act.wait_ge(S("diff_max_ready"), n + 1)
                if n >= 8:
                    act.wait_ge(S("diff_probs_transposed"), (n - 8) // 2 + 1)
                A(dp[:, n % 8, :], bank(2 + n % 4), ACT.Exp, scale=0.125, bias=small[:, 24 + n % 8:25 + n % 8],
                  accum_out=small[:, 32 + n % 8:33 + n % 8]).then_inc(S("diff_exps"), 1)

            def diff_copy(u):
                h, qt = u // 2, u % 2
                act.wait_ge(S("diff_probs_transposed"), u + 1)
                if h >= 2 and qt == 0:
                    act.wait_ge(S("diff_pv_done"), h - 1)
                copy(daT[h % 2][:, :, qt * P:(qt + 1) * P], bank((6, 1)[u % 2]).rearrange("p (a b) -> p a b", a=4)
                     ).then_inc(S("diff_probs_copied"), 1)

            for u in range(16 + 3):
                if u < 16:
                    diff_exp(2 * u)
                    diff_exp(2 * u + 1)
                if 2 <= u < 16 + 2:
                    diff_copy(u - 2)
                if u >= 3 and u % 2 == 0:
                    h = (u - 3) // 2
                    act.wait_ge(S("diff_pv_done"), h + 1)
                    copy(dq[:, h, :], bank((7, 0)[h % 2], 0, T)).then_inc(S("diff_out_copied"), 1)
            act.drain()
            for g in range(4):
                if g >= 2:
                    act.wait_ge(S("diff_summed"), g - 1)
                A(dsq[:, g % 2, :].rearrange("p (a b) -> p a b", a=2), dq[:, 2 * g:2 * g + 2, :], ACT.Square
                  ).then_inc(S("diff_squared"), 1)
                rsqrt(rstd[:, g % 2, :])

            with act.Fori(0, st.iters("merge")) as i:
                act.wait_ge(S("merged"), i + 1)
                for b in range(2):
                    job_done("merge", i, 2 * b)
                    for m in range(4):
                        f = i * 4 + (16 * b + m)
                        last = A(gsb[b][:, m, :], set_of(0)[:, m * T:(m + 1) * T], ACT.Exp, scale=-1.0,
                                 bias=nbgate[:, bass.ds(f, 1)])
                    last.then_inc(S("gate_exps"), 1)
            for s in range(2):
                act.wait_ge(S(f"set_read{s}"), st.set_uses("up0", 0, s, s))
            A(hC[:, :, :], x1, ACT.Square).then_inc(S("x1_squared"), 1)
            rsqrt(rstd[:, 0, 0:T])
            act.wait_ge(S("h2_scaled"), 1)
            for k in range(KD):
                last = A(hL[:, k, :], hL[:, k, :], ACT.Identity, bias=ada[:, 48 + k, 0:1], scale=amod[:, 2, k:k + 1])
            last.then_inc(S("h2_modulated"), 1)

            for j in range(4):
                split_hi(st.index("up0", j))

            def taps(part, i):
                name, f0, n = f"up{part}", (0, KFA)[part], 8
                g0 = st.index(name)

                def centre(s):
                    job_done(name, i, s)
                    for m in range(4):
                        f = i * 4 + (KF * s + f0 + m)
                        last = A(ftap[s][:, m, :], set_of(s)[:, m * T:(m + 1) * T], ACT.Identity,
                                 bias=vec[:, bass.ds(f + VROW["conv_b"], 1)],
                                 scale=vec[:, bass.ds(f + (VROW["conv_w"] + 2 * KF), 1)])
                    last.then_inc(S("taps_centred"), 1)

                for j in (4, 5):
                    split_hi(g0 + j, i, n)
                act.wait_ge(S("ffn_hidden"), i + (f0 // 4 + 1))
                centre(0)
                for j in (6, 7):
                    split_hi(g0 + j, i, n)
                act.wait_ge(S("set_read0"), st.set_uses(name, i, 1, 0))
                A(fexp, ftap[0], ACT.Exp, scale=-1.0).then_inc(S("ffn_exps"), 1)
                for j in (8, 9):
                    split_hi(g0 + j, i, n)
                centre(1)
                for j in (10, 11):
                    split_hi(g0 + j, i, n)

            for part in range(2):
                with act.Fori(0, st.iters(f"up{part}")) as i:
                    taps(part, i)
                if part == 0:
                    with act.Fori(0, 2) as i:
                        for j in range(4, 16):
                            split_hi(st.index("down0") + j, i, 12)
                else:
                    for j in range(4, 20):
                        split_hi(st.index("down1", j))

            for n in range(8):
                t, g = n // 4, n % 4
                act.wait_ge(S("mem_in_psum"), n + 1)
                copy(hC[:, 4 * g:4 * g + 4, t * P:(t + 1) * P],
                     bank(4 + n % 2).rearrange("p (a b) -> p a b", a=4)).then_inc(S("mem_transposed"), 1)
            act.drain()
            A(sq2, hC[:, :, :], ACT.Square).then_inc(S("mem_squared"), 1)
            for s in range(2):
                act.wait_ge(S(f"set_read{s}"), st.set_uses("mem", 0, s, s))
            A(hL[:, :, :], x1, ACT.Square).then_inc(S("x2_squared"), 1)
            rsqrt(rstd[:, 0, 0:T])
            rsqrt(rstd[:, 1, 0:T])
            for j in range(2):
                split_hi(st.index("in2", j))
            job_done("mem", 0, 1)
            feature_tiles(km, 0, ).then_inc(S("set_read0"), 1)
            copy(vm, set_of(1).rearrange("p (a b) -> p a b", a=2)).then_inc(S("set_read1"), 1)
            where = {"z0": zT[:, 0:4, :], "z1": zT[:, 4:8, :], "z2": zT[:, 8:12, :], "z3": zT[:, 12:16, :]}

            def in2_read(n, name):
                s = n % 2
                job_done("in2", 0, n)
                if name in ("cq", "ckv"):
                    A(rtmpsq[s], set_of(s).rearrange("p (a b) -> p a b", a=4), ACT.Square
                      ).then_inc(S("lowrank_squared"), 1)
                    last = feature_tiles((cq, ckv)[s], s)
                elif name == "krope":
                    last = copy(kpe, set_of(s)[:, 0:T])
                elif name in ("qn0", "qn1"):
                    last = feature_tiles(qn[0:96, 4 * (name == "qn1"):4 * (name == "qn1") + 4, :], s, NSA_SCALE, 4, 96)
                elif name in ("kc", "ks", "kw"):
                    last = feature_tiles({"kc": kcT, "ks": ksT, "kw": kwT}[name][0:96, :, :], s, 1.0, 2, 96)
                elif name == "vc":
                    last = copy(vcT, set_of(s)[:, 0:T])
                elif name in ("vs", "vw"):
                    last = copy({"vs": vs, "vw": vw}[name],
                                set_of(s).rearrange("p (a b) -> p a b", a=2)[:, :, 0:P])
                elif name == "gn":
                    A(gn[0:12, :], set_of(s)[0:12, 0:T], ACT.Exp, scale=-1.0).then_inc(S(f"set_read{s}"), 1)
                    return
                elif name == "qm":
                    last = feature_tiles(qm, s, MEM_SCALE)
                else:
                    last = feature_tiles(where[name], s)
                last.then_inc(S(f"set_read{s}"), 1)
                if name == "ckv":
                    rsqrt(rstd[:, 0, 0:T])
                    rsqrt(rstd[:, 1, 0:T])

            last_chunk = st.info["in2"][1] - 1
            at = 2
            for n, (name, _, _) in enumerate(IN2):
                while at <= min(st.first("in2", n + 1) + 1, last_chunk):
                    split_hi(st.index("in2", at))
                    at += 1
                in2_read(n, name)
            act.drain()
            A(zexp, larea(0, KD * T), ACT.Exp, scale=-1.0).then_inc(S("z_exps"), 1)
            for n in range(4):
                s = n % 2
                job_done("uq", 0, n)
                copy(mqn[:, 2 * n:2 * n + 2, :], set_of(s)[:, 0:2 * T].rearrange("p (a b) -> p a b", a=2), MLA_SCALE)
                copy(mqr[:, n, :], set_of(s)[:, 2 * T:3 * T], MLA_SCALE).then_inc(S(f"set_read{s}"), 1)
            for n in range(4):
                s = n % 2
                job_done("ukv", 0, n)
                copy(mkn[:, 2 * n:2 * n + 2, :], set_of(s)[:, 0:2 * T].rearrange("p (a b) -> p a b", a=2))
                copy(mv[:, :, 256 * n:256 * (n + 1)], set_of(s)[:, 2 * T:4 * T].rearrange("p (a b) -> p a b", a=2)
                     ).then_inc(S(f"set_read{s}"), 1)
            act.wait_ge(S("cmp_bounded"), 1)
            hk = hexp[0:96, 0:32].rearrange("p (a b) -> p a b", a=2)[:, :, 0:NCMP]
            A(hk, hk, ACT.Exp, scale=-1.0)
            A(hexp[:, 32:32 + NCMP], hexp[:, 32:32 + NCMP], ACT.Exp, scale=-1.0).then_inc(S("cmp_exps"), 1)

            def exp2(u):
                kind, o, h = OUTS[u // 2]
                n = keys_seen(kind, u % 2)
                act.wait_ge(S("max2_ready"), u + 1)
                if u >= 4:
                    act.wait_ge(S("probs2_transposed"), u - 3)
                src = bank(2 + u % 4, 0, n) if kind == "mem" else ssb[:, u % 4, 0:n]
                A(prob[:, u % 4, 0:n], src, ACT.Exp, bias=small[:, 36 + u % 4:37 + u % 4],
                  accum_out=small[:, 40 + u % 4:41 + u % 4]).then_inc(S("exps2"), 1)

            def copy2(u):
                kind, o, h = OUTS[u // 2]
                qt = u % 2
                n = keys_seen(kind, qt)
                act.wait_ge(S("probs2_transposed"), u + 1)
                if qt == 0 and u >= 4:
                    act.wait_ge(S("out2_ready"), u // 2 - 1)
                k, w = (n + P - 1) // P, min(n, P)
                copy(aT[(u // 2) % 2][0:w, 0:k, qt * P:(qt + 1) * P],
                     bank((6, 1)[u % 2], 0, k * P)[0:w, :].rearrange("p (a b) -> p a b", a=k)
                     ).then_inc(S("probs2_copied"), 1)

            units = 2 * len(OUTS)
            for u in range(units + 3):
                if u < units:
                    exp2(u)
                if 2 <= u < units + 2:
                    copy2(u - 2)
                if u >= 3 and u % 2 == 0:
                    act.wait_ge(S("out2_ready"), (u - 3) // 2 + 1)
                    copy(obuf[:, (u - 3) // 2, :], bank((7, 0)[(u - 3) // 2 % 2], 0, T)).then_inc(S("out2_copied"), 1)
            act.wait_ge(S("mixers_gated"), 1)
            for j in range(16):
                split_hi(st.index("out2", j))
            for s in range(2):
                act.wait_ge(S(f"set_read{s}"), st.set_uses("out2", 0, 4, s))
            A(hC[:, :, :], x1, ACT.Square).then_inc(S("x3_squared"), 1)
            rsqrt(rstd[:, 0, 0:T])
            for n in range(8):
                t, g = n // 4, n % 4
                act.wait_ge(S("out_transposed"), n + 1)
                copy(onat[:, t, 512 * g:512 * (g + 1)], bank(6 + n % 2)).then_inc(S("out_copied"), 1)

        @block.vector
        def _(dve):
            v = nc.vector
            tt, ts, stt = v.tensor_tensor, v.tensor_scalar, v.scalar_tensor_tensor
            roots = 0

            def variance(out, sums, n):
                ts(out, sums, 1.0 / n, EPS, ALU.mult, ALU.add).then_inc(S("variance_ready"), 1)

            def rsqrt_wait():
                nonlocal roots
                roots += 1
                dve.wait_ge(S("rsqrt_done"), roots)

            def split_lo(g, i=0, n=0):
                dve.wait_ge(S("weights_rounded"), i * n + st.split_count(g) + 1)
                chunk, hi = chunk_and_part(g, g % SLOTS, ws[0][g % 2][:, :].bitcast(F32))
                _, lo = chunk_and_part(g, g % SLOTS, ws[1][g % 2][:, :])
                tt(lo, chunk, hi, ALU.subtract).then_inc(S("weights_split"), 1)

            def split_values(parts, x):
                v.tensor_copy(parts[0], x)
                dve.drain()
                return tt(parts[1], x, parts[0].bitcast(F32), ALU.subtract)

            def plus_one_over(x):
                ts(x, x, 1.0, None, ALU.add)
                dve.drain()
                v.reciprocal(x, x)
                dve.drain()

            for name in ("merged", "ffn_hidden"):
                dve.sem_inc(S(name), 1)
            def modulation_bias(a, b):
                tt(ada[:, a:b, :], ada[:, a:b, :], V("b_ada", a, b - a).unsqueeze(2).to_broadcast([P, b - a, 2]), ALU.add)
                dve.drain()

            dve.wait_ge(S("vectors_transposed"), 1)
            v.tensor_copy(vec[:, 0:512], bank(6))
            v.tensor_copy(vec[:, 512:NVEC], bank(7, 0, NVEC - 512)).then_inc(S("vectors_copied"), 1)
            dve.drain()
            ts(nbgate[:, :], V("b_gate", 0, 32), -1.0, None, ALU.mult)
            ts(small[:, 5:6], V("diff_onorm_w"), 1.0 - LAM_INIT, None, ALU.mult)
            tt(small[:, 0:1], V("lambda_q1"), V("lambda_k1"), ALU.mult).then_inc(S("lambda_products"), 1)
            dve.wait_ge(S("c_exp"), 1)
            plus_one_over(ctmp[:, :])
            dve.wait_ge(S("csil_cleared"), 1)
            tt(csil[:, :, 0:2].rearrange("p k w -> p w k"), V("c", 0, 32).rearrange("p (w k) -> p w k", w=2),
               ctmp[:, :].rearrange("p (w k) -> p w k", w=2), ALU.mult).then_inc(S("c_activated"), 1)
            for n in range(2):
                dve.wait_ge(S("x_summed"), n + 1)
                variance(rstd[:, n, 0:T], bank(6 + n, 0, T), D)
            for n, (h, x) in enumerate(((hL, xT0), (hC, cT0))):
                rsqrt_wait()
                tt(h[:, :, :], x, rstd[:, n, 0:T].unsqueeze(1).to_broadcast([P, KD, T]), ALU.mult
                   ).then_inc(S("h_scaled"), 1)
            for s in range(2):
                dve.wait_ge(S(f"set_read{s}"), st.set_uses("gla_in", 0, 0, s))
            modulation_bias(0, 32)
            for n in range(2):
                last = stt(amod[:, n, :], ada[:, 16:32, n], 1.0, V("norm1_w", 0, 16), ALU.add, ALU.mult)
            last.then_inc(S("amod_ready"), 1)

            for d in range(2):
                dve.wait_ge(S("z_read"), 4 * (d + 1))
                v.memset(bufs[d][:, :, :, 0:1], 0.0)
                dve.wait_ge(S("z_log"), d + 1)
                stt(area(KC, 2048), area(KC, 2048), 0.0, ztmp, ALU.min, ALU.subtract)
                dve.drain()
                for p in range(4):
                    for half in range(2):
                        last = v.tensor_tensor_scan(bufs[d][:, p, half, 1:257], C("ones")[:, 0:1].to_broadcast([P, T]),
                                                    zb[:, p, half * T:(half + 1) * T], 0.0, ALU.mult, ALU.add)
                last.then_inc(S("gates_summed"), 1)
                dve.drain()
                if d:
                    ts(small[:, 8:12], bufs[1][:, :, 0, 256], 1 / TAU, None, ALU.mult)
                ts(refs[:, d, :, :], bufs[d].rearrange("p a b c -> p (a b) c")[:, :, 0:257:16], (1 - 2 * d) / TAU, None,
                   ALU.mult).then_inc(S("refs_ready"), 1)

            def scale_ctx_keys(n):
                dve.wait_ge(S("ctx_decay"), n + 1)
                tt(kst[:, n % 2, 0, :], kst[:, n % 2, 0, :], gk[:, n // 2, 1, :], ALU.mult
                   ).then_inc(S("ctx_keys_scaled"), 1)

            scale_ctx_keys(0)
            for n in range(8):
                if n < 7:
                    scale_ctx_keys(n + 1)
                dve.wait_ge(S("states_ready"), n + 1)
                v.tensor_copy(smem[:, n, :], bank(7, 0, P)).then_inc(S("states_copied"), 1)

            def blocks(flat):
                return flat.rearrange("p (b i) -> p b i", i=GC)

            def gla_prepare(p):
                if p == 0:
                    dve.wait_ge(S("states_ready"), 8)
                else:
                    dve.wait_ge(S("gla_out_ready"), p)
                f, b = bufs[0][:, p, 0, :], bufs[1][:, p, 0, :]
                tt(blocks(qx[:, 2, :]), blocks(f[:, 1:257]),
                   f[:, 0:256:GC].unsqueeze(2).to_broadcast([P, NB, GC]), ALU.subtract)
                tt(blocks(qx[:, 3, :]), b[:, GC:257:GC].unsqueeze(2).to_broadcast([P, NB, GC]),
                   blocks(b[:, 0:256]), ALU.subtract).then_inc(S("q_gaps"), 1)
                dve.wait_ge(S("q_decay"), p + 1)
                tt(qx, qx, gq[:, p, :].unsqueeze(1).to_broadcast([P, 4, T]), ALU.mult)
                n = 0
                for d in range(2):
                    for blk in BLOCKS[d]:
                        keys, tok = kc(d, blk)
                        lo, hi = key_range(d, blk)
                        n += 1
                        dve.wait_ge(S("k_decay"), 30 * p + n)
                        last = tt(keys[:, lo - tok:hi - tok], keys[:, lo - tok:hi - tok], gk[:, p, 0, lo:hi], ALU.mult)
                last.then_inc(S("gla_operands_ready"), 1)
                if p == 0:
                    dve.wait_ge(S("chunks_multiplied"), st.done("dv_in", 0, 1))

                def gaps(e):
                    d, t = e // 2, e % 2
                    if 4 * p + e >= 2:
                        dve.wait_ge(S("gla_diag_summed"), 4 * p + e - 1)
                    src = f[:, 1 + t * P:1 + (t + 1) * P] if d == 0 else b[:, t * P:(t + 1) * P]
                    i = src.rearrange("p (b i) -> p i b", i=GC).unsqueeze(3).to_broadcast([P, GC, 8, GC])
                    j = blocks(src).unsqueeze(1).to_broadcast([P, GC, 8, GC])
                    tt(pd[e % 2], i if d == 0 else j, j if d == 0 else i, ALU.subtract)
                    dve.drain()
                    flat = carea(2048 * (e % 2), 2048)
                    ts(flat, flat, 0.0, None, ALU.min).then_inc(S("pair_gaps"), 1)

                def pairs(e):
                    t = e % 2
                    dve.wait_ge(S("pair_decay"), 4 * p + e + 1)
                    k = blocks(gk[:, p, 0, t * P:(t + 1) * P]).unsqueeze(1).to_broadcast([P, GC, 8, GC])
                    q = gq[:, p, t * P:(t + 1) * P].rearrange("p (b i) -> p i b", i=GC).unsqueeze(3
                                                             ).to_broadcast([P, GC, 8, GC])
                    tt(pd[e % 2], pd[e % 2], k, ALU.mult)
                    dve.drain()
                    tt(pd[e % 2], pd[e % 2], q, ALU.mult).then_inc(S("gla_diag_ready"), 1)

                gaps(0)
                gaps(1)
                for e in range(4):
                    pairs(e)
                    if e < 2:
                        gaps(e + 2)

            def gla_finish(p):
                dve.wait_ge(S("gla_blocks_done"), p + 1)
                dve.wait_ge(S("gla_diag_summed"), 4 * p + 4)
                if p:
                    dve.wait_ge(S("gla_out_ready"), p)
                for h in range(2):
                    parts = []
                    for d, mask in enumerate(("mask_f", "mask_b")):
                        diag = bank(6, 64 * d, 64).rearrange("p (t i h) -> p t i h", t=2, i=GC)[:, :, :, h]
                        part = rstd[:, 1, d * T:(d + 1) * T].rearrange("p (t b i) -> p t b i", t=2, b=8)
                        tt(part, diag.unsqueeze(2).to_broadcast([P, 2, 8, GC]),
                           C(mask).rearrange("p (t b i) -> p t b i", t=2, b=8), ALU.mult)
                        parts.append(rstd[:, 1, d * T:(d + 1) * T])
                    v.tensor_copy(asum[:, h, :], bank(4 + h))
                    dve.drain()
                    quads = asum[:, h, :].rearrange("p (a b) -> p a b", a=4)[:, 0:4:3, :]
                    for d in range(2):
                        last = tt(quads, quads, parts[d].rearrange("p (a b) -> p a b", a=2), ALU.add)
                        if d == 0:
                            dve.drain()
                    last.then_inc(S("gla_scores_ready"), 1)
                    dve.drain()
                dve.wait_ge(S("gla_summed"), p + 1)
                variance(rstd[:, 0, :], bank(4), P)
                rsqrt_wait()
                stt(yg[:, 2 * p:2 * p + 2, :], two_banks(T), V("gla_onorm_w"),
                    rstd[:, 0, :].rearrange("p (a b) -> p a b", a=2), ALU.mult, ALU.mult).then_inc(S("gla_normed"), 1)

            for p in range(4):
                gla_prepare(p)
                gla_finish(p)
            dve.wait_ge(S("r_exp"), 1)
            plus_one_over(ztmp)
            grf, ygf = area(7168, 2048), area(1024, 2048)
            tt(grf, grf, ztmp, ALU.mult)
            dve.drain()
            tt(ygf, ygf, grf, ALU.mult).then_inc(S("gla_gated"), 1)

            for g in range(12):
                n = 512 if g < 4 else T
                src = (dq[:, 2 * g:2 * g + 2, :] if g < 4 else dk[:, g - 4, :, :]).rearrange("p a b -> p (a b)")
                rs = rstd[:, g % 2, :]
                dve.wait_ge(S("qk_summed"), g + 1)
                variance(rs, bank(4 + g % 2), 64)
                rsqrt_wait()
                stt(src, src, V("diff_qnorm_w" if g < 4 else "diff_knorm_w"), rs, ALU.mult, ALU.mult
                    ).then_inc(S("qk_normed"), 1)
                dve.drain()
                a = n // T

                def reps(flat):
                    return flat.rearrange("p (a b) -> p a b", a=a)

                def table(name):
                    return C(name).unsqueeze(1).to_broadcast([P, a, T])

                tt(reps(dmul[:, g % 2, 0:n]), reps(src[:, 0:n]), table("cos2d"), ALU.mult)
                dve.wait_ge(S("qk_rotated"), g + 1)
                tt(reps(rs[:, 0:n]), reps(bank(6 + g % 2, 0, n)), table("sin2d"), ALU.mult)
                dve.drain()
                tt(src[:, 0:n], dmul[:, g % 2, 0:n], rs[:, 0:n], ALU.add).then_inc(S("qk_done"), 1)
            dve.wait_ge(S("lambda_exps"), 1)
            tt(small[:, 4:5], small[:, 3:4], small[:, 2:3], ALU.subtract)
            dve.drain()
            ts(small[:, 4:5], small[:, 4:5], -LAM_INIT, None, ALU.add).then_inc(S("lambda_done"), 1)
            dve.drain()

            def diff_max(n):
                dve.wait_ge(S("diff_scores_ready"), n + 1)
                if n >= 8:
                    dve.wait_ge(S("diff_exps"), n - 7)
                v.reduce_max(small[:, 16 + n % 8:17 + n % 8], bank(2 + n % 4), AXX)
                dve.drain()
                ts(small[:, 24 + n % 8:25 + n % 8], small[:, 16 + n % 8:17 + n % 8], -0.125, None, ALU.mult
                   ).then_inc(S("diff_max_ready"), 1)

            def diff_combine(u):
                a = 2 * (u % 4)
                dve.wait_ge(S("diff_exps"), 2 * u + 2)
                v.reciprocal(small[:, 40 + a:42 + a], small[:, 32 + a:34 + a])
                dve.drain()
                tt(small[:, 41 + a:42 + a], small[:, 41 + a:42 + a], small[:, 4:5], ALU.mult)
                ts(dp[:, a, :], dp[:, a, :], small[:, 40 + a:41 + a], None, ALU.mult)
                dve.drain()
                stt(dp[:, a, :], dp[:, a + 1, :], small[:, 41 + a:42 + a], dp[:, a, :], ALU.mult, ALU.add
                    ).then_inc(S("diff_probs_ready"), 1)

            for u in range(16):
                diff_max(2 * u)
                diff_max(2 * u + 1)
                if u:
                    diff_combine(u - 1)
            diff_combine(15)
            for g in range(4):
                rs = rstd[:, g % 2, :]
                flat = dq[:, 2 * g:2 * g + 2, :].rearrange("p a b -> p (a b)")
                dve.wait_ge(S("diff_summed"), g + 1)
                variance(rs, bank(4 + g % 2), P)
                rsqrt_wait()
                stt(flat, flat, small[:, 5:6], rs, ALU.mult, ALU.mult).then_inc(S("diff_normed"), 1)

            with dve.Fori(0, st.iters("merge")) as i:
                for b in range(2):
                    dve.wait_ge(S("gate_exps"), i * 2 + (b + 1))
                    ts(gsb[b], gsb[b], 1.0, None, ALU.add).then_inc(S("set_read0"), 1)
                    dve.drain()
                    v.reciprocal(gsb[b], gsb[b])
                    dve.drain()
                    dve.wait_ge(S("chunks_multiplied"), st.done("merge", i, 2 * b + 1))
                    dst = mT[:, bass.ds(i * 4, 4), :]
                    proj = set_of(1).rearrange("p (a b) -> p a b", a=4)
                    if b == 0:
                        tt(dst, gsb[0], proj, ALU.mult).then_inc(S("set_read1"), 1)
                    else:
                        tt(gsb[1], gsb[1], proj, ALU.mult).then_inc(S("set_read1"), 1)
                        dve.drain()
                        tt(dst, dst, gsb[1], ALU.add).then_inc(S("merged"), 1)
            modulation_bias(32, 96)
            dve.wait_ge(S("x_back"), 16)
            with dve.Fori(0, st.iters("out")) as i:
                for job in range(2):
                    dve.wait_ge(S("chunks_multiplied"), st.done("out", i, job))
                    for m in range(4):
                        f = i * 8 + (4 * job + m)
                        last = stt(x1[:, bass.ds(f, 1), :].rearrange("p a b -> p (a b)"), set_of(job)[:, m * T:(m + 1) * T],
                                   ada[:, bass.ds(f + 32, 1), 0], x0[:, bass.ds(f, 1), :].rearrange("p a b -> p (a b)"),
                                   ALU.mult, ALU.add)
                    last.then_inc(S(f"set_read{job}"), 1)
            stt(amod[:, 2, :], ada[:, 64:80, 0], 1.0, V("norm2_w", 0, 16), ALU.add, ALU.mult)
            dve.wait_ge(S("x1_summed"), 1)
            variance(rstd[:, 0, 0:T], bank(4, 0, T), D)
            rsqrt_wait()
            tt(hL[:, :, :], x1, rstd[:, 0, 0:T].unsqueeze(1).to_broadcast([P, KD, T]), ALU.mult
               ).then_inc(S("h2_scaled"), 1)

            dve.wait_ge(S("h2_modulated"), 1)
            split_values([h[:, :, :] for h in hs], hL[:, :, :]).then_inc(S("h2_ready"), 1)
            for j in range(4):
                split_lo(st.index("up0", j))

            def hidden(part, i):
                name, f0, n = f"up{part}", (0, KFA)[part], 8
                g0 = st.index(name)

                def outer_taps(s):
                    dve.wait_ge(S("taps_centred"), i * 2 + (f0 // 2 + s + 1))
                    for tap in (0, 2):
                        for m in range(4):
                            f = i * 4 + (KF * s + f0 + m)
                            w = vec[:, bass.ds(f + (VROW["conv_w"] + KF * 2 * tap), 1)]
                            u = set_of(s)[:, m * T:(m + 1) * T]
                            y = ftap[s][:, m, :]
                            if tap == 0:
                                last = stt(y[:, 1:T], u[:, 0:T - 1], w, y[:, 1:T], ALU.mult, ALU.add)
                            else:
                                last = stt(y[:, 0:T - 1], u[:, 1:T], w, y[:, 0:T - 1], ALU.mult, ALU.add)
                        if tap == 0:
                            dve.drain()
                    last.then_inc(S(f"set_read{s}"), 1)

                for j in (4, 5):
                    split_lo(g0 + j, i, n)
                outer_taps(0)
                for j in (6, 7):
                    split_lo(g0 + j, i, n)
                dve.wait_ge(S("ffn_exps"), i + (f0 // 4 + 1))
                plus_one_over(fexp)
                split_lo(g0 + 8, i, n)
                tt(ftap[0], ftap[0], fexp, ALU.mult)
                split_lo(g0 + 9, i, n)
                outer_taps(1)
                split_lo(g0 + 10, i, n)
                dve.drain()
                tt(ftap[0], ftap[0], ftap[1], ALU.mult)
                dve.drain()
                split_values([f[:, bass.ds(i * 4, 4), :] for f in fh], ftap[0]).then_inc(S("ffn_hidden"), 1)
                split_lo(g0 + 11, i, n)

            def add_down(name, i, job, f0):
                s = job % 2
                dve.wait_ge(S("chunks_multiplied"), st.done(name, i, job))
                for m in range(4):
                    f = i * 8 + (f0 + m)
                    x = x1[:, bass.ds(f, 1), :].rearrange("p a b -> p (a b)")
                    last = stt(x, set_of(s)[:, m * T:(m + 1) * T], ada[:, bass.ds(f + 80, 1), 0], x,
                               ALU.mult, ALU.add)
                last.then_inc(S(f"set_read{s}"), 1)

            for part in range(2):
                with dve.Fori(0, st.iters(f"up{part}")) as i:
                    hidden(part, i)
                if part == 0:
                    with dve.Fori(0, 2) as i:
                        for job in range(2):
                            for j in range(6 * job + 4, 6 * job + 10):
                                if j == 6 * job + 8:
                                    add_down("down0", i, job, 4 * job)
                                split_lo(st.index("down0") + j, i, 12)
                else:
                    for job in range(4):
                        for j in range(5 * job + 4, 5 * job + 9):
                            if j == 5 * job + 7:
                                add_down("down1", 0, job, 4 * job)
                            if j < 20:
                                split_lo(st.index("down1", j))

            def gained(out, x, gain, rs, tiles):
                for k in range(tiles):
                    last = stt(out[:, k, :], x[:, k, :], V(gain, k), rs, ALU.mult, ALU.mult)
                return last

            dve.wait_ge(S("mem_summed"), 1)
            variance(rstd[:, 0, 0:T], bank(6, 0, T), D)
            dve.wait_ge(S("x2_summed"), 1)
            variance(rstd[:, 1, 0:T], bank(7, 0, T), D)
            rsqrt_wait()
            gained(hC, hC, "mem_norm_g_2", rstd[:, 0, 0:T], KD).then_inc(S("mem_ready"), 1)
            rsqrt_wait()
            gained(hL, x1, "norm_g_2", rstd[:, 1, 0:T], KD)
            dve.drain()
            split_values([h[:, :, :] for h in hs], hL[:, :, :]).then_inc(S("h3_ready"), 1)
            dve.wait_ge(S("consts2_loaded"), 16)
            ts(causal, C("rel")[:, T:2 * T], -1e20, MASKED, ALU.is_lt, ALU.mult)
            def lowrank_norms():
                for n in range(2):
                    dve.wait_ge(S("lowrank_summed"), n + 1)
                    variance(rstd[:, n, 0:T], bank(4 + n, 0, T), 512)
                for n, (x, gain, done) in enumerate(((cq, "q_norm_g_2", "cq_normed"), (ckv, "kv_norm_g_2", "ckv_normed"))):
                    rsqrt_wait()
                    dve.wait_ge(S(f"set_read{n}"), st.set_uses("in2", 0, 2 + n, n))
                    gained(x, x, gain, rstd[:, n, 0:T], 4).then_inc(S(done), 1)

            at = 0
            for n, (name, _, _) in enumerate(IN2):
                while at < min(st.first("in2", n + 1) + 2, st.info["in2"][1]):
                    split_lo(st.index("in2", at))
                    at += 1
                if name == "ckv":
                    lowrank_norms()
            gate_job = [n for n, (name, _, _) in enumerate(IN2) if name == "gn"][0]
            dve.wait_ge(S(f"set_read{gate_job % 2}"), st.set_uses("in2", 0, gate_job, gate_job % 2) + 1)
            ts(gn[0:12, :], gn[0:12, :], 1.0, None, ALU.add)
            dve.drain()
            v.reciprocal(gn[0:12, :], gn[0:12, :]).then_inc(S("nsa_gates_ready"), 1)

            def silu_z(a, b):
                e, z = zexp[:, a * T:b * T], larea(a * T, (b - a) * T)
                plus_one_over(e)
                tt(z, z, e, ALU.mult)

            dve.wait_ge(S("z_exps"), 1)
            silu_z(0, KD // 2)
            silu_z(KD // 2, KD)
            for n in range(5):
                dve.wait_ge(S("rope_rotated"), n + 1)
                dst = mqr[:, n, :] if n < 4 else kpe
                tt(rtmp[:, n % 2, 0:T], dst, C("cos1d"), ALU.mult)
                tt(rtmp[:, n % 2, T:2 * T], bank(4 + n % 2, 0, T), C("sin1d"), ALU.mult)
                dve.drain()
                tt(dst, rtmp[:, n % 2, 0:T], rtmp[:, n % 2, T:2 * T], ALU.add).then_inc(S("rope_done"), 1)
            dve.wait_ge(S("pe_transposed"), 1)
            v.tensor_copy(peT[0:96, 0:2, :], bank(6, 0, 64)[0:96, :].rearrange("p (a b) -> p a b", a=2))
            v.tensor_copy(peT[:, 2, :], bank(6, 64, 32))
            dve.drain()
            for a in range(2):
                for h in range(3):
                    n = 96 if h < 2 else P
                    src = (kcT[0:96, h, :] if h < 2 else vcT).rearrange("p (n b) -> p b n", b=16)[:, :, a:a + NCMP]
                    dst = (kcp[0:96, h, :, :] if h < 2 else vcp)[:, 16 * a:16 * a + 16, :]
                    last = tt(dst, src, peT[0:n, h, 16 * a:16 * a + 16].unsqueeze(2).to_broadcast([n, 16, NCMP]),
                              ALU.add)
            last.then_inc(S("cmp_blocks_ready"), 1)

            def pair(flat):
                return flat.rearrange("p (a b) -> p a b", a=2)[:, :, 0:NCMP]

            dve.wait_ge(S("chunks_multiplied"), st.done("cmp", 0, 1))
            ts(pair(hexp[0:96, 0:32]), pair(set_of(0)[0:96, 0:32]), -87.0, None, ALU.max)
            ts(hexp[:, 32:32 + NCMP], set_of(1)[:, 0:NCMP], -87.0, None, ALU.max).then_inc(S("cmp_bounded"), 1)
            dve.wait_ge(S("cmp_exps"), 1)

            plus_one_over(pair(hexp[0:96, 0:32]))
            plus_one_over(hexp[:, 32:32 + NCMP])
            tt(hidk[0:96, :, 0:NCMP], pair(hexp[0:96, 0:32]), pair(set_of(0)[0:96, 0:32]), ALU.mult
               ).then_inc(S("set_read0"), 1)
            tt(hidv[:, 0:NCMP], hexp[:, 32:32 + NCMP], set_of(1)[:, 0:NCMP], ALU.mult).then_inc(S("set_read1"), 1)
            dve.wait_ge(S("cmp_projected"), 1)
            v.tensor_copy(kcmp[0:96, :, 0:NCMP], pair(bank(6, 0, 32)[0:96, :]))
            v.tensor_copy(vcmp[0:NCMP, :], bank(7, 0, P)[0:NCMP, :]).then_inc(S("cmp_done"), 1)

            def max2(u):
                kind, o, h = OUTS[u // 2]
                qt = u % 2
                n = keys_seen(kind, qt)
                scores = bank(2 + u % 4, 0, n)
                dve.wait_ge(S("scores2_ready"), u + 1)
                if u >= 4:
                    dve.wait_ge(S("exps2"), u - 3)
                if kind != "mem":
                    out = ssb[:, u % 4, 0:n]
                    if kind == "mla":
                        tt(out, scores, causal[:, T - n:T], ALU.add)
                    else:
                        rel = C("cmprel")[:, qt * 16:qt * 16 + n] if kind == "cmp" else C("rel")[:, qt * T:qt * T + n]
                        stt(out, rel, 2.0 ** (-2.0 * (h + 1)), scores, ALU.mult, ALU.add)
                    dve.drain()
                    scores = out
                v.reduce_max(small[:, 32 + u % 4:33 + u % 4], scores, AXX)
                dve.drain()
                ts(small[:, 36 + u % 4:37 + u % 4], small[:, 32 + u % 4:33 + u % 4], -1.0, None, ALU.mult
                   ).then_inc(S("max2_ready"), 1)

            def norm2(u):
                kind, o, h = OUTS[u // 2]
                qt = u % 2
                n = keys_seen(kind, qt)
                probs, total = prob[:, u % 4, 0:n], small[:, 40 + u % 4:41 + u % 4]
                dve.wait_ge(S("exps2"), u + 1)
                if kind == "cmp":
                    tt(probs, probs, C("cmpmask")[:, qt * 16:qt * 16 + n], ALU.mult)
                    dve.drain()
                    v.reduce_sum(total, probs, AXX)
                    dve.drain()
                    ts(total, total, 1e-20, None, ALU.add)
                    dve.drain()
                v.reciprocal(small[:, 44 + u % 4:45 + u % 4], total)
                dve.drain()
                ts(probs, probs, small[:, 44 + u % 4:45 + u % 4], None, ALU.mult).then_inc(S("probs2_ready"), 1)

            for u in range(2 * len(OUTS)):
                max2(u)
                if u:
                    norm2(u - 1)
            norm2(2 * len(OUTS) - 1)
            for n in range(12):
                dve.wait_ge(S("nsa_gate_rows"), n + 1)
                tt(obuf[:, 8 + n, :], obuf[:, 8 + n, :], bank(4 + n % 2, 0, T), ALU.mult).then_inc(S("nsa_gated"), 1)
            for k in (1, 2):
                dve.drain()
                tt(obuf[:, 8:20:3, :], obuf[:, 8:20:3, :], obuf[:, 8 + k:20:3, :], ALU.add)
            dve.drain()
            tt(zT[:, 0:8, :], zT[:, 0:8, :], obuf[:, 0:8, :], ALU.mult)
            tt(zT[:, 8:12, :], zT[:, 8:12, :], obuf[:, 8:20:3, :], ALU.mult)
            tt(zT[:, 12:16, :], zT[:, 12:16, :], obuf[:, 20:24, :], ALU.mult).then_inc(S("mixers_gated"), 1)
            dve.drain()
            split_values([h[:, :, :] for h in hs], hL[:, :, :]).then_inc(S("mixed2"), 1)
            at = 0
            for job in range(4):
                while at < min(4 * job + 6, 16):
                    split_lo(st.index("out2", at))
                    at += 1
                dve.wait_ge(S("chunks_multiplied"), st.done("out2", 0, job))
                x = x1[:, 4 * job:4 * job + 4, :]
                tt(x, x, set_of(job % 2).rearrange("p (a b) -> p a b", a=4), ALU.add
                   ).then_inc(S(f"set_read{job % 2}"), 1)
            dve.wait_ge(S("x3_summed"), 1)
            variance(rstd[:, 0, 0:T], bank(4, 0, T), D)
            rsqrt_wait()
            gained(hL, x1, "final_norm_g_2", rstd[:, 0, 0:T], KD).then_inc(S("x3_normed"), 1)


_INS = ["x", "c", "ctx", "c_ctx", "w_ada", "b_ada", "norm1_w", "w_in", "w_a_up_f", "b_a_f", "w_a_up_b", "b_a_b",
        "gla_onorm_w", "diff_qnorm_w", "diff_knorm_w", "lambda_q1", "lambda_k1", "lambda_q2", "lambda_k2",
        "diff_onorm_w", "w_proj_gla", "w_proj_diff", "w_gate", "b_gate", "w_out", "norm2_w", "w_up", "conv_w",
        "conv_b", "w_down", "mem_2", "norm_g_2", "w_in_2", "q_norm_g_2", "w_uq_2", "kv_norm_g_2", "w_ukv_2",
        "cmp_pe_k_2", "cmp_pe_v_2", "cmp_w1k_2", "cmp_w2k_2", "cmp_w1v_2", "cmp_w2v_2", "mem_norm_g_2",
        "w_mem_kv_2", "w_out_2", "final_norm_g_2"]


def kernel(**inputs):
    import concourse.bacc as bacc
    from concourse.bass_utils import run_bass_kernel_spmd

    nc = bacc.Bacc("TRN2", target_bir_lowering=False, num_devices=1)
    arrays, dram = {}, {}
    for name in _INS:
        a = np.ascontiguousarray(inputs[name])
        arrays[f"in_{name}"] = a
        ap = nc.dram_tensor(f"in_{name}", a.shape, F32, kind="ExternalInput").ap()
        dram[name] = ap[0] if len(a.shape) == 3 and name not in ("x", "ctx", "mem_2") else ap
    arrays["in_consts"] = shape_constants()
    dram["consts"] = nc.dram_tensor("in_consts", arrays["in_consts"].shape, F32, kind="ExternalInput").ap()
    out = nc.dram_tensor("out", (1, T, D), F32, kind="ExternalOutput").ap()
    x_spill = nc.dram_tensor("x_spill", (P, KD, T), F32, kind="Internal").ap()
    build(nc, dram, out, x_spill)
    r = run_bass_kernel_spmd(nc, [arrays], core_ids=[0])
    return r.results[0]["out"]
```
